# Optimizing a Trainium2 kernel written in Bass

```python
import math
import jax, jax.numpy as jnp
from jax import lax
import numpy as np

D_MODEL = 1024
BATCH = 1
SEQ = 256
DEPTH = 1

GRID_W = 64
ATT_HEADS = 8
ATT_KV_HEADS = 2
ATT_HEAD_DIM = 64
ATT_WIDTH = ATT_HEADS * ATT_HEAD_DIM
ATT_KV_WIDTH = ATT_KV_HEADS * ATT_HEAD_DIM
Q_BLOCK = 128
ROPE_THETA = 10000.0
HG_HEADS = 4
HG_DK = 128
HG_DV = 128
HG_WIDTH_K = HG_HEADS * HG_DK
HG_WIDTH_V = HG_HEADS * HG_DV
HG_CHUNK = 64
N_BRANCH = 2
IN_SPLITS = (ATT_WIDTH, ATT_KV_WIDTH, ATT_KV_WIDTH,
             HG_WIDTH_K, HG_WIDTH_K, HG_WIDTH_K, HG_WIDTH_V, HG_WIDTH_V,
             N_BRANCH * D_MODEL)
IN_WIDTH = sum(IN_SPLITS)
PEER_HEADS = 8
PEER_NKEYS = 128
PEER_N_EXPERTS = PEER_NKEYS * PEER_NKEYS
PEER_DKEY = 256
PEER_TOPK = 16
PEER_TOKEN_BLOCK = 128
PLE_DIM = 256
EPS = 1e-6


def rmsnorm(x, g):
    xf = x.astype(jnp.float32)
    y = xf * lax.rsqrt(jnp.mean(xf * xf, axis=-1, keepdims=True) + EPS)
    return (y * g.astype(jnp.float32)).astype(x.dtype)

def axial_rope_tables(seq_len):
    rows = seq_len // GRID_W
    row = jnp.repeat(jnp.arange(rows), GRID_W).astype(jnp.float32)
    col = jnp.tile(jnp.arange(GRID_W), rows).astype(jnp.float32)
    axis_dim = ATT_HEAD_DIM // 2
    rot_half = axis_dim // 2
    inv = ROPE_THETA ** (-jnp.arange(rot_half, dtype=jnp.float32) / rot_half)
    ang = jnp.stack([row[:, None] * inv, col[:, None] * inv], axis=1)
    return jnp.cos(ang), jnp.sin(ang)

def apply_axial_rope(x, cos, sin):
    B, S, H, hd = x.shape
    xr = x.reshape(B, S, H, 2, 2, hd // 4).astype(jnp.float32)
    x1, x2 = xr[..., 0, :], xr[..., 1, :]
    c = cos[None, :, None]
    s = sin[None, :, None]
    out = jnp.stack([x1 * c - x2 * s, x1 * s + x2 * c], axis=-2)
    return out.reshape(B, S, H, hd).astype(x.dtype)

def gqa_attention(q, k, v):
    B, S = q.shape[:2]
    G = ATT_HEADS // ATT_KV_HEADS
    nb = S // Q_BLOCK
    scale = ATT_HEAD_DIM ** -0.5
    qb = q.reshape(B, nb, Q_BLOCK, ATT_KV_HEADS, G, ATT_HEAD_DIM).transpose(1, 0, 2, 3, 4, 5)

    def one_block(qblk):
        s = jnp.einsum('bqkgd,bskd->bkgqs', qblk, k, preferred_element_type=jnp.float32) * scale
        pr = jax.nn.softmax(s, axis=-1)
        return jnp.einsum('bkgqs,bskd->bqkgd', pr.astype(v.dtype), v)

    o = lax.map(one_block, qb)
    return o.transpose(1, 0, 2, 3, 4, 5).reshape(B, S, ATT_WIDTH)

def gla_chunk_scan(q, k, v, log_f):
    B, S, H, dk = q.shape
    dv = v.shape[-1]
    C = HG_CHUNK
    nc = S // C

    def to_chunks(a):
        return a.reshape(B, nc, C, H, a.shape[-1]).transpose(1, 0, 3, 2, 4)

    qc, kc, vc, gc = to_chunks(q), to_chunks(k), to_chunks(v), to_chunks(log_f)
    lower = jnp.tril(jnp.ones((C, C), dtype=bool))[:, :, None]

    def step(state, inp):
        qi, ki, vi, gi = inp
        b = jnp.cumsum(gi.astype(jnp.float32), axis=2)
        diff = b[:, :, :, None, :] - b[:, :, None, :, :]
        decay = jnp.exp(jnp.where(lower, diff, -jnp.inf))
        A = jnp.einsum('bhtd,bhsd,bhtsd->bhts', qi.astype(jnp.float32), ki.astype(jnp.float32), decay)
        o_intra = jnp.einsum('bhts,bhse->bhte', A, vi.astype(jnp.float32))
        o_inter = jnp.einsum('bhtd,bhde->bhte', qi.astype(jnp.float32) * jnp.exp(b), state)
        b_last = b[:, :, -1:, :]
        k_dec = ki.astype(jnp.float32) * jnp.exp(b_last - b)
        new_state = state * jnp.exp(b_last[:, :, 0, :])[..., None] + \
            jnp.einsum('bhsd,bhse->bhde', k_dec, vi.astype(jnp.float32))
        return new_state, o_intra + o_inter

    state0 = jnp.zeros((B, H, dk, dv), jnp.float32)
    _, o = lax.scan(step, state0, (qc, kc, vc, gc))
    return o.transpose(1, 0, 3, 2, 4).reshape(B, S, H, dv)

def hgrn2_bidirectional(hq, hf_f, hf_b, hi, hg, lb, out_norm):
    B, S = hq.shape[:2]
    q = jax.nn.silu(hq).reshape(B, S, HG_HEADS, HG_DK)
    i_in = hi.reshape(B, S, HG_HEADS, HG_DV)

    def gates(fpre, lbd):
        f = lbd + (1.0 - lbd) * jax.nn.sigmoid(fpre.astype(jnp.float32))
        f = f.reshape(B, S, HG_HEADS, HG_DK)
        return 1.0 - f, jnp.log(f)

    k_f, lf_f = gates(hf_f, lb[0])
    k_b, lf_b = gates(hf_b, lb[1])
    o_fwd = gla_chunk_scan(q, k_f, i_in, lf_f)
    flip = lambda a: jnp.flip(a, axis=1)
    o_bwd = flip(gla_chunk_scan(flip(q), flip(k_b), flip(i_in), flip(lf_b)))
    o = rmsnorm(o_fwd + o_bwd, out_norm)
    o = o * jax.nn.silu(hg.astype(jnp.float32).reshape(B, S, HG_HEADS, HG_DV))
    return o.reshape(B, S, HG_WIDTH_V).astype(hq.dtype)

def peer_ffn(h, w_q, sub_keys, u, v):
    B, S, D = h.shape
    T = B * S
    K = PEER_TOPK
    ht = h.reshape(T, D)
    q = (ht @ w_q).reshape(T, PEER_HEADS, 2, PEER_DKEY // 2)
    s = jnp.einsum('thpc,hpnc->thpn', q, sub_keys, preferred_element_type=jnp.float32)
    v1, i1 = lax.top_k(s[:, :, 0], K)
    v2, i2 = lax.top_k(s[:, :, 1], K)
    cand = (v1[..., :, None] + v2[..., None, :]).reshape(T, PEER_HEADS, K * K)
    cand_idx = (i1[..., :, None] * PEER_NKEYS + i2[..., None, :]).reshape(T, PEER_HEADS, K * K)
    top_s, pos = lax.top_k(cand, K)
    idx = jnp.take_along_axis(cand_idx, pos, axis=-1)
    g = jax.nn.softmax(top_s, axis=-1)
    nb = T // PEER_TOKEN_BLOCK

    def one_block(args):
        xb, ib, gb = args
        ue = jnp.take(u, ib, axis=0)
        a = jnp.einsum('thkd,td->thk', ue, xb, preferred_element_type=jnp.float32)
        w = jax.nn.gelu(a) * gb
        ve = jnp.take(v, ib, axis=0)
        return jnp.einsum('thk,thkd->td', w.astype(ve.dtype), ve)

    out = lax.map(one_block, (ht.reshape(nb, PEER_TOKEN_BLOCK, D),
                              idx.reshape(nb, PEER_TOKEN_BLOCK, PEER_HEADS, K),
                              g.reshape(nb, PEER_TOKEN_BLOCK, PEER_HEADS, K)))
    return out.reshape(B, S, D).astype(h.dtype)

def first_inputs(seed: int = 0) -> dict:
    key = jax.random.key(seed)
    ks = jax.random.split(key, 24)
    f32 = jnp.float32
    nrm = lambda k, shape, scale: jax.random.normal(k, shape, f32) * scale
    gain = lambda k, shape: 1.0 + 0.02 * jax.random.normal(k, shape, f32)
    return {
        "x": nrm(ks[0], (BATCH, SEQ, D_MODEL), 1.0),
        "p": nrm(ks[1], (DEPTH, BATCH, SEQ, PLE_DIM), 1.0),
        "norm_mix": gain(ks[2], (DEPTH, D_MODEL)),
        "w_in": nrm(ks[3], (DEPTH, D_MODEL, IN_WIDTH), D_MODEL ** -0.5),
        "q_norm": gain(ks[4], (DEPTH, ATT_HEAD_DIM)),
        "k_norm": gain(ks[5], (DEPTH, ATT_HEAD_DIM)),
        "hg_lb_raw": nrm(ks[6], (DEPTH + 1, 2, HG_WIDTH_K), 0.1),
        "hg_out_norm": gain(ks[7], (DEPTH, HG_DV)),
        "w_up_att": nrm(ks[8], (DEPTH, ATT_WIDTH, D_MODEL), ATT_WIDTH ** -0.5),
        "w_up_hg": nrm(ks[9], (DEPTH, HG_WIDTH_V, D_MODEL), HG_WIDTH_V ** -0.5),
        "w_out": nrm(ks[10], (DEPTH, D_MODEL, D_MODEL), D_MODEL ** -0.5),
        "norm_ffn": gain(ks[11], (DEPTH, D_MODEL)),
        "peer_wq": nrm(ks[12], (DEPTH, D_MODEL, PEER_HEADS * PEER_DKEY), D_MODEL ** -0.5),
        "peer_subkeys": nrm(ks[13], (DEPTH, PEER_HEADS, 2, PEER_NKEYS, PEER_DKEY // 2), (PEER_DKEY // 2) ** -0.5),
        "peer_u": nrm(ks[14], (DEPTH, PEER_N_EXPERTS, D_MODEL), D_MODEL ** -0.5),
        "peer_v": nrm(ks[15], (DEPTH, PEER_N_EXPERTS, D_MODEL), 0.3),
        "norm_ple": gain(ks[16], (DEPTH, D_MODEL)),
        "ple_gate": nrm(ks[17], (DEPTH, D_MODEL, D_MODEL), D_MODEL ** -0.5),
        "ple_proj": nrm(ks[18], (DEPTH, PLE_DIM, D_MODEL), PLE_DIM ** -0.5),
    }

def first_block(x, p, norm_mix, w_in, q_norm, k_norm, hg_lb_raw, hg_out_norm, w_up_att, w_up_hg,
              w_out, norm_ffn, peer_wq, peer_subkeys, peer_u, peer_v, norm_ple, ple_gate, ple_proj):
    B, S, D = x.shape
    cos, sin = axial_rope_tables(S)
    lb_all = jnp.cumsum(jax.nn.softmax(hg_lb_raw.astype(jnp.float32), axis=0), axis=0)
    offsets = [int(o) for o in np.cumsum(IN_SPLITS)[:-1]]
    for i in range(DEPTH):
        h = rmsnorm(x, norm_mix[i])
        proj = h @ w_in[i]
        aq, ak, av, hq, hf_f, hf_b, hi, hg, gate_pre = jnp.split(proj, offsets, axis=-1)
        q = rmsnorm(aq.reshape(B, S, ATT_HEADS, ATT_HEAD_DIM), q_norm[i])
        k = rmsnorm(ak.reshape(B, S, ATT_KV_HEADS, ATT_HEAD_DIM), k_norm[i])
        v = av.reshape(B, S, ATT_KV_HEADS, ATT_HEAD_DIM)
        q = apply_axial_rope(q, cos, sin)
        k = apply_axial_rope(k, cos, sin)
        y_att = gqa_attention(q, k, v) @ w_up_att[i]
        y_hg = hgrn2_bidirectional(hq, hf_f, hf_b, hi, hg, lb_all[i], hg_out_norm[i]) @ w_up_hg[i]
        gts = jax.nn.sigmoid(gate_pre.astype(jnp.float32)).reshape(B, S, N_BRANCH, D)
        merged = (gts[:, :, 0] * y_att + gts[:, :, 1] * y_hg).astype(x.dtype)
        x = x + merged @ w_out[i]
        x = x + peer_ffn(rmsnorm(x, norm_ffn[i]), peer_wq[i], peer_subkeys[i], peer_u[i], peer_v[i])
        g_ple = jax.nn.sigmoid(rmsnorm(x, norm_ple[i]) @ ple_gate[i])
        x = x + g_ple * (p[i] @ ple_proj[i])
    return x


ATTN_WIDTH = D_MODEL // 2
ATTN_HEAD_DIM = 64
N_ATTN_HEADS = ATTN_WIDTH // ATTN_HEAD_DIM
MLSTM_WIDTH = D_MODEL - ATTN_WIDTH
N_MLSTM_HEADS = 4
MLSTM_HEAD_DIM = MLSTM_WIDTH // N_MLSTM_HEADS
MLSTM_CHUNK = 64
CONV_WIDTH = 4
DILATED_PATTERNS = ((128, 1), (512, 4), (2048, 16))
ATTN_BLOCK = 128
ATTN_SCALE = ATTN_HEAD_DIM ** -0.5
D_FF = ((8 * D_MODEL // 3 + 255) // 256) * 256
N_MOD = 6
RMS_EPS = 1e-6
IN_SPLITS_2 = (ATTN_WIDTH, ATTN_WIDTH, ATTN_WIDTH,
             MLSTM_WIDTH, MLSTM_WIDTH, MLSTM_WIDTH,
             MLSTM_WIDTH,
             N_MLSTM_HEADS, N_MLSTM_HEADS)
IN_COLS = sum(IN_SPLITS_2)


def rms_norm(x, g):
    xf = x.astype(jnp.float32)
    y = xf * lax.rsqrt(jnp.mean(xf * xf, axis=-1, keepdims=True) + RMS_EPS)
    return (y * g.astype(jnp.float32)).astype(x.dtype)

def modulate(h, shift, scale):
    return h * (1 + scale[:, None, :]) + shift[:, None, :]

def causal_short_conv(x, w, b):
    S = x.shape[1]
    xp = jnp.pad(x, ((0, 0), (CONV_WIDTH - 1, 0), (0, 0)))
    y = b
    for j in range(CONV_WIDTH):
        y = y + xp[:, j:j + S] * w[j]
    return y

def dilated_branch(q, k, v, window, dilation):
    B, S, H, Dh = q.shape
    n_back = window // dilation
    assert n_back <= ATTN_BLOCK and S % dilation == 0
    L = S // dilation
    nb = -(-L // ATTN_BLOCK)
    Lp = nb * ATTN_BLOCK

    def to_sub(t):
        t = t.reshape(B, L, dilation, H, Dh).transpose(0, 2, 1, 3, 4)
        t = jnp.pad(t, ((0, 0), (0, 0), (0, Lp - L), (0, 0), (0, 0)))
        return t.reshape(B, dilation, nb, ATTN_BLOCK, H, Dh)

    def with_prev(t):
        prev = jnp.pad(t, ((0, 0), (0, 0), (1, 0), (0, 0), (0, 0), (0, 0)))[:, :, :-1]
        return jnp.concatenate([prev, t], axis=3)

    qb = to_sub(q)
    kb = with_prev(to_sub(k))
    vb = with_prev(to_sub(v))
    s = jnp.einsum('brnqhd,brnkhd->brnhqk', qb, kb).astype(jnp.float32)
    qi = jnp.arange(ATTN_BLOCK)[:, None] + ATTN_BLOCK
    kj = jnp.arange(2 * ATTN_BLOCK)[None, :]
    rel = qi - kj
    band = (rel >= 0) & (rel <= n_back)
    valid = band[None] & ((jnp.arange(nb)[:, None, None] > 0) | (kj[None] >= ATTN_BLOCK))
    s = jnp.where(valid[None, None, :, None], s, -jnp.inf)
    lse = jax.nn.logsumexp(s, axis=-1)
    p = jnp.exp(s - lse[..., None])
    o = jnp.einsum('brnhqk,brnkhd->brnqhd', p.astype(v.dtype), vb)
    o = o.reshape(B, dilation, Lp, H, Dh)[:, :, :L]
    o = o.transpose(0, 2, 1, 3, 4).reshape(B, S, H, Dh)
    lse = lse.transpose(0, 1, 2, 4, 3).reshape(B, dilation, Lp, H)[:, :, :L]
    lse = lse.transpose(0, 2, 1, 3).reshape(B, S, H)
    return o, lse

def dilated_attention(q, k, v):
    outs, lses = [], []
    for window, dilation in DILATED_PATTERNS:
        o, lse = dilated_branch(q, k, v, window, dilation)
        outs.append(o)
        lses.append(lse)
    w = jax.nn.softmax(jnp.stack(lses, axis=0), axis=0)
    return jnp.einsum('pbsh,pbshd->bshd', w.astype(v.dtype), jnp.stack(outs, axis=0))

def mlstm_chunkwise(q, k, v, log_i, log_f):
    B, NH, S, D = q.shape
    L = MLSTM_CHUNK
    NC = S // L
    k = k * (D ** -0.5)

    def to_chunks(t):
        return jnp.moveaxis(t.reshape(B, NH, NC, L, *t.shape[3:]), 2, 0)

    xs = (to_chunks(q), to_chunks(k), to_chunks(v), to_chunks(log_i), to_chunks(log_f))
    causal = jnp.tril(jnp.ones((L, L), dtype=bool))

    def step(carry, inp):
        C, n, m = carry
        qc, kc, vc, ic, fc = inp
        b = jnp.cumsum(fc, axis=-1)
        log_d = b[..., :, None] - b[..., None, :] + ic[..., None, :]
        log_d = jnp.where(causal, log_d, -jnp.inf)
        m_inter = b + m[..., None]
        m_t = jnp.maximum(m_inter, jnp.max(log_d, axis=-1))
        d_mat = jnp.exp(log_d - m_t[..., None])
        inter = jnp.exp(m_inter - m_t)
        s_qk = jnp.einsum('bhtd,bhsd->bhts', qc, kc) * d_mat
        num = inter[..., None] * jnp.einsum('bhtd,bhde->bhte', qc, C) + jnp.einsum('bhts,bhse->bhte', s_qk, vc)
        nq = inter * jnp.einsum('bhtd,bhd->bht', qc, n) + jnp.sum(s_qk, axis=-1)
        h = num / jnp.maximum(jnp.abs(nq), jnp.exp(-m_t))[..., None]
        b_last = b[..., -1]
        w_log = b_last[..., None] - b + ic
        m_new = jnp.maximum(b_last + m, jnp.max(w_log, axis=-1))
        w = jnp.exp(w_log - m_new[..., None])
        decay = jnp.exp(b_last + m - m_new)
        C_new = decay[..., None, None] * C + jnp.einsum('bhs,bhsd,bhse->bhde', w, kc, vc)
        n_new = decay[..., None] * n + jnp.einsum('bhs,bhsd->bhd', w, kc)
        return (C_new, n_new, m_new), h

    init = (jnp.zeros((B, NH, D, D), jnp.float32),
            jnp.zeros((B, NH, D), jnp.float32),
            jnp.zeros((B, NH), jnp.float32))
    _, h = lax.scan(step, init, xs)
    return jnp.moveaxis(h, 0, 2).reshape(B, NH, S, D)

def token_mixer(h, w_in, w_conv, b_conv, b_igate, b_fgate, q_norm_g, k_norm_g, mlstm_norm_g, w_out):
    B, S, _ = h.shape
    xin = h @ w_in
    cuts = list(np.cumsum(IN_SPLITS_2)[:-1])
    qa, ka, va, qm, km, vm, og, ig, fg = jnp.split(xin, cuts, axis=-1)
    qa = rms_norm(qa.reshape(B, S, N_ATTN_HEADS, ATTN_HEAD_DIM), q_norm_g) * ATTN_SCALE
    ka = rms_norm(ka.reshape(B, S, N_ATTN_HEADS, ATTN_HEAD_DIM), k_norm_g)
    va = va.reshape(B, S, N_ATTN_HEADS, ATTN_HEAD_DIM)
    attn = dilated_attention(qa, ka, va).reshape(B, S, ATTN_WIDTH)
    qkm = jax.nn.silu(causal_short_conv(jnp.concatenate([qm, km], axis=-1), w_conv, b_conv))
    qm, km = jnp.split(qkm, 2, axis=-1)

    def heads(t):
        return t.reshape(B, S, N_MLSTM_HEADS, MLSTM_HEAD_DIM).transpose(0, 2, 1, 3).astype(jnp.float32)

    log_i = (ig + b_igate).astype(jnp.float32).transpose(0, 2, 1)
    log_f = jax.nn.log_sigmoid((fg + b_fgate).astype(jnp.float32)).transpose(0, 2, 1)
    hm = mlstm_chunkwise(heads(qm), heads(km), heads(vm), log_i, log_f)
    hm = hm.transpose(0, 2, 1, 3).astype(h.dtype)
    hm = rms_norm(hm, mlstm_norm_g.reshape(N_MLSTM_HEADS, MLSTM_HEAD_DIM)).reshape(B, S, MLSTM_WIDTH)
    hm = jax.nn.sigmoid(og) * hm
    return jnp.concatenate([attn, hm], axis=-1) @ w_out

def swiglu(h, w_gate, w_up, w_down):
    return (jax.nn.silu(h @ w_gate) * (h @ w_up)) @ w_down

def second_inputs(seed: int = 0) -> dict:
    key = jax.random.key(seed)
    ks = jax.random.split(key, 20)
    f32 = jnp.float32
    D = D_MODEL

    def nrm(k, shape, scale):
        return jax.random.normal(k, shape, f32) * scale

    b_ada = nrm(ks[15], (DEPTH, N_MOD * D), 0.02)
    gate_cols = jnp.zeros((N_MOD, D), f32).at[2].set(1.0).at[5].set(1.0).reshape(-1)
    b_ada = b_ada + gate_cols
    f_bias = jnp.linspace(3.0, 6.0, N_MLSTM_HEADS, dtype=f32)[None, :]
    return {
        "x": nrm(ks[0], (BATCH, SEQ, D), 1.0),
        "c": nrm(ks[1], (BATCH, D), 1.0),
        "g_mix": 1.0 + nrm(ks[2], (DEPTH, D), 0.02),
        "w_in": nrm(ks[3], (DEPTH, D, IN_COLS), D ** -0.5),
        "w_conv": nrm(ks[4], (DEPTH, CONV_WIDTH, 2 * MLSTM_WIDTH), CONV_WIDTH ** -0.5),
        "b_conv": nrm(ks[5], (DEPTH, 2 * MLSTM_WIDTH), 0.02),
        "b_igate": nrm(ks[6], (DEPTH, N_MLSTM_HEADS), 0.1),
        "b_fgate": f_bias + nrm(ks[7], (DEPTH, N_MLSTM_HEADS), 0.1),
        "q_norm_g": 1.0 + nrm(ks[8], (DEPTH, ATTN_HEAD_DIM), 0.02),
        "k_norm_g": 1.0 + nrm(ks[9], (DEPTH, ATTN_HEAD_DIM), 0.02),
        "mlstm_norm_g": 1.0 + nrm(ks[10], (DEPTH, MLSTM_WIDTH), 0.02),
        "w_out": nrm(ks[11], (DEPTH, D, D), D ** -0.5),
        "g_ffn": 1.0 + nrm(ks[12], (DEPTH, D), 0.02),
        "w_gate": nrm(ks[13], (DEPTH, D, D_FF), D ** -0.5),
        "w_up": nrm(ks[14], (DEPTH, D, D_FF), D ** -0.5),
        "w_down": nrm(ks[16], (DEPTH, D_FF, D), D_FF ** -0.5),
        "w_ada": nrm(ks[17], (DEPTH, D, N_MOD * D), 0.1 * D ** -0.5),
        "b_ada": b_ada,
    }

def second_block(x, c, g_mix, w_in, w_conv, b_conv, b_igate, b_fgate, q_norm_g, k_norm_g,
              mlstm_norm_g, w_out, g_ffn, w_gate, w_up, w_down, w_ada, b_ada):
    for l in range(DEPTH):
        mod = jax.nn.silu(c) @ w_ada[l] + b_ada[l]
        sh_m, sc_m, gt_m, sh_f, sc_f, gt_f = jnp.split(mod, N_MOD, axis=-1)
        h = modulate(rms_norm(x, g_mix[l]), sh_m, sc_m)
        y = token_mixer(h, w_in[l], w_conv[l], b_conv[l], b_igate[l], b_fgate[l],
                        q_norm_g[l], k_norm_g[l], mlstm_norm_g[l], w_out[l])
        x = x + gt_m[:, None, :] * y
        h = modulate(rms_norm(x, g_ffn[l]), sh_f, sc_f)
        x = x + gt_f[:, None, :] * swiglu(h, w_gate[l], w_up[l], w_down[l])
    return x


def setup_inputs(seed=0):
    out = dict(first_inputs(seed))
    for name, value in second_inputs(seed + 1).items():
        if name != "x":
            out[name + "_2"] = value
    return out


def reference(
    x, p, norm_mix, w_in, q_norm, k_norm, hg_lb_raw, hg_out_norm, w_up_att, w_up_hg, w_out,
    norm_ffn, peer_wq, peer_subkeys, peer_u, peer_v, norm_ple, ple_gate, ple_proj, c_2, g_mix_2,
    w_in_2, w_conv_2, b_conv_2, b_igate_2, b_fgate_2, q_norm_g_2, k_norm_g_2, mlstm_norm_g_2,
    w_out_2, g_ffn_2, w_gate_2, w_up_2, w_down_2, w_ada_2, b_ada_2,
):
    x = first_block(
        x, p, norm_mix, w_in, q_norm, k_norm, hg_lb_raw, hg_out_norm, w_up_att, w_up_hg, w_out,
        norm_ffn, peer_wq, peer_subkeys, peer_u, peer_v, norm_ple, ple_gate, ple_proj,
    )
    return second_block(
        x, c_2, g_mix_2, w_in_2, w_conv_2, b_conv_2, b_igate_2, b_fgate_2, q_norm_g_2,
        k_norm_g_2, mlstm_norm_g_2, w_out_2, g_ffn_2, w_gate_2, w_up_2, w_down_2, w_ada_2,
        b_ada_2,
    )


_drawn_inputs = setup_inputs


def setup_inputs(seed=0):
    import zlib

    import numpy as np

    out = dict(_drawn_inputs(seed))
    spreads = {}
    factors = {'norm_mix': 2.936,
     'q_norm': 8.0,
     'k_norm': 8.0,
     'hg_lb_raw': 5.286,
     'hg_out_norm': 3.672,
     'norm_ple': 66.32,
     'g_mix_2': 4.669,
     'b_conv_2': 31.896,
     'b_igate_2': 64.0,
     'q_norm_g_2': 8.0,
     'k_norm_g_2': 8.0,
     'mlstm_norm_g_2': 30.745,
     'g_ffn_2': 12.958,
     'norm_ffn': 3.111}
    for name, (base, spread) in spreads.items():
        noise = np.random.default_rng([zlib.crc32(name.encode()), seed]).standard_normal(out[name].shape)
        drawn = base * np.exp(spread * noise) if base else spread * noise
        out[name] = __import__('jax').numpy.asarray(drawn.astype(out[name].dtype))
    for name, factor in factors.items():
        out[name] = (out[name] * factor).astype(out[name].dtype)
    return out
```

```python
from contextlib import ExitStack

import numpy as np
import concourse.bass as bass
from concourse import mybir

F32 = mybir.dt.float32
U32 = mybir.dt.uint32
U8 = mybir.dt.uint8
ALU = mybir.AluOpType
ACT = mybir.ActivationFunctionType
AX = mybir.AxisListType.X

P = 128
S = 256
NB = S // P
D = 1024
KD = D // P
EPS = 1e-6
HD = 64
AH, AKV = 8, 2
GH = 4
LEVELS = 8
PH = 8
TOPK = 16
NKEYS = 128
SLOTS = PH * TOPK
HALF = 8
U_RING, V_RING, DIAG_RING = 4, 16, 8
FF = 2816
FC = FF // P
NEG = -3.0e38
W_SLOTS = 3
TILE = KD * 512
GELU_C = 0.7978845608028654

C_ROPE = 0
C_LOGC = C_ROPE + NB * 64
C_TRI = C_LOGC + NB * S
C_IOTA = C_TRI + S
C_IDENT = C_IOTA + TOPK
C_SEL = C_IDENT + P
C_ONE = C_SEL + GH * P
C_END = C_ONE + 1

L_LB = 0
L_CONV = 16
L_CONVB = 48
L_C = 56
L_IF = 64
L_END = 66


def tile_list():
    t, at = [], 0
    for n, w in (("q", 512), ("kv", 256), ("hq", 512), ("hf", 512), ("hb", 512), ("hi", 512), ("hg", 512),
                 ("g0", 512), ("g1", 512), ("g2", 512), ("g3", 512)):
        t.append(("in_" + n, KD, w, "w_in", 0, at))
        at += w
    t += [("up_att", 4, D, "w_up_att", 0, 0), ("up_hg", 4, D, "w_up_hg", 0, 0)]
    t += [(f"out{i}", KD, 512, "w_out", 0, 512 * i) for i in range(2)]
    t += [(f"peer_q{i}", KD, 512, "peer_wq", 0, 512 * i) for i in range(4)]
    t += [("keys", 1, 2 * PH * NKEYS, "subkeys", 0, 0)]
    t += [(f"ada{i}", KD, 512, "w_ada", 0, 512 * i) for i in range(12)] + [("ple_proj", 2, D, "ple_proj", 0, 0)]
    t += [(f"ple{i}", KD, 512, "ple_gate", 0, 512 * i) for i in range(2)]
    t += [("in2_" + n, KD, 512, "w_in_2", 0, 512 * i) for i, n in enumerate(("q", "k", "v", "qm", "km", "vm", "og"))]
    t += [("in2_if", KD, 2 * GH, "w_in_2", 0, 7 * 512)]
    t += [(f"out2_{i}", KD, 512, "w_out_2", 0, 512 * i) for i in range(2)]
    for i in range(6):
        w = min(512, FF - 512 * i)
        t += [(f"gate{i}", KD, w, "w_gate", 0, 512 * i), (f"up{i}", KD, w, "w_up", 0, 512 * i)]
    t += [(f"down{i}", min(4, FC - 4 * i), D, "w_down", 512 * i, 0) for i in range(6)]
    return t


TILES = tile_list()
TILE_NO = {t[0]: n for n, t in enumerate(TILES)}


def product_list():
    def turned(n):
        return [(n, b, h) for b in range(NB) for h in range(2)]

    def rows(n):
        return [(n, b) for b in range(NB)]

    def cols(n, halves=2):
        return [(n, h) for h in range(halves)]

    p = turned("n1T") + rows("in_q") + rows("in_kv") + cols("in_hq") + cols("in_hf") + cols("in_hb")
    p += rows("in_hi") + rows("in_hg")
    for i in range(4):
        p += rows(f"in_g{i}")
    p += [("a_qT", 0), ("a_qT", 1), ("a_kT",)]
    p += [("a_S", b, i, g) for b in range(NB) for i in range(2) for g in range(2)]
    for b in range(NB):
        p += [("a_PT", b, sb, q) for sb in range(NB) for q in range(2)] + [("a_Y", b), ("a_YT", b)]
    p += [("g_diag", 0), ("g_diag", 1)]
    for lv in reversed(range(LEVELS)):
        p += [("g_A", lv, b, d) for d in range(2) for b in (range(NB) if lv < LEVELS - 1 else [0])]
    p += [("g_O", 0), ("g_O", 1), ("g_OT", 0), ("g_OT", 1)]
    p += [(n, b, h) for b in range(NB) for h in range(2) for n in ("up_att", "up_hg")]
    p += turned("mT") + rows("out0") + rows("out1")
    p += turned("n2T")
    for i in range(4):
        p += cols(f"peer_q{i}")
    p += [("keys", b, q) for b in range(NB) for q in range(4)]
    p += [(f"ada{i}",) for i in range(12)] + [("ple_proj", b, h) for b in range(NB) for h in range(2)]
    p += [("experts", b, h) for b in range(NB) for h in range(2)]
    p += turned("n3T") + rows("ple0") + rows("ple1")
    p += turned("n4T") + rows("in2_q") + rows("in2_k") + rows("in2_v") + cols("in2_qm") + cols("in2_km")
    p += rows("in2_vm") + rows("in2_og") + [("in2_if",)]
    p += [("d_qT", b) for b in range(NB)] + [("d_kT", b) for b in range(NB)]
    p += [("d_S", b, i, g) for b in range(NB) for i in range(2) for g in range(2)]
    p += [("m_cols",), ("m_M", 0), ("m_M", 1)] + [("m_S", h) for h in range(GH)]
    for b in range(NB):
        p += [("d_PT", b, sb, q) for sb in range(b + 1) for q in range(2)] + [("d_Y", b)]
    for b in range(NB):
        p += [("m_num", b), ("m_den", b)]
    p += turned("catT") + rows("out2_0") + rows("out2_1") + turned("n5T")
    for i in range(6):
        for n in (f"gate{i}", f"up{i}"):
            p += cols(n, 2 if i < 5 else 1)
    p += [("down", b, h) for b in range(NB) for h in range(2)]
    return p


PLAN = {name: n for n, name in enumerate(product_list())}


def two_blocks(nc, a, out):
    with ExitStack() as ctx:
        def sb(name, cols, dt=F32):
            return ctx.enter_context(nc.sbuf_tensor(name, [P, cols], dt))

        def sem(name):
            return ctx.enter_context(nc.semaphore(name))

        x_t = sb("x_t", NB * D)
        big = sb("big", 30720)
        rows2 = sb("rows2", 2 * D)
        const = sb("const", C_END)
        lmask = sb("lmask", LEVELS * 2 * P, U8)
        gqk = sb("gqk", 10 * HD)
        g_o = sb("g_o", P)
        gqk2 = sb("gqk2", 2 * HD)
        g_m = sb("g_m", 512)
        lane = sb("lane", L_END)
        ms = sb("ms", 80)
        lnms = sb("lnms", 80)
        rstd = sb("rstd", 80)
        small = sb("small", 448)
        idx_t = sb("idx_t", NB * SLOTS, U32)
        gate_t = sb("gate_t", NB * SLOTS)
        idx_now = sb("idx_now", TOPK, U32)
        wring = sb("wring", W_SLOTS * TILE)
        ps = ctx.enter_context(nc.psum_tensor("ps", [P, 8, 512], F32))

        def at(t, lo, n):
            return t[:, lo:lo + n]

        x = x_t[:, :].rearrange("p (b d) -> p b d", b=NB)
        hT = at(big, 0, KD * S).rearrange("p (c t) -> p c t", c=KD)
        gts = at(big, 2048, 4096).rearrange("p (b n) -> p b n", b=NB)
        qkv = at(big, 6144, 1536).rearrange("p (b n) -> p b n", b=NB)
        hi = at(big, 7680, 1024).rearrange("p (b n) -> p b n", b=NB)
        hgs = at(big, 8704, 1024).rearrange("p (b n) -> p b n", b=NB)
        hqs = at(big, 9728, 1024)
        kk = at(big, 10752, 2048).rearrange("p (d n) -> p d n", d=2)
        Pc = at(big, 12800, 2048).rearrange("p (d n) -> p d n", d=2)
        lf = at(big, 14848, 2048).rearrange("p (d n) -> p d n", d=2)
        AT = at(big, 14848, 2048).rearrange("p (s h t) -> p s h t", s=NB, h=GH)
        ksum = at(big, 16896, 1024)
        yT = at(big, 17920, 1024).rearrange("p (c t) -> p c t", c=4)
        oT = at(big, 18944, 1024).rearrange("p (c t) -> p c t", c=4)
        pT = at(big, 19968, 512).rearrange("p (c t) -> p c t", c=2)
        R = 20480
        qn = at(big, R, 1280).rearrange("p (b n) -> p b n", b=NB)
        rot = at(big, R + 1280, 1280).rearrange("p (b n) -> p b n", b=NB)
        a_qT = at(big, R + 2560, 1024).rearrange("p (j t) -> p j t", j=4)
        a_kT = at(big, R + 3584, S)
        a_P = at(big, R + 3840, 4096).rearrange("p (b h s) -> p b h s", b=NB, h=AH)
        a_PT = at(big, R + 7936, 2048).rearrange("p (s h t) -> p s h t", s=NB, h=AH)
        a_y = at(big, R, 1024).rearrange("p (b n) -> p b n", b=NB)
        lmask_f = at(big, R + 4096, LEVELS * 2 * P)
        E = [at(big, R, 2048), rows2[:, :]]
        qd = [at(big, R + 2048 + 4096 * i, 2048).rearrange("p (d n) -> p d n", d=2) for i in range(2)]
        kd = [at(big, R + 4096 + 4096 * i, 2048).rearrange("p (d n) -> p d n", d=2) for i in range(2)]
        o_t = at(big, R, 1024).rearrange("p (b n) -> p b n", b=NB)
        o_sq = at(big, R + 1024, 512)
        merged = at(big, R + 2048, 2048).rearrange("p (b n) -> p b n", b=NB)
        tmp = at(big, R + 4096, 512)
        pqT = at(big, 2048, 4096).rearrange("p (n t) -> p n t", n=16)
        sc = at(big, 6144, 4096).rearrange("p (b n k) -> p b n k", b=NB, n=16)
        cand = at(big, 10240, 2048).rearrange("p (h i j) -> p h i j", h=PH, i=TOPK)
        hot = at(big, 12288, 2048)
        top_v = at(big, 14336, 256).rearrange("p (n k) -> p n k", n=16)
        top_i = at(big, 14592, 256).bitcast(U32).rearrange("p (n k) -> p n k", n=16)
        top_f = at(big, 14848, 256).rearrange("p (h s k) -> p h s k", h=PH, s=2)
        best_v = at(big, 15104, 128).rearrange("p (h k) -> p h k", h=PH)
        best_i = at(big, 15232, 128).bitcast(U32).rearrange("p (h k) -> p h k", h=PH)
        pos_u = at(big, 15360, 256).bitcast(U32).rearrange("p (s n) -> p s n", s=2)
        pos_f = at(big, 15616, 256).rearrange("p (s n) -> p s n", s=2)
        part = at(big, 15872, 256).rearrange("p (s n) -> p s n", s=2)
        cut = at(big, 16128, 256)
        u_ring = at(big, 0, U_RING * D).rearrange("p (r d) -> p r d", r=U_RING)
        v_ring = at(big, U_RING * D, V_RING * D).rearrange("p (r d) -> p r d", r=V_RING)
        mod = at(big, 20480, 6 * D).rearrange("p (j d) -> p j d", j=6)
        pp = at(big, 26624, NB * D).rearrange("p (b d) -> p b d", b=NB)
        h_t = at(big, 28672, NB * D).rearrange("p (b d) -> p b d", b=NB)
        gain = at(rows2, 0, D)
        scratch_row = at(rows2, D, D)
        diag = at(rows2, 0, DIAG_RING * P).rearrange("p (r n) -> p r n", r=DIAG_RING)
        qk2 = at(big, 2048, 2048).rearrange("p (b n) -> p b n", b=NB)
        va = at(big, 4096, 1024).rearrange("p (b n) -> p b n", b=NB)
        vm = at(big, 5120, 1024).rearrange("p (b n) -> p b n", b=NB)
        ogs = at(big, 6144, 1024).rearrange("p (b n) -> p b n", b=NB)
        qkm = at(big, 7168, 2048).rearrange("p (c t) -> p c t", c=8)
        silu_e = at(big, 9216, 2048).rearrange("p (c t) -> p c t", c=8)
        d_PT = at(big, 9216, 2048).rearrange("p (s h t) -> p s h t", s=NB, h=AH)
        sq2 = at(big, 11264, 2048).rearrange("p (b n) -> p b n", b=NB)
        d_qT = at(big, 11264, 1024).rearrange("p (j t) -> p j t", j=4)
        d_kT = at(big, 12288, 1024).rearrange("p (j t) -> p j t", j=4)
        d_P0 = at(big, 13312, 1024).rearrange("p (h s) -> p h s", h=AH)
        d_P1 = at(big, 14336, 2048).rearrange("p (h s) -> p h s", h=AH)
        DT0 = at(big, 16384, 1024).rearrange("p (h t) -> p h t", h=GH)
        DT1 = at(big, 17408, 512).rearrange("p (h t) -> p h t", h=GH)
        gl = at(big, 17920, 2560).rearrange("p (r t) -> p r t", r=10)
        cat = at(big, 26624, 2048).rearrange("p (b n) -> p b n", b=NB)
        hm_sq = at(big, 17920, 512)
        gT = at(big, 2048, FC * S).rearrange("p (c t) -> p c t", c=FC)
        ff_e = at(big, 7680, 512)
        tmp2 = at(big, 19456, 1024)

        ident = at(const, C_IDENT, P)
        iota = at(const, C_IOTA, TOPK)
        tri = at(const, C_TRI, S)
        one = at(const, C_ONE, 1)
        lbs = at(small, 0, 24)
        lb, one_lb = at(small, 24, 8), at(small, 32, 8)
        mx1, sum1 = at(small, 40, 16), at(small, 56, 16)
        g_max, g_sum = at(small, 72, 8), at(small, 80, 8)
        mx2, sum2 = at(small, 88, 16), at(small, 104, 16)
        mcols, emt, den = at(small, 120, 16), at(small, 136, 8), at(small, 144, 8)
        a_dot = at(small, 152, HALF)
        ge = [at(small, 160 + 8 * i, HALF) for i in range(4)]
        w_now = at(small, 192, 2 * HALF)
        c_e, c_s = at(small, 208, 8), at(small, 216, 8)
        ssum = at(small, 224, 10)

        c_rep = at(big, 16384, KD * P).rearrange("p (c n) -> p c n", c=KD)

        product_done = sem("product_done")
        bank_emptied = [sem(f"bank_emptied{i}") for i in range(8)]
        tile_landed = [sem(f"tile_landed{i}") for i in range(W_SLOTS)]
        down_used = sem("down_used")
        x_landed, const_landed, lane_landed = sem("x_landed"), sem("const_landed"), sem("lane_landed")
        rows_landed, mask_landed, pT_landed = sem("rows_landed"), sem("mask_landed"), sem("pT_landed")
        gain_landed, row_landed, row_added = sem("gain_landed"), sem("row_landed"), sem("row_added")
        sq_summed, ms_ready, rstd_ready, h_ready = sem("sq_summed"), sem("ms_ready"), sem("rstd_ready"), sem("h_ready")
        dve_step, act_step, pool_step = sem("dve_step"), sem("act_step"), sem("pool_step")
        lb_sub, lb_exp, lb_done = sem("lb_sub"), sem("lb_exp"), sem("lb_done")
        hq_exp, hf_ready, lf_ready, hg_exp = sem("hq_exp"), sem("hf_ready"), sem("lf_ready"), sem("hg_exp")
        a_rot, a_max, a_probs, a_out = sem("a_rot"), sem("a_max"), sem("a_probs"), sem("a_out")
        g_zeroed, g_diff, g_exp, g_decayed, g_ks = (sem(n) for n in ("g_zeroed", "g_diff", "g_exp", "g_decayed", "g_ks"))
        g_scanned, g_filled, g_out, gates_ready, merged_ready = (
            sem(n) for n in ("g_scanned", "g_filled", "g_out", "gates_ready", "merged_ready"))
        c_exp, c_ready, best_ready, best_exp, routed = (
            sem(n) for n in ("c_exp", "c_ready", "best_ready", "best_exp", "routed"))
        u_landed = [sem(f"u_landed{i}") for i in range(U_RING)]
        v_landed = [sem(f"v_landed{i}") for i in range(V_RING)]
        u_free, v_free = sem("u_free"), sem("v_free")
        idx_copied, gelu_in, gelu_exp, w_ready, diag_built = (
            sem(n) for n in ("idx_copied", "gelu_in", "gelu_exp", "w_ready", "diag_built"))
        ple_exp, mod_ready, x_ready = sem("ple_exp"), sem("mod_ready"), sem("x_ready")
        d_norm, d_max, d_probs, cat_ready = sem("d_norm"), sem("d_max"), sem("d_probs"), sem("cat_ready")
        conv_done, conv_exp, qkm_ready, og_exp = sem("conv_done"), sem("conv_exp"), sem("qkm_ready"), sem("og_exp")
        m_abs, m_log, m_rows, m_D, m_Dexp, m_A, m_mt = (
            sem(n) for n in ("m_abs", "m_log", "m_rows", "m_D", "m_Dexp", "m_A", "m_mt"))
        ff_exp, ff_ready, stored = sem("ff_exp"), sem("ff_ready"), sem("stored")
        mask_packed, slot_granted = sem("mask_packed"), sem("slot_granted")
        residual_ready, ple_done, gelu_step = sem("residual_ready"), sem("ple_done"), sem("gelu_step")

        def bank(name, n=512, lo=0):
            return ps[:, PLAN[name] % 8, lo:lo + n]

        def wait_product(eng, *name):
            eng.wait_ge(product_done, PLAN[name] + 1)

        def wait_moved(eng, *name):
            eng.wait_ge(bank_emptied[PLAN[name] % 8], PLAN[name] // 8 + 1)

        def emptied(*name):
            return bank_emptied[PLAN[name] % 8]

        STAT = [1, 1, 10, 10, 4, 4, 1, 1, 1, 1, 1, 1, 16, 16, 4, 4, 1, 1]
        STAT_AT = [sum(STAT[:i]) for i in range(len(STAT))]
        NORM_STAT = [0, 6, 8, 10, 16]
        A_STAT, G_STAT, DA_STAT, M_STAT = 2, 4, 12, 14

        def stat(t, n):
            return t[:, STAT_AT[n]:STAT_AT[n] + STAT[n]]

        block = ctx.enter_context(nc.Block())

        @block.sync
        def _(sp):
            sp.dma_start(x, a["x"].rearrange("(b p) d -> p b d", p=P)).then_inc(x_landed, 16)
            sp.dma_start(const[:, :], a["const"]).then_inc(const_landed, 16)
            sp.dma_start(lane[:, :], a["lane"]).then_inc(lane_landed, 16)
            for n, (name, k, w, src, r0, c0) in enumerate(TILES):
                if n >= W_SLOTS:
                    before = TILES[n - W_SLOTS][0]
                    if before.startswith("down"):
                        sp.wait_ge(down_used, int(before[4:]) + 1)
                    else:
                        sp.wait_ge(product_done, 1 + max(v for p, v in PLAN.items() if p[0] == before))
                slot = n % W_SLOTS * TILE
                sp.dma_start(wring[:, slot:slot + k * w].rearrange("p (c n) -> p c n", c=k),
                             a[src][r0:r0 + k * P, :].rearrange("(c p) n -> p c n", p=P)[:, :, c0:c0 + w])\
                  .then_inc(tile_landed[n % W_SLOTS], 16)
                if n == 0:
                    sp.dma_start(gqk[:, 0:512].rearrange("p (h n) -> p h n", h=AH),
                                 a["q_norm"].partition_broadcast(P).unsqueeze(1).to_broadcast([P, AH, HD]))\
                      .then_inc(rows_landed, 16)
                    sp.dma_start(gqk[:, 512:640].rearrange("p (h n) -> p h n", h=AKV),
                                 a["k_norm"].partition_broadcast(P).unsqueeze(1).to_broadcast([P, AKV, HD]))\
                      .then_inc(rows_landed, 16)
                    sp.dma_start(lmask_f, a["lmask"]).then_inc(mask_landed, 16)
                    for t, name_ in ((g_o[:, :], "hg_out_norm"), (gqk2[:, 0:HD], "q_norm_g_2"),
                                     (gqk2[:, HD:2 * HD], "k_norm_g_2"), (g_m[:, :], "mlstm_norm_g_2")):
                        sp.dma_start(t, a[name_].partition_broadcast(P)).then_inc(rows_landed, 16)
            for b in range(NB):
                sp.wait_ge(x_ready, b + 1)
                sp.dma_start(out[b * P:(b + 1) * P, :], x[:, b, :]).then_inc(stored, 16)
            sp.wait_ge(stored, NB * 16)

        @block.tensor
        def _(pe):
            made = [0]

            def begin(*name):
                n = PLAN[name]
                assert n == made[0], (name, n, made[0])
                made[0] += 1
                if n >= 8:
                    pe.wait_ge(bank_emptied[n % 8], n // 8)
                return ps[:, n % 8, :]

            def tile(name, k, w):
                n = TILE_NO[name]
                pe.wait_ge(tile_landed[n % W_SLOTS], 16 * (n // W_SLOTS + 1))
                slot = n % W_SLOTS * TILE
                return wring[:, slot:slot + k * w].rearrange("p (c n) -> p c n", c=k)

            def turn(name, src):
                for b in range(NB):
                    for h in range(2):
                        o = begin(name, b, h)
                        for c in range(4):
                            last = nc.tensor.transpose(o[:, c * P:(c + 1) * P],
                                                       src[:, b, (4 * h + c) * P:(4 * h + c + 1) * P], ident)
                        last.then_inc(product_done, 1)

            def by_rows(name, lhs, k=KD, w=512, wide=512):
                wt = tile(name, k, wide)
                for b in range(NB):
                    for c0 in range(0, wide, w):
                        o = begin(*((name, b) if wide == w else (name, b, c0 // w)))
                        for c in range(k):
                            last = nc.tensor.matmul(o[:, 0:w], lhs[:, c, b * P:(b + 1) * P], wt[:, c, c0:c0 + w],
                                                    start=(c == 0), stop=(c == k - 1))
                        last.then_inc(product_done, 1)

            def by_cols(name, w=512):
                wt = tile(name, KD, w)
                for h in range(w // 256):
                    o = begin(name, h)
                    for c2 in range(2):
                        for c in range(KD):
                            n0 = (2 * h + c2) * P
                            last = nc.tensor.matmul(o[:, c2 * S:(c2 + 1) * S], wt[:, c, n0:n0 + P], hT[:, c, :],
                                                    start=(c == 0), stop=(c == KD - 1))
                    last.then_inc(product_done, 1)

            def wait_turned(name):
                for b in range(NB):
                    for h in range(2):
                        wait_moved(pe, name, b, h)

            pe.wait_ge(const_landed, 16)
            pe.wait_ge(h_ready, 2)
            turn("n1T", h_t)
            wait_turned("n1T")
            by_rows("in_q", hT)
            by_rows("in_kv", hT, w=256, wide=256)
            for n in ("in_hq", "in_hf", "in_hb"):
                by_cols(n)
            for n in ("in_hi", "in_hg", "in_g0", "in_g1", "in_g2", "in_g3"):
                by_rows(n, hT)

            pe.wait_ge(a_rot, 2)
            for b in range(NB):
                o = begin("a_qT", b)
                for j in range(4):
                    last = nc.tensor.transpose(o[:, j * P:(j + 1) * P], qn[:, b, j * P:(j + 1) * P], ident)
                last.then_inc(product_done, 1)
            o = begin("a_kT")
            for b in range(NB):
                last = nc.tensor.transpose(o[:, b * P:(b + 1) * P], qn[:, b, 512:640], ident)
            last.then_inc(product_done, 1)
            wait_moved(pe, "a_qT", 0)
            wait_moved(pe, "a_qT", 1)
            wait_moved(pe, "a_kT")
            for b in range(NB):
                for i in range(2):
                    for g in range(AKV):
                        o = begin("a_S", b, i, g)
                        r = slice(g * HD, (g + 1) * HD)
                        for j in range(2):
                            last = nc.tensor.matmul(o[:, j * S:(j + 1) * S], a_qT[r, 2 * i + j, b * P:(b + 1) * P],
                                                    a_kT[r, :], start=True, stop=True)
                        last.then_inc(product_done, 1)
            for b in range(NB):
                pe.wait_ge(a_probs, 8 * b + 8)
                for s_b in range(NB):
                    for q in range(2):
                        o = begin("a_PT", b, s_b, q)
                        for i in range(4):
                            last = nc.tensor.transpose(o[:, i * P:(i + 1) * P],
                                                       a_P[:, b, 4 * q + i, s_b * P:(s_b + 1) * P], ident)
                        last.then_inc(product_done, 1)
                for s_b in range(NB):
                    for q in range(2):
                        wait_moved(pe, "a_PT", b, s_b, q)
                o = begin("a_Y", b)
                for h in range(AH):
                    for s_b in range(NB):
                        g = h % 2
                        last = nc.tensor.matmul(o[:, h * HD:(h + 1) * HD], a_PT[:, s_b, h, :],
                                                qkv[:, s_b, 640 + g * HD:640 + (g + 1) * HD],
                                                start=(s_b == 0), stop=(s_b == NB - 1))
                last.then_inc(product_done, 1)
                pe.wait_ge(a_out, b + 1)
                o = begin("a_YT", b)
                for c in range(4):
                    last = nc.tensor.transpose(o[:, c * P:(c + 1) * P], a_y[:, b, c * P:(c + 1) * P], ident)
                last.then_inc(product_done, 1)

            pe.wait_ge(g_ks, 1)
            for b in range(NB):
                o = begin("g_diag", b)
                for h in range(GH):
                    c = slice(h * S + b * P, h * S + (b + 1) * P)
                    last = nc.tensor.matmul(o[:, h * P:(h + 1) * P], ksum[:, c], hqs[:, c], start=True, stop=True)
                last.then_inc(product_done, 1)
            for n, lv in enumerate(reversed(range(LEVELS))):
                pe.wait_ge(g_decayed, n + 1)
                for d in range(2):
                    for b in (range(NB) if lv < LEVELS - 1 else [0]):
                        o = begin("g_A", lv, b, d)
                        sb_, tb = (b, b) if lv < LEVELS - 1 else (d, 1 - d)
                        for h in range(GH):
                            last = nc.tensor.matmul(o[:, h * P:(h + 1) * P],
                                                    kd[n % 2][:, d, h * S + sb_ * P:h * S + (sb_ + 1) * P],
                                                    qd[n % 2][:, d, h * S + tb * P:h * S + (tb + 1) * P],
                                                    start=True, stop=True)
                        last.then_inc(product_done, 1)
            pe.wait_ge(g_filled, 1)
            for b in range(NB):
                o = begin("g_O", b)
                for h in range(GH):
                    for s_b in range(NB):
                        last = nc.tensor.matmul(o[:, h * P:(h + 1) * P], AT[:, s_b, h, b * P:(b + 1) * P],
                                                hi[:, s_b, h * P:(h + 1) * P], start=(s_b == 0), stop=(s_b == NB - 1))
                last.then_inc(product_done, 1)
            for b in range(NB):
                pe.wait_ge(g_out, b + 1)
                o = begin("g_OT", b)
                for c in range(4):
                    last = nc.tensor.transpose(o[:, c * P:(c + 1) * P], o_t[:, b, c * P:(c + 1) * P], ident)
                last.then_inc(product_done, 1)

            for b in range(NB):
                wait_moved(pe, "a_YT", b)
                wait_moved(pe, "g_OT", b)
            wa, wh = tile("up_att", 4, D), tile("up_hg", 4, D)
            for b in range(NB):
                for h in range(2):
                    for name, lhs, wt in (("up_att", yT, wa), ("up_hg", oT, wh)):
                        o = begin(name, b, h)
                        for c in range(4):
                            last = nc.tensor.matmul(o, lhs[:, c, b * P:(b + 1) * P], wt[:, c, h * 512:(h + 1) * 512],
                                                    start=(c == 0), stop=(c == 3))
                        last.then_inc(product_done, 1)
            pe.wait_ge(merged_ready, 4)
            turn("mT", merged)
            wait_turned("mT")
            for n in ("out0", "out1"):
                by_rows(n, hT)

            pe.wait_ge(h_ready, 4)
            turn("n2T", h_t)
            wait_turned("n2T")
            for i in range(4):
                by_cols(f"peer_q{i}")
            for i in range(4):
                for h in range(2):
                    wait_moved(pe, f"peer_q{i}", h)
            keys = tile("keys", 1, 2048)
            for b in range(NB):
                for q in range(4):
                    o = begin("keys", b, q)
                    for i in range(4):
                        n = 4 * q + i
                        last = nc.tensor.matmul(o[:, i * P:(i + 1) * P], pqT[:, n, b * P:(b + 1) * P],
                                                keys[:, 0, n * P:(n + 1) * P], start=True, stop=True)
                    last.then_inc(product_done, 1)
            pe.wait_ge(c_ready, 1)
            for i in range(12):
                wt = tile(f"ada{i}", KD, 512)
                o = begin(f"ada{i}")
                for c in range(KD):
                    last = nc.tensor.matmul(o, c_rep[:, c, :], wt[:, c, :], start=(c == 0), stop=(c == KD - 1))
                last.then_inc(product_done, 1)
            pe.wait_ge(pT_landed, 16)
            by_rows("ple_proj", pT, k=2, w=512, wide=D)

            pe.sem_inc(v_free, V_RING)

            def experts(head, banks, closing=False):
                for j in range(TOPK):
                    pe.wait_ge(diag_built, head * TOPK + j + 1)
                    pe.wait_ge(v_landed[j], (head + 1) * 16)
                    for h in range(2):
                        last = nc.tensor.matmul(banks[h], diag[:, j % DIAG_RING, :],
                                                v_ring[:, j, h * 512:(h + 1) * 512],
                                                start=False, stop=(closing and j == TOPK - 1), skip_group_check=True)
                    last.then_inc(v_free, 1)

            for b in range(NB):
                banks = [begin("experts", b, 0), begin("experts", b, 1)]
                for h in range(2):
                    nc.tensor.matmul(banks[h], ident, x[:, b, h * 512:(h + 1) * 512], start=True, stop=False,
                                     skip_group_check=True)
                with pe.Fori(b * PH, b * PH + PH - 1) as head:
                    experts(head, banks)
                experts(b * PH + PH - 1, banks, closing=True)
                pe.wait_ge(v_free, (b + 1) * SLOTS + V_RING)
                pe.sem_inc(product_done, 2)

            pe.wait_ge(h_ready, 6)
            turn("n3T", h_t)
            wait_turned("n3T")
            for n in ("ple0", "ple1"):
                by_rows(n, hT)

            pe.wait_ge(h_ready, 8)
            turn("n4T", h_t)
            wait_turned("n4T")
            for n in ("in2_q", "in2_k", "in2_v"):
                by_rows(n, hT)
            for n in ("in2_qm", "in2_km"):
                by_cols(n)
            for n in ("in2_vm", "in2_og"):
                by_rows(n, hT)
            wt = tile("in2_if", KD, 8)
            o = begin("in2_if")
            for g in range(2):
                for c in range(KD):
                    last = nc.tensor.matmul(o[0:GH, g * S:(g + 1) * S], wt[:, c, g * GH:(g + 1) * GH], hT[:, c, :],
                                            start=(c == 0), stop=(c == KD - 1))
            last.then_inc(product_done, 1)
            pe.wait_ge(d_norm, 2)
            for name, lo in (("d_qT", 0), ("d_kT", 512)):
                for b in range(NB):
                    o = begin(name, b)
                    for j in range(4):
                        last = nc.tensor.transpose(o[:, j * P:(j + 1) * P], qk2[:, b, lo + j * P:lo + (j + 1) * P],
                                                   ident)
                    last.then_inc(product_done, 1)
            for b in range(NB):
                wait_moved(pe, "d_qT", b)
                wait_moved(pe, "d_kT", b)
            for b in range(NB):
                w = (b + 1) * P
                for i in range(2):
                    for g in range(2):
                        o = begin("d_S", b, i, g)
                        r = slice(g * HD, (g + 1) * HD)
                        for j in range(2):
                            last = nc.tensor.matmul(o[:, j * w:(j + 1) * w], d_qT[r, 2 * i + j, b * P:(b + 1) * P],
                                                    d_kT[r, 2 * i + j, 0:w], start=True, stop=True)
                        last.then_inc(product_done, 1)
            pe.wait_ge(m_rows, 1)
            o = begin("m_cols")
            for n, row in enumerate((5, 7)):
                for b in range(NB):
                    last = nc.tensor.transpose(o[:, (2 * n + b) * GH:(2 * n + b + 1) * GH],
                                               gl[0:GH, row, b * P:(b + 1) * P], ident[0:GH, 0:GH])
            last.then_inc(product_done, 1)
            for i in range(2):
                o = begin("m_M", i)
                for g in range(2):
                    last = nc.tensor.matmul(o[:, g * S:(g + 1) * S],
                                            const[0:GH, C_SEL + (2 * i + g) * P:C_SEL + (2 * i + g + 1) * P],
                                            gl[0:GH, 6, :], start=True, stop=True)
                last.then_inc(product_done, 1)
            pe.wait_ge(qkm_ready, 1)
            for h in range(GH):
                o = begin("m_S", h)
                nc.tensor.matmul(o[:, 0:S], qkm[:, 4 + h, 0:P], qkm[:, h, :], start=True, stop=True)
                nc.tensor.matmul(o[:, S:S + P], qkm[:, 4 + h, P:S], qkm[:, h, P:S], start=True, stop=True)\
                  .then_inc(product_done, 1)
            for b in range(NB):
                pe.wait_ge(d_probs, 8 * b + 8)
                P2 = (d_P0, d_P1)[b]
                for s_b in range(b + 1):
                    for q in range(2):
                        o = begin("d_PT", b, s_b, q)
                        for i in range(4):
                            last = nc.tensor.transpose(o[:, i * P:(i + 1) * P],
                                                       P2[:, 4 * q + i, s_b * P:(s_b + 1) * P], ident)
                        last.then_inc(product_done, 1)
                for s_b in range(b + 1):
                    for q in range(2):
                        wait_moved(pe, "d_PT", b, s_b, q)
                o = begin("d_Y", b)
                for h in range(AH):
                    for s_b in range(b + 1):
                        last = nc.tensor.matmul(o[:, h * HD:(h + 1) * HD], d_PT[:, s_b, h, :],
                                                va[:, s_b, h * HD:(h + 1) * HD], start=(s_b == 0), stop=(s_b == b))
                last.then_inc(product_done, 1)
            pe.wait_ge(m_A, GH)
            for b in range(NB):
                def pair(s_b, h):
                    return DT0[:, h, b * P:(b + 1) * P] if s_b == 0 else DT1[:, h, :]
                o = begin("m_num", b)
                for h in range(GH):
                    for s_b in range(b + 1):
                        last = nc.tensor.matmul(o[:, h * P:(h + 1) * P], pair(s_b, h), vm[:, s_b, h * P:(h + 1) * P],
                                                start=(s_b == 0), stop=(s_b == b))
                last.then_inc(product_done, 1)
                o = begin("m_den", b)
                for h in range(GH):
                    for s_b in range(b + 1):
                        last = nc.tensor.matmul(o[:, h:h + 1], pair(s_b, h), one, start=(s_b == 0), stop=(s_b == b))
                last.then_inc(product_done, 1)
            pe.wait_ge(cat_ready, 4)
            turn("catT", cat)
            wait_turned("catT")
            for n in ("out2_0", "out2_1"):
                by_rows(n, hT)
            pe.wait_ge(h_ready, 10)
            turn("n5T", h_t)
            wait_turned("n5T")
            for i in range(6):
                by_cols(f"gate{i}", TILES[TILE_NO[f"gate{i}"]][2])
                by_cols(f"up{i}", TILES[TILE_NO[f"up{i}"]][2])
            outs = [begin("down", b, h) for b in range(NB) for h in range(2)]
            for i in range(6):
                k = TILES[TILE_NO[f"down{i}"]][1]
                wt = tile(f"down{i}", k, D)
                pe.wait_ge(ff_ready, min(2 * i + 2, FC // 2))
                for n, o in enumerate(outs):
                    b, h = n // 2, n % 2
                    for c in range(k):
                        f = 4 * i + c
                        last = nc.tensor.matmul(o, gT[:, f, b * P:(b + 1) * P], wt[:, c, h * 512:(h + 1) * 512],
                                                start=(f == 0), stop=(f == FC - 1))
                    if i == 5:
                        last.then_inc(product_done, 1)
                if i < 5:
                    last.then_inc(down_used, 1)

        @block.scalar
        def _(act):
            steps = [0]

            def link(ins):
                steps[0] += 1
                ins.then_inc(act_step, 1)
                act.wait_ge(act_step, steps[0])

            def rsqrt(n):
                act.wait_ge(ms_ready, n + 1)
                link(nc.scalar.activation(stat(lnms, n), stat(ms, n), ACT.Ln))
                nc.scalar.activation(stat(rstd, n), stat(lnms, n), ACT.Exp, scale=-0.5).then_inc(rstd_ready, 1)

            def squares(k):
                for b in range(NB):
                    n = NORM_STAT[k] + b
                    nc.scalar.activation(h_t[:, b, :], x[:, b, :], ACT.Square, accum_out=stat(ms, n))\
                      .then_inc(sq_summed, 1)
                for b in range(NB):
                    rsqrt(NORM_STAT[k] + b)

            def move(dst, *name, n=512, src=None):
                wait_product(act, *name)
                nc.scalar.activation(dst, bank(name, n) if src is None else src, ACT.Copy).then_inc(emptied(*name), 1)

            def move_turned(name):
                for b in range(NB):
                    for h in range(2):
                        o = PLAN[(name, b, h)] % 8
                        move(hT[:, 4 * h:4 * h + 4, b * P:(b + 1) * P], name, b, h,
                             src=ps[:, o, :].rearrange("p (c t) -> p c t", c=4))

            act.wait_ge(lb_sub, 1)
            nc.scalar.activation(lbs[:, 0:16], lbs[:, 0:16], ACT.Exp).then_inc(lb_exp, 1)
            act.wait_ge(x_landed, 16)
            squares(0)
            move_turned("n1T")
            rsqrt(A_STAT)
            rsqrt(A_STAT + 1)
            for h in range(2):
                wait_product(act, "in_hq", h)
                nc.scalar.activation(hqs[:, h * 512:(h + 1) * 512], bank(("in_hq", h)), ACT.Tanh, scale=0.5)\
                  .then_inc(hq_exp, 1)
            for d, n in enumerate(("in_hf", "in_hb")):
                for h in range(2):
                    wait_product(act, n, h)
                    nc.scalar.activation(kk[:, d, h * 512:(h + 1) * 512], bank((n, h)), ACT.Exp, scale=-1.0)\
                      .then_inc(emptied(n, h), 1)
            for b in range(NB):
                move(hi[:, b, :], "in_hi", b)
            for b in range(NB):
                wait_product(act, "in_hg", b)
                nc.scalar.activation(hgs[:, b, :], bank(("in_hg", b)), ACT.Tanh, scale=0.5).then_inc(hg_exp, 1)
            for d in range(2):
                act.wait_ge(hf_ready, d + 1)
                nc.scalar.activation(lf[:, d, :], kk[:, d, :], ACT.Ln).then_inc(lf_ready, 1)
            for i in range(4):
                for b in range(NB):
                    n = f"in_g{i}"
                    wait_product(act, n, b)
                    nc.scalar.activation(gts[:, b, i * 512:(i + 1) * 512], bank((n, b)), ACT.Tanh, scale=0.5)\
                      .then_inc(emptied(n, b), 1)
            for b in range(NB):
                o = PLAN[("a_qT", b)] % 8
                move(a_qT[:, :, b * P:(b + 1) * P], "a_qT", b, src=ps[:, o, :].rearrange("p (c t) -> p c t", c=4))
            move(a_kT, "a_kT", n=S)
            act.wait_ge(mask_packed, 1)
            for b in range(NB):
                for n in range(4):
                    i, g = n // 2, n % 2
                    act.wait_ge(a_max, 4 * b + n + 1)
                    for j in range(2):
                        h = 4 * i + 2 * j + g
                        nc.scalar.activation(a_P[:, b, h, :], bank(("a_S", b, i, g), S, j * S), ACT.Exp,
                                             bias=mx1[:, 8 * b + h:8 * b + h + 1], scale=HD ** -0.5,
                                             accum_out=sum1[:, 8 * b + h:8 * b + h + 1]).then_inc(a_probs, 1)
            for b in range(NB):
                for q in range(2):
                    o = PLAN[("a_PT", b, 0, q)] % 8
                    move(a_PT[:, 0, 4 * q:4 * q + 4, :], "a_PT", b, 0, q,
                         src=ps[:, o, :].rearrange("p (c t) -> p c t", c=4))
                o = PLAN[("a_YT", b)] % 8
                move(yT[:, :, b * P:(b + 1) * P], "a_YT", b, src=ps[:, o, :].rearrange("p (c t) -> p c t", c=4))
            for n in range(LEVELS):
                act.wait_ge(g_diff, n + 1)
                nc.scalar.activation(E[n % 2], E[n % 2], ACT.Exp).then_inc(g_exp, 1)
            for b in range(NB):
                rsqrt(G_STAT + b)
            for b in range(NB):
                o = PLAN[("g_OT", b)] % 8
                move(oT[:, :, b * P:(b + 1) * P], "g_OT", b, src=ps[:, o, :].rearrange("p (c t) -> p c t", c=4))
            move_turned("mT")
            act.wait_ge(residual_ready, 1)
            squares(1)
            move_turned("n2T")
            for i in range(4):
                for h in range(2):
                    o = PLAN[(f"peer_q{i}", h)] % 8
                    move(pqT[:, 4 * i + 2 * h:4 * i + 2 * h + 2, :], f"peer_q{i}", h,
                         src=ps[:, o, :].rearrange("p (c t) -> p c t", c=2))
            act.wait_ge(lane_landed, 16)
            nc.scalar.activation(c_e, lane[:, L_C:L_C + KD], ACT.Tanh, scale=0.5).then_inc(c_exp, 1)
            for b in range(NB):
                for q in range(4):
                    o = PLAN[("keys", b, q)] % 8
                    move(sc[:, b, 4 * q:4 * q + 4, :], "keys", b, q, src=ps[:, o, :].rearrange("p (c t) -> p c t", c=4))

            def best(b):
                act.wait_ge(best_ready, b + 1)
                nc.scalar.activation(best_v, best_v, ACT.Exp).then_inc(best_exp, 1)

            for i in range(12):
                move(mod[:, i // 2, (i % 2) * 512:(i % 2 + 1) * 512], f"ada{i}")
                if i == 7:
                    best(0)
            for b in range(NB):
                for h in range(2):
                    move(pp[:, b, h * 512:(h + 1) * 512], "ple_proj", b, h)
            best(1)

            def spread(head):
                for half in range(2):
                    act.wait_ge(gelu_in, 2 * head + half + 1)
                    nc.scalar.activation(ge[1], ge[0], ACT.Tanh, scale=GELU_C).then_inc(gelu_exp, 1)
                    act.wait_ge(w_ready, 2 * head + half + 1)
                    for j in range(HALF):
                        act.wait_ge(v_free, head * TOPK + half * HALF + j + 1 + V_RING - DIAG_RING)
                        nc.scalar.activation(diag[:, j, :], ident, ACT.Copy,
                                             scale=w_now[:, half * HALF + j:half * HALF + j + 1])\
                          .then_inc(diag_built, 1)

            with act.Fori(0, NB * PH) as head:
                spread(head)
            for b in range(NB):
                for h in range(2):
                    move(x[:, b, h * 512:(h + 1) * 512], "experts", b, h)
            squares_after = [("experts", b, h) for b in range(NB) for h in range(2)]
            for n in squares_after:
                wait_moved(act, *n)
            squares(2)
            move_turned("n3T")
            for i in range(2):
                for b in range(NB):
                    n = f"ple{i}"
                    wait_product(act, n, b)
                    if i == 1:
                        act.wait_ge(ple_done, b + 1)
                    nc.scalar.activation(tmp2[:, b * 512:(b + 1) * 512], bank((n, b)), ACT.Tanh, scale=0.5)\
                      .then_inc(ple_exp, 1)
            act.wait_ge(ple_done, 4)
            squares(3)
            move_turned("n4T")
            rsqrt(DA_STAT)
            rsqrt(DA_STAT + 1)
            for b in range(NB):
                move(va[:, b, :], "in2_v", b)
            for c in range(2):
                act.wait_ge(conv_done, c + 1)
                nc.scalar.activation(silu_e[:, 4 * c:4 * c + 4, :], qkm[:, 4 * c:4 * c + 4, :], ACT.Tanh, scale=0.5)\
                  .then_inc(conv_exp, 1)
            for b in range(NB):
                move(vm[:, b, :], "in2_vm", b)
            for b in range(NB):
                wait_product(act, "in2_og", b)
                nc.scalar.activation(ogs[:, b, :], bank(("in2_og", b)), ACT.Tanh, scale=0.5)\
                  .then_inc(emptied("in2_og", b), 1)
            act.wait_ge(m_abs, 1)
            link(nc.scalar.activation(gl[0:GH, 2, :], gl[0:GH, 2, :], ACT.Exp))
            nc.scalar.activation(gl[0:GH, 2, :], gl[0:GH, 2, :], ACT.Ln, bias=1.0).then_inc(m_log, 1)
            for name, dst in (("d_qT", d_qT), ("d_kT", d_kT)):
                for b in range(NB):
                    o = PLAN[(name, b)] % 8
                    move(dst[:, :, b * P:(b + 1) * P], name, b, src=ps[:, o, :].rearrange("p (c t) -> p c t", c=4))
            for b in range(NB):
                P2 = (d_P0, d_P1)[b]
                act.wait_ge(d_max, b + 1)
                for h in range(AH):
                    nc.scalar.activation(P2[:, h, :], P2[:, h, :], ACT.Exp, bias=mx2[:, 8 * b + h:8 * b + h + 1],
                                         accum_out=sum2[:, 8 * b + h:8 * b + h + 1]).then_inc(d_probs, 1)
            move(mcols, "m_cols", n=16)
            wait_moved(act, "m_cols")
            link(nc.scalar.activation(emt, mcols[:, 8:16], ACT.Exp, scale=-1.0))
            act.wait_ge(m_D, 2)
            for h in range(GH):
                nc.scalar.activation(DT0[:, h, :], DT0[:, h, :], ACT.Exp, bias=mcols[:, h:h + 1])
                nc.scalar.activation(DT1[:, h, :], DT1[:, h, :], ACT.Exp, bias=mcols[:, GH + h:GH + h + 1])\
                  .then_inc(m_Dexp, 1)
            for b in range(NB):
                for q in range(2):
                    o = PLAN[("d_PT", b, 0, q)] % 8
                    move(d_PT[:, 0, 4 * q:4 * q + 4, :], "d_PT", b, 0, q,
                         src=ps[:, o, :].rearrange("p (c t) -> p c t", c=4))
            rsqrt(M_STAT)
            rsqrt(M_STAT + 1)
            move_turned("catT")
            act.wait_ge(residual_ready, 2)
            squares(4)
            move_turned("n5T")
            for i in range(6):
                for h in range(2 if i < 5 else 1):
                    n = 2 * i + h
                    wait_product(act, f"gate{i}", h)
                    if n >= 1:
                        act.wait_ge(ff_ready, n)
                    nc.scalar.activation(ff_e, bank((f"gate{i}", h)), ACT.Tanh, scale=0.5).then_inc(ff_exp, 1)

        @block.gpsimd
        def _(pool):
            steps = [0]

            def link(ins):
                steps[0] += 1
                ins.then_inc(pool_step, 1)
                pool.wait_ge(pool_step, steps[0])

            pool.dma_start(gain, a["norm_mix"].partition_broadcast(P)).then_inc(gain_landed, 16)
            pool.dma_start(pT, a["pT"].rearrange("(c p) t -> p c t", p=P)).then_inc(pT_landed, 16)
            pool.wait_ge(mask_landed, 16)
            nc.gpsimd.tensor_copy(lmask[:, :], lmask_f).then_inc(mask_packed, 1)
            pool.wait_ge(g_scanned, 1)
            nc.gpsimd.tensor_tensor(ksum, kk[:, 0, :], kk[:, 1, :], ALU.add).then_inc(g_ks, 1)
            nc.gpsimd.memset(at(big, 14848, 2048), 0.0).then_inc(g_zeroed, 1)
            wait_product(pool, "a_YT", 1)
            for i in range(2):
                nc.gpsimd.memset(at(big, R + 2048 + 4096 * i, 4096), 0.0).then_inc(g_zeroed, 1)
            wait_moved(pool, "g_O", 0)
            pool.dma_start(gain, a["norm_ffn"].partition_broadcast(P)).then_inc(gain_landed, 16)
            wait_product(pool, "keys", NB - 1, 3)
            for j in range(6):
                pool.dma_start(scratch_row, a["b_ada"][j * D:(j + 1) * D].partition_broadcast(P))\
                    .then_inc(row_landed, 16)
                wait_moved(pool, f"ada{2 * j}")
                wait_moved(pool, f"ada{2 * j + 1}")
                pool.wait_ge(row_landed, 16 * (j + 1))
                link(nc.gpsimd.tensor_tensor(mod[:, j, :], mod[:, j, :], scratch_row, ALU.add))
            for i, (j, n) in enumerate(((1, "g_mix"), (4, "g_ffn"))):
                pool.dma_start(scratch_row, a[n].partition_broadcast(P)).then_inc(row_landed, 16)
                link(nc.gpsimd.tensor_scalar(mod[:, j, :], mod[:, j, :], 1.0, None, ALU.add))
                pool.wait_ge(row_landed, 16 * (7 + i))
                last = nc.gpsimd.tensor_tensor(mod[:, j, :], mod[:, j, :], scratch_row, ALU.mult)
                if i == 0:
                    link(last)
            last.then_inc(mod_ready, 1)

            pool.wait_ge(routed, NB)
            wait_product(pool, "ple_proj", NB - 1, 1)
            for b in range(NB):
                for h in range(2):
                    wait_moved(pool, "ple_proj", b, h)

            def copy_idx(head, half, count):
                nc.gpsimd.tensor_copy(idx_now[:, half * HALF:(half + 1) * HALF],
                                      idx_t[:, bass.ds(head * TOPK + half * HALF, HALF)]).then_inc(idx_copied, 1)
                pool.wait_ge(idx_copied, count)

            def gather(ring, table, slot, j, landed):
                pool.sem_inc(slot_granted, 1)
                pool.indirect_dma_start(ring[:, slot, :], None, table,
                                        bass.IndirectOffsetOnAxis(idx_now[:, j:j + 1], 0)).then_inc(landed, 16)

            with pool.Fori(0, NB * PH) as head:
                for half in range(2):
                    pool.wait_ge(v_free, head * TOPK + (half + 1) * HALF)
                    copy_idx(head, half, 2 * head + half + 1)
                    for j in range(half * HALF, (half + 1) * HALF):
                        pool.wait_ge(u_free, head * TOPK + j + 1)
                        gather(u_ring, a["peer_u"], j % U_RING, j, u_landed[j % U_RING])
                    for j in range(half * HALF, (half + 1) * HALF):
                        pool.wait_ge(v_free, head * TOPK + j + 1)
                        gather(v_ring, a["peer_v"], j, j, v_landed[j])
            wait_product(pool, "experts", NB - 1, 1)
            pool.dma_start(gain, a["norm_ple"].partition_broadcast(P)).then_inc(gain_landed, 16)

        @block.vector
        def _(dve):
            steps = [0]

            def link(ins):
                steps[0] += 1
                ins.then_inc(dve_step, 1)
                dve.wait_ge(dve_step, steps[0])

            tt = nc.vector.tensor_tensor
            ts = nc.vector.tensor_scalar
            stt = nc.vector.scalar_tensor_tensor

            def mean(n, width):
                ts(stat(ms, n), stat(ms, n), 1.0 / width, EPS, ALU.mult, ALU.add).then_inc(ms_ready, 1)

            def group_squares(n, src, sq, groups, width):
                link(tt(sq, src, src, ALU.mult))
                link(nc.vector.tensor_reduce(stat(ms, n), sq.rearrange("p (g n) -> p g n", g=groups), AX, ALU.add))
                mean(n, width)

            def norm(k, gain_row, shift_row=None):
                for b in range(NB):
                    dve.wait_ge(sq_summed, 2 * k + b + 1)
                    mean(NORM_STAT[k] + b, D)
                for b in range(NB):
                    dve.wait_ge(rstd_ready, NORM_STAT[k] + b + 1)
                    last = stt(h_t[:, b, :], x[:, b, :], stat(rstd, NORM_STAT[k] + b), gain_row, ALU.mult, ALU.mult)
                    if shift_row is not None:
                        link(last)
                        last = tt(h_t[:, b, :], h_t[:, b, :], shift_row, ALU.add)
                    last.then_inc(h_ready, 1)

            def heads(t, n):
                return t.rearrange("p (h n) -> p h n", h=n)

            def sigmoid(t):
                link(ts(t, t, 1.0, None, ALU.add))
                link(nc.vector.reciprocal(t, t))

            dve.wait_ge(lane_landed, 16)
            r0, r1 = lane[:, L_LB:L_LB + 8], lane[:, L_LB + 8:L_LB + 16]
            link(tt(lbs[:, 16:24], r0, r1, ALU.max))
            tt(lbs[:, 0:8], r0, lbs[:, 16:24], ALU.subtract)
            tt(lbs[:, 8:16], r1, lbs[:, 16:24], ALU.subtract).then_inc(lb_sub, 1)
            dve.wait_ge(lb_exp, 1)
            link(tt(one_lb, lbs[:, 0:8], lbs[:, 8:16], ALU.add))
            link(nc.vector.reciprocal(one_lb, one_lb))
            link(tt(lb, lbs[:, 0:8], one_lb, ALU.mult))
            link(ts(one_lb, lb, -1.0, 1.0, ALU.mult, ALU.add))

            dve.wait_ge(gain_landed, 16)
            norm(0, gain)
            for b in range(NB):
                wait_product(dve, "in_q", b)
                nc.vector.tensor_copy(qkv[:, b, 0:512], bank(("in_q", b))).then_inc(emptied("in_q", b), 1)
            for b in range(NB):
                wait_product(dve, "in_kv", b)
                nc.vector.tensor_copy(qkv[:, b, 512:768], bank(("in_kv", b), 256)).then_inc(emptied("in_kv", b), 1)
            dve.wait_ge(rows_landed, 16 * 6)
            dve.wait_ge(const_landed, 16)
            for b in range(NB):
                wait_moved(dve, "in_q", b)
                wait_moved(dve, "in_kv", b)
                group_squares(A_STAT + b, qkv[:, b, 0:640], rot[:, b, :], 10, HD)
            for b in range(NB):
                dve.wait_ge(rstd_ready, A_STAT + b + 1)
                q = qkv[:, b, 0:640]
                link(tt(heads(q, 10), heads(q, 10), stat(rstd, A_STAT + b).unsqueeze(2).to_broadcast([P, 10, HD]),
                        ALU.mult))
                link(tt(q, q, gqk[:, :], ALU.mult))
                cs = const[:, C_ROPE + 64 * b:C_ROPE + 64 * (b + 1)].rearrange("p (f a n) -> p f a n", f=2, a=2)
                v5 = q.rearrange("p (h a s n) -> p h a s n", h=10, a=2, s=2)
                o5 = qn[:, b, :].rearrange("p (h a s n) -> p h a s n", h=10, a=2, s=2)
                r5 = rot[:, b, :].rearrange("p (h a s n) -> p h a s n", h=10, a=2, s=2)
                cos = cs[:, 0].unsqueeze(1).to_broadcast([P, 10, 2, 16])
                sin = cs[:, 1].unsqueeze(1).to_broadcast([P, 10, 2, 16])
                for s in range(2):
                    tt(o5[:, :, :, s, :], v5[:, :, :, s, :], cos, ALU.mult)
                    last = tt(r5[:, :, :, s, :], v5[:, :, :, 1 - s, :], sin, ALU.mult)
                link(last)
                tt(o5[:, :, :, 0, :], o5[:, :, :, 0, :], r5[:, :, :, 0, :], ALU.subtract)
                tt(o5[:, :, :, 1, :], o5[:, :, :, 1, :], r5[:, :, :, 1, :], ALU.add).then_inc(a_rot, 1)
            for h in range(2):
                dve.wait_ge(hq_exp, h + 1)
                t = hqs[:, h * 512:(h + 1) * 512]
                stt(t, t, 1.0, bank(("in_hq", h)), ALU.add, ALU.mult).then_inc(emptied("in_hq", h), 1)
            for d, n in enumerate(("in_hf", "in_hb")):
                for h in range(2):
                    wait_moved(dve, n, h)
                sigmoid(kk[:, d, :])
                for h in range(GH):
                    t = kk[:, d, h * S:(h + 1) * S]
                    c = d * GH + h
                    last = ts(t, t, one_lb[:, c:c + 1], lb[:, c:c + 1], ALU.mult, ALU.add)
                last.then_inc(hf_ready, 1)
            for d in range(2):
                dve.wait_ge(lf_ready, d + 1)
                ts(kk[:, d, :], kk[:, d, :], -1.0, 1.0, ALU.mult, ALU.add)
                for h in range(GH):
                    l, o = lf[:, d, h * S:(h + 1) * S], Pc[:, d, h * S:(h + 1) * S]
                    if d == 0:
                        last = nc.vector.tensor_tensor_scan(o, one.to_broadcast([P, S]), l, 0.0, ALU.mult, ALU.add)
                    else:
                        nc.vector.memset(o[:, 0:1], 0.0)
                        last = nc.vector.tensor_tensor_scan(o[:, 1:S], one.to_broadcast([P, S - 1]), l[:, 0:S - 1],
                                                            0.0, ALU.mult, ALU.add)
                if d == 1:
                    last.then_inc(g_scanned, 1)
            for b in range(NB):
                dve.wait_ge(hg_exp, b + 1)
                stt(hgs[:, b, :], hgs[:, b, :], 1.0, bank(("in_hg", b)), ALU.add, ALU.mult).then_inc(emptied("in_hg", b), 1)
            for b in range(NB):
                for n in range(4):
                    i, g = n // 2, n % 2
                    wait_product(dve, "a_S", b, i, g)
                    m = mx1[:, 8 * b + 4 * i + g:8 * b + 4 * i + g + 3:2]
                    link(nc.vector.tensor_reduce(m, heads(bank(("a_S", b, i, g)), 2), AX, ALU.max))
                    ts(m, m, -HD ** -0.5, None, ALU.mult).then_inc(a_max, 1)
            for b in range(NB):
                for n in range(4):
                    dve.wait_ge(a_probs, 8 * b + 2 * n + 2)
                    dve.sem_inc(emptied("a_S", b, n // 2, n % 2), 1)
            for b in range(NB):
                s8 = sum1[:, 8 * b:8 * b + 8]
                link(nc.vector.reciprocal(s8, s8))
                for q in range(2):
                    wait_product(dve, "a_PT", b, 1, q)
                    nc.vector.tensor_copy(a_PT[:, 1, 4 * q:4 * q + 4, :], heads(bank(("a_PT", b, 1, q)), 4))\
                      .then_inc(emptied("a_PT", b, 1, q), 1)
                wait_product(dve, "a_Y", b)
                tt(heads(a_y[:, b, :], AH), heads(bank(("a_Y", b)), AH), s8.unsqueeze(2).to_broadcast([P, AH, HD]),
                   ALU.mult).then_inc(a_out, 1)
                dve.wait_ge(a_out, b + 1)
                dve.sem_inc(emptied("a_Y", b), 1)
            dve.wait_ge(g_zeroed, 3)
            dve.wait_ge(mask_packed, 1)
            wait_product(dve, "a_YT", 1)

            def masked(mask, dst, *name):
                wait_product(dve, *name)
                nc.vector.copy_predicated(dst, mask.unsqueeze(1).to_broadcast([P, GH, P]), heads(bank(name), GH))\
                  .then_inc(emptied(*name), 1)

            def level_mask(lv, d):
                return lmask[:, (2 * lv + d) * P:(2 * lv + d + 1) * P]

            def differences(n):
                m = 1 << (LEVELS - 1 - n)
                p4 = Pc.rearrange("p d (g s m) -> p (d g) s m", s=2, m=m)
                e4 = E[n % 2].rearrange("p (g s m) -> p g s m", s=2, m=m)
                ref = p4[:, :, 0, m - 1:m].to_broadcast([P, 2 * GH * S // (2 * m), m])
                tt(e4[:, :, 0, :], ref, p4[:, :, 0, :], ALU.subtract)
                tt(e4[:, :, 1, :], p4[:, :, 1, :], ref, ALU.subtract).then_inc(g_diff, 1)

            def decayed(n):
                m = 1 << (LEVELS - 1 - n)
                dve.wait_ge(g_exp, n + 1)
                if n >= 2:
                    lv = LEVELS - 1 - (n - 2)
                    wait_product(dve, "g_A", lv, 0 if n == 2 else NB - 1, 1)
                view = "p (g s m) -> p g s m"
                for d in range(2):
                    e = E[n % 2][:, d * GH * S:(d + 1) * GH * S].rearrange(view, s=2, m=m)
                    q4, k4 = hqs.rearrange(view, s=2, m=m), kk[:, d, :].rearrange(view, s=2, m=m)
                    qo, ko = (t[n % 2][:, d, :].rearrange(view, s=2, m=m) for t in (qd, kd))
                    qs, ks = (1, 0) if d == 0 else (0, 1)
                    tt(qo[:, :, qs, :], q4[:, :, qs, :], e[:, :, qs, :], ALU.mult)
                    last = tt(ko[:, :, ks, :], k4[:, :, ks, :], e[:, :, ks, :], ALU.mult)
                last.then_inc(g_decayed, 1)

            def collect(n):
                lv = LEVELS - 1 - n
                if n == 0:
                    for d in range(2):
                        wait_product(dve, "g_A", lv, 0, d)
                        last = nc.vector.tensor_copy(AT[:, d, :, (1 - d) * P:(2 - d) * P],
                                                     heads(bank(("g_A", lv, 0, d)), GH))
                        last.then_inc(emptied("g_A", lv, 0, d), 1)
                    return
                for d in range(2):
                    for b in range(NB):
                        wait_moved(dve, *(("g_A", lv, b, 0) if d else ("g_A", lv + 1, b, 1) if n > 1 else
                                          ("g_diag", b)))
                        masked(level_mask(lv, d), AT[:, b, :, b * P:(b + 1) * P], "g_A", lv, b, d)

            for b in range(NB):
                masked(level_mask(LEVELS - 1, 0), AT[:, b, :, b * P:(b + 1) * P], "g_diag", b)
            differences(0)
            for n in range(LEVELS):
                if n + 1 < LEVELS:
                    if n >= 1:
                        dve.wait_ge(g_decayed, n)
                    differences(n + 1)
                decayed(n)
                if n >= 1:
                    collect(n - 1)
            collect(LEVELS - 1)
            wait_moved(dve, "g_A", 0, NB - 1, 1)
            dve.sem_inc(g_filled, 1)
            for b in range(NB):
                wait_product(dve, "g_O", b)
                ts(o_t[:, b, :], bank(("g_O", b)), 0.5, None, ALU.mult).then_inc(emptied("g_O", b), 1)
                wait_moved(dve, "g_O", b)
                group_squares(G_STAT + b, o_t[:, b, :], o_sq, GH, P)
            for b in range(NB):
                o = heads(o_t[:, b, :], GH)
                dve.wait_ge(rstd_ready, G_STAT + b + 1)
                link(tt(o, o, stat(rstd, G_STAT + b).unsqueeze(2).to_broadcast([P, GH, P]), ALU.mult))
                link(stt(o, o, 0.5, g_o[:, :].unsqueeze(1).to_broadcast([P, GH, P]), ALU.mult, ALU.mult))
                tt(o_t[:, b, :], o_t[:, b, :], hgs[:, b, :], ALU.mult).then_inc(g_out, 1)
            for i in range(4):
                for b in range(NB):
                    wait_moved(dve, f"in_g{i}", b)
            for b in range(NB):
                for h in range(2):
                    c = slice(h * 512, (h + 1) * 512)
                    wait_product(dve, "up_att", b, h)
                    stt(merged[:, b, c], gts[:, b, c], 1.0, bank(("up_att", b, h)), ALU.add, ALU.mult)\
                        .then_inc(emptied("up_att", b, h), 1)
                    wait_product(dve, "up_hg", b, h)
                    stt(tmp, gts[:, b, D + h * 512:D + (h + 1) * 512], 1.0, bank(("up_hg", b, h)), ALU.add, ALU.mult)\
                        .then_inc(emptied("up_hg", b, h), 1)
                    wait_moved(dve, "up_att", b, h)
                    wait_moved(dve, "up_hg", b, h)
                    tt(merged[:, b, c], merged[:, b, c], tmp, ALU.add).then_inc(merged_ready, 1)
                    dve.wait_ge(merged_ready, 2 * b + h + 1)
            for i in range(2):
                for b in range(NB):
                    c = slice(i * 512, (i + 1) * 512)
                    n = (f"out{i}", b)
                    wait_product(dve, *n)
                    stt(x[:, b, c], bank(n), 0.5, x[:, b, c], ALU.mult, ALU.add).then_inc(emptied(*n), 1)
            for i in range(2):
                for b in range(NB):
                    wait_moved(dve, f"out{i}", b)
            dve.sem_inc(residual_ready, 1)
            dve.wait_ge(gain_landed, 32)
            norm(1, gain)
            dve.wait_ge(c_exp, 1)
            link(ts(c_e, c_e, 0.5, 0.5, ALU.mult, ALU.add))
            link(tt(c_s, c_e, lane[:, L_C:L_C + KD], ALU.mult))
            nc.vector.tensor_copy(c_rep, c_s.unsqueeze(2).to_broadcast([P, KD, P])).then_inc(c_ready, 1)

            def top16(values, indices, src, spare):
                link(nc.vector.max(values[:, 0:8], src))
                link(nc.vector.match_replace(spare, values[:, 0:8], src, NEG))
                nc.vector.max_index(indices[:, 0:8], values[:, 0:8], src)
                link(nc.vector.max(values[:, 8:16], spare))
                return nc.vector.max_index(indices[:, 8:16], values[:, 8:16], spare)

            for b in range(NB):
                for q in range(4):
                    wait_moved(dve, "keys", b, q)
                for n in range(2 * PH):
                    last = top16(top_v[:, n, :], top_i[:, n, :], sc[:, b, n, :], cut[:, 0:NKEYS])
                link(last)
                nc.vector.tensor_copy(top_f.rearrange("p h s k -> p (h s k)"), top_i.rearrange("p n k -> p (n k)"))
                v4 = top_v.rearrange("p (h s) k -> p h s k", s=2)
                link(tt(cand, v4[:, :, 0, :].unsqueeze(3).to_broadcast([P, PH, TOPK, TOPK]),
                        v4[:, :, 1, :].unsqueeze(2).to_broadcast([P, PH, TOPK, TOPK]), ALU.add))
                if b >= 1:
                    dve.wait_ge(best_exp, b)
                for h in range(PH):
                    last = top16(best_v[:, h, :], best_i[:, h, :], cand[:, h].rearrange("p i j -> p (i j)"), cut)
                link(last)
                nc.vector.tensor_copy(g_max, best_v[:, :, 0])
                flat_i = best_i.rearrange("p h k -> p (h k)")
                ts(pos_u[:, 0, :], flat_i, 4, None, ALU.logical_shift_right)
                link(ts(pos_u[:, 1, :], flat_i, 15, None, ALU.bitwise_and))
                tt(best_v, best_v, g_max.unsqueeze(2).to_broadcast([P, PH, TOPK]), ALU.subtract)\
                    .then_inc(best_ready, 1)
                link(nc.vector.tensor_copy(pos_f.rearrange("p s n -> p (s n)"), pos_u.rearrange("p s n -> p (s n)")))
                for s in range(2):
                    h2 = hot.rearrange("p (n k) -> p n k", k=TOPK)
                    h4 = hot.rearrange("p (h n k) -> p h n k", h=PH, k=TOPK)
                    link(tt(h2, iota.unsqueeze(1).to_broadcast([P, SLOTS, TOPK]),
                            pos_f[:, s, :].unsqueeze(2).to_broadcast([P, SLOTS, TOPK]), ALU.is_equal))
                    link(tt(h4, h4, top_f[:, :, s, :].unsqueeze(2).to_broadcast([P, PH, TOPK, TOPK]), ALU.mult))
                    link(nc.vector.tensor_reduce(part[:, s, :], h2, AX, ALU.add))
                stt(idx_t[:, b * SLOTS:(b + 1) * SLOTS], part[:, 0, :], float(NKEYS), part[:, 1, :],
                    ALU.mult, ALU.add)
                dve.wait_ge(best_exp, b + 1)
                link(nc.vector.tensor_reduce(g_sum, best_v, AX, ALU.add))
                link(nc.vector.reciprocal(g_sum, g_sum))
                gb = heads(gate_t[:, b * SLOTS:(b + 1) * SLOTS], PH)
                tt(gb, best_v, g_sum.unsqueeze(2).to_broadcast([P, PH, TOPK]), ALU.mult).then_inc(routed, 1)

            dve.wait_ge(routed, NB)
            dve.wait_ge(h_ready, 4)
            dve.sem_inc(u_free, U_RING)
            for b in range(NB):
                with dve.Fori(b * PH, (b + 1) * PH) as head:
                    for half in range(2):
                        for j in range(HALF):
                            n = half * HALF + j
                            r = n % U_RING
                            per = TOPK // U_RING
                            dve.wait_ge(u_landed[r], 16 * (head * per + n // U_RING + 1))
                            nc.vector.tensor_tensor_reduce(u_ring[:, r, :], u_ring[:, r, :], h_t[:, b, :], 1.0, 0.0,
                                                           ALU.mult, ALU.add, a_dot[:, j:j + 1]).then_inc(u_free, 1)
                        dve.wait_ge(u_free, head * TOPK + (half + 1) * HALF + U_RING)
                        g = 2 * head + half

                        def chain(ins, k):
                            ins.then_inc(gelu_step, 1)
                            dve.wait_ge(gelu_step, g * 4 + k)
                        chain(tt(ge[2], a_dot, a_dot, ALU.mult), 1)
                        chain(ts(ge[2], ge[2], 0.044715, 1.0, ALU.mult, ALU.add), 2)
                        tt(ge[0], ge[2], a_dot, ALU.mult).then_inc(gelu_in, 1)
                        chain(stt(ge[3], a_dot, 0.5, gate_t[:, bass.ds(head * TOPK + half * HALF, HALF)],
                                  ALU.mult, ALU.mult), 3)
                        dve.wait_ge(gelu_exp, g + 1)
                        stt(w_now[:, half * HALF:(half + 1) * HALF], ge[1], 1.0, ge[3], ALU.add, ALU.mult)\
                            .then_inc(w_ready, 1)
                        dve.wait_ge(w_ready, g + 1)
                        dve.sem_inc(gelu_step, 1)
            dve.wait_ge(gain_landed, 48)
            norm(2, gain)
            for i in range(2):
                for b in range(NB):
                    n = (f"ple{i}", b)
                    c = slice(i * 512, (i + 1) * 512)
                    t = tmp2[:, b * 512:(b + 1) * 512]
                    dve.wait_ge(ple_exp, 2 * i + b + 1)
                    dve.sem_inc(emptied(*n), 1)
                    link(stt(t, t, 1.0, pp[:, b, c], ALU.add, ALU.mult))
                    stt(x[:, b, c], t, 0.5, x[:, b, c], ALU.mult, ALU.add).then_inc(ple_done, 1)
            dve.wait_ge(ple_done, 4)
            dve.wait_ge(mod_ready, 1)
            norm(3, mod[:, 1, :], mod[:, 0, :])
            for i, n in enumerate(("in2_q", "in2_k")):
                for b in range(NB):
                    wait_product(dve, n, b)
                    nc.vector.tensor_copy(qk2[:, b, i * 512:(i + 1) * 512], bank((n, b))).then_inc(emptied(n, b), 1)
            for b in range(NB):
                wait_moved(dve, "in2_q", b)
                wait_moved(dve, "in2_k", b)
                group_squares(DA_STAT + b, qk2[:, b, :], sq2[:, b, :], 16, HD)
            for b in range(NB):
                dve.wait_ge(rstd_ready, DA_STAT + b + 1)
                q = qk2[:, b, :]
                link(tt(heads(q, 16), heads(q, 16), stat(rstd, DA_STAT + b).unsqueeze(2).to_broadcast([P, 16, HD]),
                        ALU.mult))
                q4 = q.rearrange("p (s h n) -> p s h n", s=2, h=AH)
                tt(q4, q4, heads(gqk2[:, :], 2).unsqueeze(2).to_broadcast([P, 2, AH, HD]), ALU.mult)\
                    .then_inc(d_norm, 1)
            for i, n in enumerate(("in2_qm", "in2_km")):
                for h in range(2):
                    wait_product(dve, n, h)
                    for c2 in range(2):
                        ch = 4 * i + 2 * h + c2
                        z = bank((n, h), S, c2 * S)
                        y = qkm[:, ch, :]
                        w = [lane[:, L_CONV + 8 * k + ch:L_CONV + 8 * k + ch + 1] for k in range(4)]
                        link(ts(y, z, w[3], lane[:, L_CONVB + ch:L_CONVB + ch + 1], ALU.mult, ALU.add))
                        for k in range(3):
                            back = 3 - k
                            last = stt(y[:, back:S], z[:, 0:S - back], w[k], y[:, back:S], ALU.mult, ALU.add)
                            link(last)
                    dve.sem_inc(emptied(n, h), 1)
                dve.sem_inc(conv_done, 1)
            for c in range(2):
                dve.wait_ge(conv_exp, c + 1)
                last = stt(qkm[:, 4 * c:4 * c + 4, :], silu_e[:, 4 * c:4 * c + 4, :], 1.0,
                           qkm[:, 4 * c:4 * c + 4, :], ALU.add, ALU.mult)
            last.then_inc(qkm_ready, 1)
            wait_product(dve, "in2_if")
            row = [gl[0:GH, r, :] for r in range(10)]
            bi = bank(("in2_if",))
            ts(row[0], bi[0:GH, 0:S], lane[0:GH, L_IF:L_IF + 1], None, ALU.add)
            link(ts(row[1], bi[0:GH, S:2 * S], lane[0:GH, L_IF + 1:L_IF + 2], None, ALU.add))
            dve.sem_inc(emptied("in2_if"), 1)
            link(ts(row[3], row[1], 0.0, None, ALU.min))
            stt(row[2], row[3], 2.0, row[1], ALU.mult, ALU.subtract).then_inc(m_abs, 1)
            link(nc.vector.memset(row[9], 0.0))
            dve.wait_ge(m_log, 1)
            link(tt(row[3], row[3], row[2], ALU.subtract))
            link(nc.vector.tensor_tensor_scan(row[4], one[0:GH, :].to_broadcast([GH, S]), row[3], 0.0, ALU.mult, ALU.add))
            link(tt(row[5], row[0], row[4], ALU.subtract))
            link(nc.vector.tensor_tensor_scan(row[6], row[9], row[5], 0.0, ALU.add, ALU.max))
            tt(row[7], row[4], row[6], ALU.add).then_inc(m_rows, 1)
            for b in range(NB):
                w = (b + 1) * P
                P2 = (d_P0, d_P1)[b]
                for n in range(4):
                    i, g = n // 2, n % 2
                    wait_product(dve, "d_S", b, i, g)
                    lc = const[:, C_LOGC + b * S:C_LOGC + b * S + w].unsqueeze(1).to_broadcast([P, 2, w])
                    stt(P2[:, 4 * i + g:4 * i + g + 3:2, :], heads(bank(("d_S", b, i, g), 2 * w), 2), HD ** -0.5, lc,
                        ALU.mult, ALU.add).then_inc(emptied("d_S", b, i, g), 1)
                for n in range(4):
                    wait_moved(dve, "d_S", b, n // 2, n % 2)
                m = mx2[:, 8 * b:8 * b + 8]
                link(nc.vector.tensor_reduce(m, P2, AX, ALU.max))
                ts(m, m, -1.0, None, ALU.mult).then_inc(d_max, 1)
            for i in range(2):
                wait_product(dve, "m_M", i)
                mb = heads(bank(("m_M", i)), 2)
                tt(DT0[:, 2 * i:2 * i + 2, :], tri.unsqueeze(1).to_broadcast([P, 2, S]), mb, ALU.subtract)
                tt(DT1[:, 2 * i:2 * i + 2, :], tri[:, 0:P].unsqueeze(1).to_broadcast([P, 2, P]), mb[:, :, P:S],
                   ALU.subtract).then_inc(m_D, 1)
                dve.wait_ge(m_D, i + 1)
                dve.sem_inc(emptied("m_M", i), 1)
            for h in range(GH):
                dve.wait_ge(m_Dexp, h + 1)
                wait_product(dve, "m_S", h)
                s_ = bank(("m_S", h))
                stt(DT0[:, h, :], s_[:, 0:S], 0.25 * P ** -0.5, DT0[:, h, :], ALU.mult, ALU.mult)
                stt(DT1[:, h, :], s_[:, S:S + P], 0.25 * P ** -0.5, DT1[:, h, :], ALU.mult, ALU.mult).then_inc(m_A, 1)
                dve.wait_ge(m_A, h + 1)
                dve.sem_inc(emptied("m_S", h), 1)
            for b in range(NB):
                s8 = sum2[:, 8 * b:8 * b + 8]
                dve.wait_ge(d_probs, 8 * b + 8)
                link(nc.vector.reciprocal(s8, s8))
                if b == 1:
                    for q in range(2):
                        wait_product(dve, "d_PT", b, 1, q)
                        nc.vector.tensor_copy(d_PT[:, 1, 4 * q:4 * q + 4, :], heads(bank(("d_PT", b, 1, q)), 4))\
                          .then_inc(emptied("d_PT", b, 1, q), 1)
                wait_product(dve, "d_Y", b)
                tt(heads(cat[:, b, 0:512], AH), heads(bank(("d_Y", b)), AH), s8.unsqueeze(2).to_broadcast([P, AH, HD]),
                   ALU.mult).then_inc(cat_ready, 1)
                dve.wait_ge(cat_ready, b + 1)
                dve.sem_inc(emptied("d_Y", b), 1)
            for b in range(NB):
                wait_product(dve, "m_den", b)
                wait_moved(dve, "m_cols")
                dn, em = den[:, 4 * b:4 * b + 4], emt[:, 4 * b:4 * b + 4]
                nq = bank(("m_den", b), GH)
                link(stt(dn, nq, -1.0, em, ALU.mult, ALU.max))
                link(tt(dn, nq, dn, ALU.max))
                dve.sem_inc(emptied("m_den", b), 1)
                link(nc.vector.reciprocal(dn, dn))
                hm = cat[:, b, 512:1024]
                tt(heads(hm, GH), heads(bank(("m_num", b)), GH), dn.unsqueeze(2).to_broadcast([P, GH, P]), ALU.mult)\
                    .then_inc(emptied("m_num", b), 1)
                wait_moved(dve, "m_num", b)
                group_squares(M_STAT + b, hm, hm_sq, GH, P)
            for b in range(NB):
                hm = cat[:, b, 512:1024]
                dve.wait_ge(rstd_ready, M_STAT + b + 1)
                link(tt(heads(hm, GH), heads(hm, GH), stat(rstd, M_STAT + b).unsqueeze(2).to_broadcast([P, GH, P]),
                        ALU.mult))
                link(stt(hm, hm, 0.5, g_m[:, :], ALU.mult, ALU.mult))
                wait_moved(dve, "in2_og", b)
                stt(hm, ogs[:, b, :], 1.0, hm, ALU.add, ALU.mult).then_inc(cat_ready, 1)

            def gated_add(src, gate_row, b, c, t, factor):
                link(stt(t, src, factor, gate_row[:, c], ALU.mult, ALU.mult))
                return tt(x[:, b, c], x[:, b, c], t, ALU.add)

            for i in range(2):
                for b in range(NB):
                    n = (f"out2_{i}", b)
                    wait_product(dve, *n)
                    if i == 1:
                        wait_moved(dve, "out2_0", b)
                    gated_add(bank(n), mod[:, 2, :], b, slice(i * 512, (i + 1) * 512),
                              tmp2[:, b * 512:(b + 1) * 512], 1.0)\
                        .then_inc(emptied(*n), 1)
            for i in range(2):
                for b in range(NB):
                    wait_moved(dve, f"out2_{i}", b)
            dve.sem_inc(residual_ready, 1)
            norm(4, mod[:, 4, :], mod[:, 3, :])
            for i in range(6):
                for h in range(2 if i < 5 else 1):
                    n = 2 * i + h
                    dve.wait_ge(ff_exp, n + 1)
                    link(stt(ff_e, ff_e, 1.0, bank((f"gate{i}", h)), ALU.add, ALU.mult))
                    dve.sem_inc(emptied(f"gate{i}", h), 1)
                    wait_product(dve, f"up{i}", h)
                    tt(gT[:, 2 * n:2 * n + 2, :].rearrange("p c t -> p (c t)"), ff_e, bank((f"up{i}", h)), ALU.mult)\
                        .then_inc(ff_ready, 1)
                    dve.wait_ge(ff_ready, n + 1)
                    dve.sem_inc(emptied(f"up{i}", h), 1)
            for b in range(NB):
                for h in range(2):
                    wait_product(dve, "down", b, h)
                    if b == 1 and h == 0:
                        dve.wait_ge(x_ready, 1)
                    last = gated_add(bank(("down", b, h)), mod[:, 5, :], b, slice(h * 512, (h + 1) * 512),
                                     tmp2[:, h * 512:(h + 1) * 512], 0.5)
                last.then_inc(x_ready, 1)


def kernel(**inputs):
    import concourse.bacc as bacc
    from concourse.bass_utils import run_bass_kernel_spmd

    i = {k: np.asarray(v) for k, v in inputs.items()}
    order = np.arange(AH * HD).reshape(AKV, AH // AKV, HD).transpose(1, 0, 2).reshape(-1)
    w_in = i["w_in"][0]
    arrays = {
        "x": i["x"][0], "w_in": np.concatenate([w_in[:, order], w_in[:, AH * HD:]], axis=1),
        "w_up_att": i["w_up_att"][0][order], "w_up_hg": i["w_up_hg"][0], "w_out": i["w_out"][0],
        "peer_wq": i["peer_wq"][0],
        "subkeys": i["peer_subkeys"][0].transpose(3, 0, 1, 2).reshape(P, -1),
        "peer_u": i["peer_u"][0], "peer_v": i["peer_v"][0],
        "w_ada": i["w_ada_2"][0], "b_ada": i["b_ada_2"][0], "ple_gate": i["ple_gate"][0],
        "ple_proj": i["ple_proj"][0], "pT": i["p"][0, 0].T, "w_in_2": i["w_in_2"][0], "w_out_2": i["w_out_2"][0],
        "w_gate": i["w_gate_2"][0], "w_up": i["w_up_2"][0], "w_down": i["w_down_2"][0],
        "norm_mix": i["norm_mix"][0], "norm_ffn": i["norm_ffn"][0], "norm_ple": i["norm_ple"][0],
        "g_mix": i["g_mix_2"][0], "g_ffn": i["g_ffn_2"][0],
        "q_norm": i["q_norm"][0], "k_norm": i["k_norm"][0], "hg_out_norm": i["hg_out_norm"][0],
        "q_norm_g_2": i["q_norm_g_2"][0], "k_norm_g_2": i["k_norm_g_2"][0], "mlstm_norm_g_2": i["mlstm_norm_g_2"][0],
    }
    pad = np.zeros((P, 2), np.float32)
    pad[:GH, 0], pad[:GH, 1] = i["b_igate_2"][0], i["b_fgate_2"][0]
    arrays["lane"] = np.concatenate([
        i["hg_lb_raw"].reshape(2, 2, GH, P).transpose(3, 0, 1, 2).reshape(P, 16),
        i["w_conv_2"][0].reshape(4, 8, P).transpose(2, 0, 1).reshape(P, 32),
        i["b_conv_2"][0].reshape(8, P).T, i["c_2"][0].reshape(KD, P).T, pad], axis=1)

    pos = np.arange(S)
    inv = 10000.0 ** (-np.arange(16, dtype=np.float32) / 16)
    ang = np.stack([(pos // 64)[:, None] * inv, (pos % 64)[:, None] * inv], axis=1).astype(np.float32)
    const = np.zeros((P, C_END), np.float32)
    rope = np.stack([np.cos(ang), np.sin(ang)], axis=1).reshape(NB, P, 64)
    const[:, C_ROPE:C_LOGC] = rope.transpose(1, 0, 2).reshape(P, -1)
    back = pos[:, None] - pos[None, :]
    count = sum(((back >= 0) & (back <= w) & (back % d == 0)).astype(int) for w, d in ((128, 1), (512, 4), (2048, 16)))
    logc = np.where(count > 0, np.log(np.maximum(count, 1)), -1e30).astype(np.float32)
    const[:, C_LOGC:C_TRI] = logc.reshape(NB, P, S).transpose(1, 0, 2).reshape(P, -1)
    const[:, C_TRI:C_IOTA] = np.where(pos[None, :] >= np.arange(P)[:, None], 0.0, -1e30)
    const[:, C_IOTA:C_IDENT] = np.arange(TOPK)
    const[:, C_IDENT:C_SEL] = np.eye(P)
    for h in range(GH):
        const[h, C_SEL + h * P:C_SEL + (h + 1) * P] = 1.0
    const[:, C_ONE] = 1.0
    arrays["const"] = const
    lmask = np.zeros((P, LEVELS, 2, P), np.float32)
    s_, t_ = np.arange(P)[:, None], np.arange(P)[None, :]
    for lv in range(LEVELS - 1):
        m = 1 << lv
        same = s_ // (2 * m) == t_ // (2 * m)
        lmask[:, lv, 0] = same & (s_ // m % 2 == 0) & (t_ // m % 2 == 1)
        lmask[:, lv, 1] = same & (s_ // m % 2 == 1) & (t_ // m % 2 == 0)
    lmask[:, LEVELS - 1, 0] = s_ == t_
    arrays["lmask"] = lmask.reshape(P, -1)

    nc = bacc.Bacc("TRN2", target_bir_lowering=False, num_devices=1)
    sent, a = {}, {}
    for name, v in arrays.items():
        v = np.ascontiguousarray(v)
        sent[f"in_{name}"] = v
        a[name] = nc.dram_tensor(f"in_{name}", v.shape, mybir.dt.from_np(v.dtype), kind="ExternalInput").ap()
    out = nc.dram_tensor("out", (S, D), F32, kind="ExternalOutput").ap()
    two_blocks(nc, a, out)
    r = run_bass_kernel_spmd(nc, [sent], core_ids=[0])
    return r.results[0]["out"].reshape(1, S, D)
```

```python
from contextlib import ExitStack

import numpy as np
import concourse.bass as bass
from concourse import mybir

F32 = mybir.dt.float32
U32 = mybir.dt.uint32
U8 = mybir.dt.uint8
ALU = mybir.AluOpType
ACT = mybir.ActivationFunctionType
AX = mybir.AxisListType.X

P = 128
S = 256
NB = S // P
D = 1024
KD = D // P
EPS = 1e-6
HD = 64
AH, AKV = 8, 2
GH = 4
LEVELS = 8
PH = 8
TOPK = 16
NKEYS = 128
SLOTS = PH * TOPK
HALF = 8
U_RING, V_RING, DIAG_RING = 8, 8, 8
FF = 2816
FC = FF // P
NEG = -3.0e38
W_SLOTS = 3
TILE = KD * 512
ADA_PARTS = (0, 1, 2, 3, 6, 7, 8, 9, 4, 5, 10, 11)
LATE = 9
EARLY = 6
ADA_AT = {0: 3, 2: 4, 4: 5}
PLE_SCALE, PLE_TURN, PLE_GATE, PLE_ADD = PH + 2, PH + 4, PH + 6, PH + 7
SEARCH_END = 6
GELU_C = 0.7978845608028654

C_ROPE = 0
C_LOGC = C_ROPE + NB * 64
C_TRI = C_LOGC + NB * S
C_IOTA = C_TRI + S
C_IDENT = C_IOTA + TOPK
C_SEL = C_IDENT + P
C_ONE = C_SEL + GH * P
C_END = C_ONE + 1

L_LB = 0
L_CONV = 16
L_CONVB = 48
L_C = 56
L_IF = 64
L_MIX, L_PLE = 66, 74
L_ADA = 82
L_GAIN2 = 114
L_EPS = 130
L_END = 131


def tile_list():
    ada = [(f"ada{i}", KD, 512, "w_ada", 0, 512 * ADA_PARTS[i]) for i in range(12)]
    t, at = [ada[0]], 0
    for n, w in (("q", 512), ("kv", 256), ("hq", 512), ("hf", 512), ("hb", 512), ("hi", 512), ("hg", 512),
                 ("g0", 512), ("g1", 512), ("g2", 512), ("g3", 512)):
        t.append(("in_" + n, KD, w, "w_in", 0, at))
        at += w
    t += ada[1:EARLY]
    t += [("up_att", 4, D, "w_up_att", 0, 0), ("up_hg", 4, D, "w_up_hg", 0, 0)]
    t += [(f"out{i}", KD, 512, "w_out", 0, 512 * i) for i in range(2)]
    t += [(f"peer_q{i}", KD, 512, "peer_wq", 0, 512 * i) for i in range(4)]
    t += [("peer_q0b", KD, 512, "peer_wq", 0, 0), ("ple_proj", 2, D, "ple_proj", 0, 0)]
    t += ada[EARLY:]
    t += [(f"ple{i}", KD, 512, "ple_gate", 0, 512 * i) for i in range(2)]
    t += [("in2_" + n, KD, 512, "w_in_2", 0, 512 * i) for i, n in enumerate(("q", "k", "v", "qm", "km"))]
    t += [("in2_if", KD, 2 * GH, "w_in_2", 0, 7 * 512)]
    t += [(f"in2_{n}", KD, 512, "w_in_2", 0, 512 * i) for i, n in ((5, "vm"), (6, "og"))]
    t += [(f"out2_{i}", KD, 512, "w_out_2", 0, 512 * i) for i in range(2)]
    for i in range(6):
        w = min(512, FF - 512 * i)
        t += [(f"gate{i}", KD, w, "w_gate", 0, 512 * i), (f"up{i}", KD, w, "w_up", 0, 512 * i)]
    t += [(f"down{i}", min(4, FC - 4 * i), D, "w_down", 512 * i, 0) for i in range(6)]
    return t


TILES = tile_list()
TILE_NO = {t[0]: n for n, t in enumerate(TILES)}


def ada_products(i):
    return [(f"ada{i}",)] + ([("ada_col", i - 1)] if i not in (0, 1, EARLY) and i <= 8 else [])


def product_list():
    def turned(n):
        return [(n, b, h) for b in range(NB) for h in range(2)]

    def half(n, b):
        return [(n, b, h) for h in range(2)]

    def rows(n):
        return [(n, b) for b in range(NB)]

    def cols(n, halves=2):
        return [(n, h) for h in range(halves)]

    p = [("ada0",)] + turned("n1T") + [("ada_col", 0)]
    p += rows("in_q") + rows("in_kv") + cols("in_hq") + cols("in_hf") + cols("in_hb")
    p += rows("in_hi") + rows("in_hg")
    for i in range(4):
        p += rows(f"in_g{i}")
    p += [("a_qT", 0), ("a_qT", 1), ("a_kT",)]
    p += [("a_S", b, i, g) for b in range(NB) for i in range(2) for g in range(2)]
    for b in range(NB):
        p += [("a_PT", b, sb, q) for sb in range(NB) for q in range(2)] + [("a_Y", b), ("a_YT", b)]
    p += [("g_diag", 0), ("g_diag", 1)]
    made = 1
    for n, lv in enumerate(reversed(range(LEVELS))):
        for i in range(made, ADA_AT.get(n, made)):
            p += ada_products(i)
        made = ADA_AT.get(n, made)
        p += [("g_A", lv, b, d) for d in range(2) for b in (range(NB) if lv < LEVELS - 1 else [0])]
    p += [("g_O", 0), ("g_O", 1)] + ada_products(EARLY - 1)
    p += [("g_OT", 0), ("g_OT", 1), ("ada_col", EARLY - 1)]
    p += [(n, b, h) for b in range(NB) for h in range(2) for n in ("up_att", "up_hg")]
    p += turned("mT") + rows("out0") + rows("out1")
    p += half("n2T", 0) + [("peer_q0", 0), ("peer_q1", 0), ("keys", 0, 0), ("peer_q2", 0), ("keys", 0, 1)]
    p += half("n2T", 1) + [("peer_q3", 0), ("keys", 0, 2), ("keys", 0, 3)]
    p += [("peer_q1", 1), ("peer_q2", 1), ("keys", 1, 1), ("peer_q3", 1), ("keys", 1, 2), ("peer_q0b", 1)]
    p += [("keys", 1, 3), ("keys", 1, 0)]
    p += [("ple_proj", b, h) for b in range(NB) for h in range(2)]
    for i in range(EARLY, 12):
        p += ada_products(i)
    p += half("experts", 0) + half("n3T", 0) + [("ple0", 0), ("ple1", 0)] + half("experts", 1)
    p += half("n4T", 0) + [("in2_q", 0)] + half("n3T", 1) + [("ple0", 1), ("ple1", 1), ("in2_k", 0)]
    p += half("n4T", 1) + [("in2_q", 1), ("in2_k", 1)] + rows("in2_v") + cols("in2_qm") + cols("in2_km")
    p += [("d_qT", b) for b in range(NB)] + [("d_kT", b) for b in range(NB)] + [("in2_if",)] + rows("in2_vm")
    p += [("d_S", b, i, g) for b in range(NB) for i in range(2) for g in range(2)] + rows("in2_og")
    p += [("m_cols",), ("m_M", 0), ("m_M", 1)] + [("m_S", h) for h in range(GH)]
    p += [("d_PT", 0, 0, q) for q in range(2)] + [("d_Y", 0)]
    p += [("d_PT", 1, sb, q) for sb in range(NB) for q in range(2)]
    for b in range(NB):
        p += [("m_num", b), ("m_den", b)]
    p += [("d_Y", 1)]
    p += half("catT", 0) + [("out2_0", 0)] + half("catT", 1) + [("out2_0", 1)] + rows("out2_1") + turned("n5T")
    for i in range(6):
        for n in (f"gate{i}", f"up{i}"):
            p += cols(n, 2 if i < 5 else 1)
    p += [("down", b, h) for b in range(NB) for h in range(2)]
    return p


PLAN = {name: n for n, name in enumerate(product_list())}


def two_blocks(nc, a, out):
    with ExitStack() as ctx:
        def sb(name, cols, dt=F32):
            return ctx.enter_context(nc.sbuf_tensor(name, [P, cols], dt))

        def sem(name):
            return ctx.enter_context(nc.semaphore(name))

        x_t = sb("x_t", NB * D)
        big = sb("big", 30720)
        rows2 = sb("rows2", 2 * D)
        const = sb("const", C_END)
        lmask = sb("lmask", LEVELS * 2 * P, U8)
        gqk = sb("gqk", 10 * HD)
        g_o = sb("g_o", P)
        gqk2 = sb("gqk2", 2 * HD)
        g_m = sb("g_m", 512)
        lane = sb("lane", L_END)
        ms = sb("ms", 80)
        lnms = sb("lnms", 80)
        rstd = sb("rstd", 80)
        small = sb("small", 448)
        idx_t = sb("idx_t", NB * SLOTS, U32)
        gate_t = sb("gate_t", NB * SLOTS)
        idx_now = sb("idx_now", 4 * HALF, U32)
        wring = sb("wring", W_SLOTS * TILE)
        c_rep_t = sb("c_rep", KD * P)
        ps = ctx.enter_context(nc.psum_tensor("ps", [P, 8, 512], F32))

        def at(t, lo, n):
            return t[:, lo:lo + n]

        x = x_t[:, :].rearrange("p (b d) -> p b d", b=NB)
        c_rep = c_rep_t[:, :].rearrange("p (c n) -> p c n", c=KD)
        hT = at(big, 0, KD * S).rearrange("p (c t) -> p c t", c=KD)
        gts = at(big, 2048, 4096).rearrange("p (b n) -> p b n", b=NB)
        qkv = at(big, 6144, 1536).rearrange("p (b n) -> p b n", b=NB)
        hi = at(big, 7680, 1024).rearrange("p (b n) -> p b n", b=NB)
        hgs = at(big, 8704, 1024).rearrange("p (b n) -> p b n", b=NB)
        hqs = at(big, 9728, 1024)
        kk = at(big, 10752, 2048).rearrange("p (d n) -> p d n", d=2)
        Pc = at(big, 12800, 2048).rearrange("p (d n) -> p d n", d=2)
        lf = at(big, 14848, 2048).rearrange("p (d n) -> p d n", d=2)
        AT = at(big, 14848, 2048).rearrange("p (s h t) -> p s h t", s=NB, h=GH)
        ksum = at(big, 16896, 1024)
        yT = at(big, 17920, 1024).rearrange("p (c t) -> p c t", c=4)
        oT = at(big, 18944, 1024).rearrange("p (c t) -> p c t", c=4)
        pT = at(big, 26112, 512).rearrange("p (c t) -> p c t", c=2)
        R = 20480
        qn = at(big, R, 1280).rearrange("p (b n) -> p b n", b=NB)
        rot = at(big, R + 1280, 1280).rearrange("p (b n) -> p b n", b=NB)
        a_qT = at(big, R + 2560, 1024).rearrange("p (j t) -> p j t", j=4)
        a_kT = at(big, R + 3584, S)
        a_P = at(big, R + 3840, 4096).rearrange("p (b h s) -> p b h s", b=NB, h=AH)
        a_PT = at(big, R + 7936, 2048).rearrange("p (s h t) -> p s h t", s=NB, h=AH)
        a_y = at(big, R, 1024).rearrange("p (b n) -> p b n", b=NB)
        lmask_f = at(big, R + 4096, LEVELS * 2 * P)
        E = [at(big, R, 2048), rows2[:, :]]
        qd = [at(big, R + 2048 + 4096 * i, 2048).rearrange("p (d n) -> p d n", d=2) for i in range(2)]
        kd = [at(big, R + 4096 + 4096 * i, 2048).rearrange("p (d n) -> p d n", d=2) for i in range(2)]
        o_t = at(big, R, 1024).rearrange("p (b n) -> p b n", b=NB)
        o_sq = at(big, R + 1024, 512)
        merged = at(big, R + 2048, 2048).rearrange("p (b n) -> p b n", b=NB)
        tmp = at(big, R + 4096, 512)
        h2T = [at(big, lo, D).rearrange("p (c t) -> p c t", c=KD) for lo in (0, 26624)]
        pqT = [at(big, lo, 2048).rearrange("p (n t) -> p n t", n=16) for lo in (2048, 20480)]
        sc = [at(big, lo, 2048).rearrange("p (n k) -> p n k", n=16) for lo in (6144, 16384)]
        cand = at(big, 18432, 2048).rearrange("p (h i j) -> p h i j", h=PH, i=TOPK)
        hot = at(big, 18432, 2048)
        mod = at(big, 20480, 2 * D).rearrange("p (j d) -> p j d", j=2)
        ada_rows = [at(big, 512 * (i % 4) if 0 < i < EARLY else 22528 + 512 * (i % 2), 512) for i in range(8)]
        subkeys = at(big, 12288, 2 * PH * NKEYS)
        top_v = at(big, 23552, 256).rearrange("p (n k) -> p n k", n=16)
        top_i = at(big, 23808, 256).bitcast(U32).rearrange("p (n k) -> p n k", n=16)
        top_f = at(big, 24064, 256).rearrange("p (h s k) -> p h s k", h=PH, s=2)
        best_v = at(big, 24320, 128).rearrange("p (h k) -> p h k", h=PH)
        best_i = at(big, 24448, 128).bitcast(U32).rearrange("p (h k) -> p h k", h=PH)
        pos_u = at(big, 24576, 256).bitcast(U32).rearrange("p (s n) -> p s n", s=2)
        pos_f = at(big, 24832, 256).rearrange("p (s n) -> p s n", s=2)
        part = at(big, 25088, 256).rearrange("p (s n) -> p s n", s=2)
        two_in = at(big, 25344, 512)
        cut = at(rows2, D, 512)
        two_v = at(big, 25856, 2 * TOPK).rearrange("p (n k) -> p n k", n=2)
        two_i = at(big, 25888, 2 * TOPK).bitcast(U32).rearrange("p (n k) -> p n k", n=2)
        u_ring = at(big, 0, U_RING * D).rearrange("p (r d) -> p r d", r=U_RING)
        v_ring = at(big, U_RING * D, V_RING * D).rearrange("p (r d) -> p r d", r=V_RING)
        pp = at(big, 26624, NB * D).rearrange("p (b d) -> p b d", b=NB)
        h_t = at(big, 28672, NB * D).rearrange("p (b d) -> p b d", b=NB)
        gain = at(rows2, 0, D)
        scratch_row = at(rows2, D, D)
        diag = at(rows2, 0, DIAG_RING * P).rearrange("p (r n) -> p r n", r=DIAG_RING)
        qk2 = at(big, 2048, 2048).rearrange("p (b n) -> p b n", b=NB)
        va = at(big, 4096, 1024).rearrange("p (b n) -> p b n", b=NB)
        vm = at(big, 5120, 1024).rearrange("p (b n) -> p b n", b=NB)
        ogs = at(big, 6144, 1024).rearrange("p (b n) -> p b n", b=NB)
        qkm = at(big, 7168, 2048).rearrange("p (c t) -> p c t", c=8)
        silu_e = at(big, 9216, 2048).rearrange("p (c t) -> p c t", c=8)
        d_PT = at(big, 9216, 2048).rearrange("p (s h t) -> p s h t", s=NB, h=AH)
        sq2 = at(big, 11264, 2048).rearrange("p (b n) -> p b n", b=NB)
        d_qT = at(big, 11264, 1024).rearrange("p (j t) -> p j t", j=4)
        d_kT = at(big, 12288, 1024).rearrange("p (j t) -> p j t", j=4)
        d_P0 = at(big, 13312, 1024).rearrange("p (h s) -> p h s", h=AH)
        d_P1 = at(big, 14336, 2048).rearrange("p (h s) -> p h s", h=AH)
        DT0 = at(big, 16384, 1024).rearrange("p (h t) -> p h t", h=GH)
        DT1 = at(big, 17408, 512).rearrange("p (h t) -> p h t", h=GH)
        gl = at(big, 17920, 2560).rearrange("p (r t) -> p r t", r=10)
        cat = at(big, 26624, 2048).rearrange("p (b n) -> p b n", b=NB)
        hm_sq = at(big, 17920, 512)
        gT = at(big, 2048, FC * S).rearrange("p (c t) -> p c t", c=FC)
        ff_e = at(big, 7680, 512)
        tmp2 = at(big, 19456, 1024)
        h3T = at(big, 16384, KD * S).rearrange("p (c t) -> p c t", c=KD)

        ident = at(const, C_IDENT, P)
        iota = at(const, C_IOTA, TOPK)
        tri = at(const, C_TRI, S)
        one = at(const, C_ONE, 1)
        eps = at(lane, L_EPS, 1)
        lbs = at(small, 0, 24)
        lb, one_lb = at(small, 24, 8), at(small, 32, 8)
        mx1, sum1 = at(small, 40, 16), at(small, 56, 16)
        g_max, g_sum = at(small, 72, 8), at(small, 80, 8)
        mx2, sum2 = at(small, 88, 16), at(small, 104, 16)
        mcols, emt, den = at(small, 120, 16), at(small, 136, 8), at(small, 144, 8)
        a_dot = at(small, 152, HALF)
        ge = [at(small, 160 + 8 * i, HALF) for i in range(4)]
        w_now = at(small, 192, 2 * HALF)
        c_e, c_s = at(small, 208, 8), at(small, 216, 8)
        modc = at(small, 224, 4 * KD)


        product_done = sem("product_done")
        bank_emptied = [sem(f"bank_emptied{i}") for i in range(8)]
        tile_landed = [sem(f"tile_landed{i}") for i in range(W_SLOTS)]
        down_used = sem("down_used")
        x_landed, const_landed, lane_landed = sem("x_landed"), sem("const_landed"), sem("lane_landed")
        keys_landed = sem("keys_landed")
        rows_landed, mask_landed, pT_landed = sem("rows_landed"), sem("mask_landed"), sem("pT_landed")
        gain_landed, row_landed, row_added = sem("gain_landed"), sem("row_landed"), sem("row_added")
        ms_ready, rstd_ready, h_ready = sem("ms_ready"), sem("rstd_ready"), sem("h_ready")
        dve_step, act_step, pool_step = sem("dve_step"), sem("act_step"), sem("pool_step")
        lb_sub, lb_exp, lb_done = sem("lb_sub"), sem("lb_exp"), sem("lb_done")
        hq_exp, hf_ready, lf_ready, hg_exp = sem("hq_exp"), sem("hf_ready"), sem("lf_ready"), sem("hg_exp")
        a_rot, a_max, a_probs, a_out = sem("a_rot"), sem("a_max"), sem("a_probs"), sem("a_out")
        g_zeroed, g_diff, g_exp, g_decayed, g_ks = (sem(n) for n in ("g_zeroed", "g_diff", "g_exp", "g_decayed", "g_ks"))
        g_scanned, g_filled, g_out, gates_ready, merged_ready = (
            sem(n) for n in ("g_scanned", "g_filled", "g_out", "gates_ready", "merged_ready"))
        c_exp, c_ready, best_ready, best_exp, routed, indexed = (
            sem(n) for n in ("c_exp", "c_ready", "best_ready", "best_exp", "routed", "indexed"))
        u_landed = [sem(f"u_landed{i}") for i in range(U_RING)]
        v_landed = [sem(f"v_landed{i}") for i in range(V_RING)]
        u_free, v_free = sem("u_free"), sem("v_free")
        idx_copied, gelu_in, gelu_exp, w_ready, diag_built = (
            sem(n) for n in ("idx_copied", "gelu_in", "gelu_exp", "w_ready", "diag_built"))
        ple_exp, mod_ready, x_ready = sem("ple_exp"), sem("mod_ready"), sem("x_ready")
        modc_ready = sem("modc_ready")
        d_norm, d_max, d_probs, cat_ready = sem("d_norm"), sem("d_max"), sem("d_probs"), sem("cat_ready")
        conv_done, conv_exp, qkm_ready, og_exp = sem("conv_done"), sem("conv_exp"), sem("qkm_ready"), sem("og_exp")
        m_abs, m_log, m_rows, m_D, m_Dexp, m_A, m_mt = (
            sem(n) for n in ("m_abs", "m_log", "m_rows", "m_D", "m_Dexp", "m_A", "m_mt"))
        ff_exp, ff_ready, stored = sem("ff_exp"), sem("ff_ready"), sem("stored")
        search_step, search_go = sem("search_step"), sem("search_go")
        mask_packed, slot_granted = sem("mask_packed"), sem("slot_granted")
        x_whole, ple_done, gelu_step = sem("x_whole"), sem("ple_done"), sem("gelu_step")

        def bank(name, n=512, lo=0):
            return ps[:, PLAN[name] % 8, lo:lo + n]

        def wait_product(eng, *name):
            eng.wait_ge(product_done, PLAN[name] + 1)

        def wait_moved(eng, *name):
            eng.wait_ge(bank_emptied[PLAN[name] % 8], PLAN[name] // 8 + 1)

        def emptied(*name):
            return bank_emptied[PLAN[name] % 8]

        STATS = [(n, b) for n in ("norm0", "a", "g", "norm1") for b in range(NB)]
        STATS += [("norm2", 0), ("norm3", 0), ("norm2", 1), ("norm3", 1)]
        STATS += [(n, b) for n in ("da", "m", "norm4") for b in range(NB)]
        STAT = [{"a": 10, "g": 4, "da": 16, "m": 4}.get(n, 1) for n, _ in STATS]
        STAT_AT = [sum(STAT[:i]) for i in range(len(STAT))]
        A_STAT, G_STAT, DA_STAT, M_STAT = (STATS.index((n, 0)) for n in ("a", "g", "da", "m"))
        GROUPED = [n for n, w in enumerate(STAT) if w > 1]

        def norm_stat(k, b):
            return STATS.index((f"norm{k}", b))

        def stat(t, n):
            return t[:, STAT_AT[n]:STAT_AT[n] + STAT[n]]

        block = ctx.enter_context(nc.Block())

        @block.sync
        def _(sp):
            sp.dma_start(lane[:, :], a["lane"]).then_inc(lane_landed, 16)
            sp.dma_start(x, a["x"].rearrange("(b p) d -> p b d", p=P)).then_inc(x_landed, 16)
            for n, (name, k, w, src, r0, c0) in enumerate(TILES):
                if n >= W_SLOTS:
                    before = TILES[n - W_SLOTS][0]
                    if before.startswith("down"):
                        sp.wait_ge(down_used, int(before[4:]) + 1)
                    else:
                        sp.wait_ge(product_done, 1 + max(v for p, v in PLAN.items() if p[0] == before))
                if name == "out0":
                    wait_product(sp, "g_O", 0)
                    sp.dma_start(subkeys, a["subkeys"]).then_inc(keys_landed, 16)
                slot = n % W_SLOTS * TILE
                sp.dma_start(wring[:, slot:slot + k * w].rearrange("p (c n) -> p c n", c=k),
                             a[src][r0:r0 + k * P, :].rearrange("(c p) n -> p c n", p=P)[:, :, c0:c0 + w])\
                  .then_inc(tile_landed[n % W_SLOTS], 16)
                if n == 0:
                    sp.dma_start(const[:, :], a["const"]).then_inc(const_landed, 16)
                    sp.dma_start(gqk[:, 0:512].rearrange("p (h n) -> p h n", h=AH),
                                 a["q_norm"].partition_broadcast(P).unsqueeze(1).to_broadcast([P, AH, HD]))\
                      .then_inc(rows_landed, 16)
                    sp.dma_start(gqk[:, 512:640].rearrange("p (h n) -> p h n", h=AKV),
                                 a["k_norm"].partition_broadcast(P).unsqueeze(1).to_broadcast([P, AKV, HD]))\
                      .then_inc(rows_landed, 16)
                    sp.dma_start(lmask_f, a["lmask"]).then_inc(mask_landed, 16)
                    for t, name_ in ((g_o[:, :], "hg_out_norm"), (gqk2[:, 0:HD], "q_norm_g_2"),
                                     (gqk2[:, HD:2 * HD], "k_norm_g_2"), (g_m[:, :], "mlstm_norm_g_2")):
                        sp.dma_start(t, a[name_].partition_broadcast(P)).then_inc(rows_landed, 16)
            for b in range(NB):
                sp.wait_ge(x_ready, b + 1)
                sp.dma_start(out[b * P:(b + 1) * P, :], x[:, b, :]).then_inc(stored, 16)
            sp.wait_ge(stored, NB * 16)

        @block.tensor
        def _(pe):
            made = [0]

            def reserved(*name):
                n = PLAN[name]
                pe.wait_ge(bank_emptied[n % 8], n // 8)
                return ps[:, n % 8, :]

            def begin(*name):
                n = PLAN[name]
                assert n == made[0], (name, n, made[0])
                made[0] += 1
                if n >= 8:
                    pe.wait_ge(bank_emptied[n % 8], n // 8)
                return ps[:, n % 8, :]

            def tile(name, k, w):
                n = TILE_NO[name]
                pe.wait_ge(tile_landed[n % W_SLOTS], 16 * (n // W_SLOTS + 1))
                slot = n % W_SLOTS * TILE
                return wring[:, slot:slot + k * w].rearrange("p (c n) -> p c n", c=k)

            def turn(name, src, blocks=range(NB)):
                for b in blocks:
                    for h in range(2):
                        o = begin(name, b, h)
                        for c in range(4):
                            last = nc.tensor.transpose(o[:, c * P:(c + 1) * P],
                                                       src[:, b, (4 * h + c) * P:(4 * h + c + 1) * P], ident)
                        last.then_inc(product_done, 1)

            def by_rows(name, lhs, k=KD, w=512, wide=512, blocks=range(NB)):
                wt = tile(name, k, wide)
                for b in blocks:
                    for c0 in range(0, wide, w):
                        o = begin(*((name, b) if wide == w else (name, b, c0 // w)))
                        for c in range(k):
                            last = nc.tensor.matmul(o[:, 0:w], lhs[:, c, b * P:(b + 1) * P], wt[:, c, c0:c0 + w],
                                                    start=(c == 0), stop=(c == k - 1))
                        last.then_inc(product_done, 1)

            def by_cols(name, w=512):
                wt = tile(name, KD, w)
                for h in range(w // 256):
                    o = begin(name, h)
                    for c2 in range(2):
                        for c in range(KD):
                            n0 = (2 * h + c2) * P
                            last = nc.tensor.matmul(o[:, c2 * S:(c2 + 1) * S], wt[:, c, n0:n0 + P], hT[:, c, :],
                                                    start=(c == 0), stop=(c == KD - 1))
                    last.then_inc(product_done, 1)

            def wait_turned(name, blocks=range(NB)):
                for b in blocks:
                    for h in range(2):
                        wait_moved(pe, name, b, h)

            def ada_part(i):
                wt = tile(f"ada{i}", KD, 512)
                o = begin(f"ada{i}")
                for c in range(KD):
                    last = nc.tensor.matmul(o, c_rep[:, c, :], wt[:, c, :], start=(c == 0), stop=(c == KD - 1))
                last.then_inc(product_done, 1)
                if i not in (0, 1, EARLY) and i <= 8:
                    ada_col(i - 1)

            def ada_col(i):
                wait_moved(pe, f"ada{i}")
                o = begin("ada_col", i)
                for n in range(4):
                    last = nc.tensor.matmul(o[:, n:n + 1], ada_rows[i][:, n * P:(n + 1) * P], ident[:, 0:1],
                                            start=True, stop=True)
                last.then_inc(product_done, 1)

            pe.wait_ge(c_ready, 1)
            ada_part(0)
            pe.wait_ge(const_landed, 16)
            pe.wait_ge(h_ready, 2)
            turn("n1T", h_t)
            ada_col(0)
            wait_turned("n1T")
            by_rows("in_q", hT)
            by_rows("in_kv", hT, w=256, wide=256)
            for n in ("in_hq", "in_hf", "in_hb"):
                by_cols(n)
            for n in ("in_hi", "in_hg", "in_g0", "in_g1", "in_g2", "in_g3"):
                by_rows(n, hT)

            pe.wait_ge(a_rot, 2)
            for b in range(NB):
                o = begin("a_qT", b)
                for j in range(4):
                    last = nc.tensor.transpose(o[:, j * P:(j + 1) * P], qn[:, b, j * P:(j + 1) * P], ident)
                last.then_inc(product_done, 1)
            o = begin("a_kT")
            for b in range(NB):
                last = nc.tensor.transpose(o[:, b * P:(b + 1) * P], qn[:, b, 512:640], ident)
            last.then_inc(product_done, 1)
            wait_moved(pe, "a_qT", 0)
            wait_moved(pe, "a_qT", 1)
            wait_moved(pe, "a_kT")
            for b in range(NB):
                for i in range(2):
                    for g in range(AKV):
                        o = begin("a_S", b, i, g)
                        r = slice(g * HD, (g + 1) * HD)
                        for j in range(2):
                            last = nc.tensor.matmul(o[:, j * S:(j + 1) * S], a_qT[r, 2 * i + j, b * P:(b + 1) * P],
                                                    a_kT[r, :], start=True, stop=True)
                        last.then_inc(product_done, 1)
            for b in range(NB):
                pe.wait_ge(a_probs, 8 * b + 8)
                for s_b in range(NB):
                    for q in range(2):
                        o = begin("a_PT", b, s_b, q)
                        for i in range(4):
                            last = nc.tensor.transpose(o[:, i * P:(i + 1) * P],
                                                       a_P[:, b, 4 * q + i, s_b * P:(s_b + 1) * P], ident)
                        last.then_inc(product_done, 1)
                for s_b in range(NB):
                    for q in range(2):
                        wait_moved(pe, "a_PT", b, s_b, q)
                o = begin("a_Y", b)
                for h in range(AH):
                    for s_b in range(NB):
                        g = h % 2
                        last = nc.tensor.matmul(o[:, h * HD:(h + 1) * HD], a_PT[:, s_b, h, :],
                                                qkv[:, s_b, 640 + g * HD:640 + (g + 1) * HD],
                                                start=(s_b == 0), stop=(s_b == NB - 1))
                last.then_inc(product_done, 1)
                pe.wait_ge(a_out, b + 1)
                o = begin("a_YT", b)
                for c in range(4):
                    last = nc.tensor.transpose(o[:, c * P:(c + 1) * P], a_y[:, b, c * P:(c + 1) * P], ident)
                last.then_inc(product_done, 1)

            pe.wait_ge(g_ks, 1)
            for b in range(NB):
                o = begin("g_diag", b)
                for h in range(GH):
                    c = slice(h * S + b * P, h * S + (b + 1) * P)
                    last = nc.tensor.matmul(o[:, h * P:(h + 1) * P], ksum[:, c], hqs[:, c], start=True, stop=True)
                last.then_inc(product_done, 1)
            parts = 1
            for n, lv in enumerate(reversed(range(LEVELS))):
                for i in range(parts, ADA_AT.get(n, parts)):
                    ada_part(i)
                parts = ADA_AT.get(n, parts)
                pe.wait_ge(g_decayed, n + 1)
                for d in range(2):
                    for b in (range(NB) if lv < LEVELS - 1 else [0]):
                        o = begin("g_A", lv, b, d)
                        sb_, tb = (b, b) if lv < LEVELS - 1 else (d, 1 - d)
                        for h in range(GH):
                            last = nc.tensor.matmul(o[:, h * P:(h + 1) * P],
                                                    kd[n % 2][:, d, h * S + sb_ * P:h * S + (sb_ + 1) * P],
                                                    qd[n % 2][:, d, h * S + tb * P:h * S + (tb + 1) * P],
                                                    start=True, stop=True)
                        last.then_inc(product_done, 1)
            pe.wait_ge(g_filled, 1)
            for b in range(NB):
                o = begin("g_O", b)
                for h in range(GH):
                    for s_b in range(NB):
                        last = nc.tensor.matmul(o[:, h * P:(h + 1) * P], AT[:, s_b, h, b * P:(b + 1) * P],
                                                hi[:, s_b, h * P:(h + 1) * P], start=(s_b == 0), stop=(s_b == NB - 1))
                last.then_inc(product_done, 1)
            ada_part(EARLY - 1)
            for b in range(NB):
                pe.wait_ge(g_out, b + 1)
                o = begin("g_OT", b)
                for c in range(4):
                    last = nc.tensor.transpose(o[:, c * P:(c + 1) * P], o_t[:, b, c * P:(c + 1) * P], ident)
                last.then_inc(product_done, 1)

            ada_col(EARLY - 1)

            for b in range(NB):
                wait_moved(pe, "a_YT", b)
                wait_moved(pe, "g_OT", b)
            wa, wh = tile("up_att", 4, D), tile("up_hg", 4, D)
            for b in range(NB):
                for h in range(2):
                    for name, lhs, wt in (("up_att", yT, wa), ("up_hg", oT, wh)):
                        o = begin(name, b, h)
                        for c in range(4):
                            last = nc.tensor.matmul(o, lhs[:, c, b * P:(b + 1) * P], wt[:, c, h * 512:(h + 1) * 512],
                                                    start=(c == 0), stop=(c == 3))
                        last.then_inc(product_done, 1)
            pe.wait_ge(merged_ready, 4)
            turn("mT", merged)
            wait_turned("mT")
            for n in ("out0", "out1"):
                by_rows(n, hT)

            def turn_query(b):
                pe.wait_ge(h_ready, 3 + b)
                turn("n2T", h_t, [b])

            def query(name, b):
                wt = tile(name, KD, 512)
                o = begin(name, b)
                for n in range(4):
                    for c in range(KD):
                        last = nc.tensor.matmul(o[:, n * P:(n + 1) * P], wt[:, c, n * P:(n + 1) * P], h2T[b][:, c, :],
                                                start=(c == 0), stop=(c == KD - 1))
                last.then_inc(product_done, 1)

            def score(b, q):
                wait_moved(pe, "peer_q0b" if b and q == 0 else f"peer_q{q}", b)
                o = begin("keys", b, q)
                for i in range(4):
                    n = 4 * q + i
                    last = nc.tensor.matmul(o[:, i * P:(i + 1) * P], pqT[b][:, n, :], subkeys[:, n * P:(n + 1) * P],
                                            start=True, stop=True)
                last.then_inc(product_done, 1)

            turn_query(0)
            wait_turned("n2T", [0])
            pe.wait_ge(keys_landed, 16)
            query("peer_q0", 0)
            query("peer_q1", 0)
            score(0, 0)
            query("peer_q2", 0)
            score(0, 1)
            turn_query(1)
            query("peer_q3", 0)
            score(0, 2)
            score(0, 3)
            wait_turned("n2T", [1])
            query("peer_q1", 1)
            query("peer_q2", 1)
            score(1, 1)
            query("peer_q3", 1)
            score(1, 2)
            query("peer_q0b", 1)
            score(1, 3)
            score(1, 0)
            pe.sem_inc(v_free, V_RING)
            pe.wait_ge(pT_landed, 16)
            by_rows("ple_proj", pT, k=2, w=512, wide=D)
            for i in range(EARLY, LATE):
                ada_part(i)

            def experts(head, banks, closing=False):
                for j in range(TOPK):
                    pe.wait_ge(diag_built, head * TOPK + j + 1)
                    pe.wait_ge(v_landed[j % V_RING], (head * (TOPK // V_RING) + j // V_RING + 1) * 16)
                    for h in range(2):
                        last = nc.tensor.matmul(banks[h], diag[:, j % DIAG_RING, :],
                                                v_ring[:, j % V_RING, h * 512:(h + 1) * 512],
                                                start=False, stop=(closing and j == TOPK - 1), skip_group_check=True)
                    last.then_inc(v_free, 1)

            def residual(b, banks):
                for h in range(2):
                    nc.tensor.matmul(banks[h], ident, x[:, b, h * 512:(h + 1) * 512], start=True, stop=False,
                                     skip_group_check=True)

            banks = [reserved("experts", 0, h) for h in range(2)]
            residual(0, banks)
            for i in range(LATE, 12):
                with pe.Fori(0 if i == LATE else i - LATE + 1, i - LATE + 2) as head:
                    experts(head, banks)
                ada_part(i)
            with pe.Fori(12 - LATE + 1, PH - 1) as head:
                experts(head, banks)
            experts(PH - 1, banks, closing=True)
            for h in range(2):
                begin("experts", 0, h)
            pe.wait_ge(v_free, SLOTS + V_RING)
            pe.sem_inc(product_done, 2)
            banks = [reserved("experts", 1, h) for h in range(2)]
            residual(1, banks)
            with pe.Fori(PH, PLE_SCALE) as head:
                experts(head, banks)
            pe.wait_ge(h_ready, 5)
            turn("n3T", h_t, [0])
            with pe.Fori(PLE_SCALE, PLE_TURN) as head:
                experts(head, banks)
            wait_turned("n3T", [0])
            by_rows("ple0", h3T, blocks=[0])
            by_rows("ple1", h3T, blocks=[0])
            with pe.Fori(PLE_TURN, 2 * PH - 1) as head:
                experts(head, banks)
            experts(2 * PH - 1, banks, closing=True)
            for h in range(2):
                begin("experts", 1, h)
            pe.wait_ge(v_free, 2 * SLOTS + V_RING)
            pe.sem_inc(product_done, 2)

            pe.wait_ge(h_ready, 6)
            turn("n4T", h_t, [0])
            wait_turned("n4T", [0])
            by_rows("in2_q", hT, blocks=[0])
            pe.wait_ge(h_ready, 7)
            turn("n3T", h_t, [1])
            wait_turned("n3T", [1])
            by_rows("ple0", h3T, blocks=[1])
            by_rows("ple1", h3T, blocks=[1])
            by_rows("in2_k", hT, blocks=[0])
            pe.wait_ge(h_ready, 8)
            turn("n4T", h_t, [1])
            wait_turned("n4T", [1])
            by_rows("in2_q", hT, blocks=[1])
            by_rows("in2_k", hT, blocks=[1])
            by_rows("in2_v", hT)
            for n in ("in2_qm", "in2_km"):
                by_cols(n)
            pe.wait_ge(d_norm, 2)
            for name, lo in (("d_qT", 0), ("d_kT", 512)):
                for b in range(NB):
                    o = begin(name, b)
                    for j in range(4):
                        last = nc.tensor.transpose(o[:, j * P:(j + 1) * P], qk2[:, b, lo + j * P:lo + (j + 1) * P],
                                                   ident)
                    last.then_inc(product_done, 1)
            wt = tile("in2_if", KD, 8)
            o = begin("in2_if")
            for g in range(2):
                for c in range(KD):
                    last = nc.tensor.matmul(o[0:GH, g * S:(g + 1) * S], wt[:, c, g * GH:(g + 1) * GH], hT[:, c, :],
                                            start=(c == 0), stop=(c == KD - 1))
            last.then_inc(product_done, 1)
            by_rows("in2_vm", hT)
            for b in range(NB):
                wait_moved(pe, "d_qT", b)
                wait_moved(pe, "d_kT", b)
            for b in range(NB):
                w = (b + 1) * P
                for i in range(2):
                    for g in range(2):
                        o = begin("d_S", b, i, g)
                        r = slice(g * HD, (g + 1) * HD)
                        for j in range(2):
                            last = nc.tensor.matmul(o[:, j * w:(j + 1) * w], d_qT[r, 2 * i + j, b * P:(b + 1) * P],
                                                    d_kT[r, 2 * i + j, 0:w], start=True, stop=True)
                        last.then_inc(product_done, 1)
            by_rows("in2_og", hT)
            pe.wait_ge(m_rows, 1)
            o = begin("m_cols")
            for n, row in enumerate((5, 7)):
                for b in range(NB):
                    last = nc.tensor.transpose(o[:, (2 * n + b) * GH:(2 * n + b + 1) * GH],
                                               gl[0:GH, row, b * P:(b + 1) * P], ident[0:GH, 0:GH])
            last.then_inc(product_done, 1)
            for i in range(2):
                o = begin("m_M", i)
                for g in range(2):
                    last = nc.tensor.matmul(o[:, g * S:(g + 1) * S],
                                            const[0:GH, C_SEL + (2 * i + g) * P:C_SEL + (2 * i + g + 1) * P],
                                            gl[0:GH, 6, :], start=True, stop=True)
                last.then_inc(product_done, 1)
            pe.wait_ge(qkm_ready, 1)
            for h in range(GH):
                o = begin("m_S", h)
                nc.tensor.matmul(o[:, 0:S], qkm[:, 4 + h, 0:P], qkm[:, h, :], start=True, stop=True)
                nc.tensor.matmul(o[:, S:S + P], qkm[:, 4 + h, P:S], qkm[:, h, P:S], start=True, stop=True)\
                  .then_inc(product_done, 1)
            def probs_turned(b):
                pe.wait_ge(d_probs, 8 * b + 8)
                P2 = (d_P0, d_P1)[b]
                for s_b in range(b + 1):
                    for q in range(2):
                        o = begin("d_PT", b, s_b, q)
                        for i in range(4):
                            last = nc.tensor.transpose(o[:, i * P:(i + 1) * P],
                                                       P2[:, 4 * q + i, s_b * P:(s_b + 1) * P], ident)
                        last.then_inc(product_done, 1)

            def attended(b):
                for s_b in range(b + 1):
                    for q in range(2):
                        wait_moved(pe, "d_PT", b, s_b, q)
                o = begin("d_Y", b)
                for h in range(AH):
                    for s_b in range(b + 1):
                        last = nc.tensor.matmul(o[:, h * HD:(h + 1) * HD], d_PT[:, s_b, h, :],
                                                va[:, s_b, h * HD:(h + 1) * HD], start=(s_b == 0), stop=(s_b == b))
                last.then_inc(product_done, 1)

            probs_turned(0)
            attended(0)
            probs_turned(1)
            pe.wait_ge(m_A, GH)
            for b in range(NB):
                def pair(s_b, h):
                    return DT0[:, h, b * P:(b + 1) * P] if s_b == 0 else DT1[:, h, :]
                o = begin("m_num", b)
                for h in range(GH):
                    for s_b in range(b + 1):
                        last = nc.tensor.matmul(o[:, h * P:(h + 1) * P], pair(s_b, h), vm[:, s_b, h * P:(h + 1) * P],
                                                start=(s_b == 0), stop=(s_b == b))
                last.then_inc(product_done, 1)
                o = begin("m_den", b)
                for h in range(GH):
                    for s_b in range(b + 1):
                        last = nc.tensor.matmul(o[:, h:h + 1], pair(s_b, h), one, start=(s_b == 0), stop=(s_b == b))
                last.then_inc(product_done, 1)
            attended(1)
            for b in range(NB):
                pe.wait_ge(cat_ready, 2 + 2 * b)
                turn("catT", cat, [b])
                wait_turned("catT", [b])
                by_rows("out2_0", hT, blocks=[b])
            by_rows("out2_1", hT)
            wt = tile("gate0", KD, 512)
            outs = [reserved("gate0", h) for h in range(2)]
            for b in range(NB):
                pe.wait_ge(h_ready, 9 + b)
                turn("n5T", h_t, [b])
                wait_turned("n5T", [b])
                for h, o in enumerate(outs):
                    for c2 in range(2):
                        n0 = (2 * h + c2) * P
                        for c in range(KD):
                            last = nc.tensor.matmul(o[:, c2 * S + b * P:c2 * S + (b + 1) * P], wt[:, c, n0:n0 + P],
                                                    hT[:, c, b * P:(b + 1) * P], start=(c == 0), stop=(c == KD - 1))
                    if b == NB - 1:
                        begin("gate0", h)
                        last.then_inc(product_done, 1)
            for i in range(6):
                if i:
                    by_cols(f"gate{i}", TILES[TILE_NO[f"gate{i}"]][2])
                by_cols(f"up{i}", TILES[TILE_NO[f"up{i}"]][2])
            outs = [begin("down", b, h) for b in range(NB) for h in range(2)]
            for i in range(6):
                k = TILES[TILE_NO[f"down{i}"]][1]
                wt = tile(f"down{i}", k, D)
                pe.wait_ge(ff_ready, min(2 * i + 2, FC // 2))
                for n, o in enumerate(outs):
                    b, h = n // 2, n % 2
                    for c in range(k):
                        f = 4 * i + c
                        last = nc.tensor.matmul(o, gT[:, f, b * P:(b + 1) * P], wt[:, c, h * 512:(h + 1) * 512],
                                                start=(f == 0), stop=(f == FC - 1))
                    if i == 5:
                        last.then_inc(product_done, 1)
                if i < 5:
                    last.then_inc(down_used, 1)

        @block.scalar
        def _(act):
            steps = [0]

            def link(ins):
                steps[0] += 1
                ins.then_inc(act_step, 1)
                act.wait_ge(act_step, steps[0])

            def rsqrt(n):
                act.wait_ge(ms_ready, GROUPED.index(n) + 1)
                link(nc.scalar.activation(stat(lnms, n), stat(ms, n), ACT.Ln))
                nc.scalar.activation(stat(rstd, n), stat(lnms, n), ACT.Exp, scale=-0.5).then_inc(rstd_ready, 1)

            def rms(k, b):
                n = norm_stat(k, b)
                link(nc.scalar.activation(h_t[:, b, :], x[:, b, :], ACT.Square, accum_out=stat(ms, n)))
                link(nc.scalar.activation(stat(lnms, n), stat(ms, n), ACT.Ln, bias=eps, scale=1.0 / D))
                nc.scalar.activation(stat(rstd, n), stat(lnms, n), ACT.Exp, scale=-0.5).then_inc(rstd_ready, 1)

            def move(dst, *name, n=512, src=None):
                wait_product(act, *name)
                nc.scalar.activation(dst, bank(name, n) if src is None else src, ACT.Copy).then_inc(emptied(*name), 1)

            def move_turned(name):
                for b in range(NB):
                    for h in range(2):
                        o = PLAN[(name, b, h)] % 8
                        move(hT[:, 4 * h:4 * h + 4, b * P:(b + 1) * P], name, b, h,
                             src=ps[:, o, :].rearrange("p (c t) -> p c t", c=4))

            def ada_moves(i):
                if i < 8:
                    move(ada_rows[i], f"ada{i}")
                else:
                    move(mod[:, (i - 8) // 2, (i % 2) * 512:(i % 2 + 1) * 512], f"ada{i}")
                if i not in (0, 1, EARLY) and i <= 8:
                    move(modc[:, 4 * i - 4:4 * i], "ada_col", i - 1, n=4)

            act.wait_ge(lane_landed, 16)
            nc.scalar.activation(c_e, lane[:, L_C:L_C + KD], ACT.Tanh, scale=0.5).then_inc(c_exp, 1)
            act.wait_ge(lb_sub, 1)
            nc.scalar.activation(lbs[:, 0:16], lbs[:, 0:16], ACT.Exp).then_inc(lb_exp, 1)
            act.wait_ge(x_landed, 16)
            for b in range(NB):
                rms(0, b)
            move(ada_rows[0], "ada0")
            move(modc[:, 0:4], "ada_col", 0, n=4)
            rsqrt(A_STAT)
            rsqrt(A_STAT + 1)
            for h in range(2):
                wait_product(act, "in_hq", h)
                nc.scalar.activation(hqs[:, h * 512:(h + 1) * 512], bank(("in_hq", h)), ACT.Tanh, scale=0.5)\
                  .then_inc(hq_exp, 1)
            for d, n in enumerate(("in_hf", "in_hb")):
                for h in range(2):
                    wait_product(act, n, h)
                    nc.scalar.activation(kk[:, d, h * 512:(h + 1) * 512], bank((n, h)), ACT.Exp, scale=-1.0)\
                      .then_inc(emptied(n, h), 1)
            for b in range(NB):
                move(hi[:, b, :], "in_hi", b)
            for b in range(NB):
                wait_product(act, "in_hg", b)
                nc.scalar.activation(hgs[:, b, :], bank(("in_hg", b)), ACT.Tanh, scale=0.5).then_inc(hg_exp, 1)
            for d in range(2):
                act.wait_ge(hf_ready, d + 1)
                nc.scalar.activation(lf[:, d, :], kk[:, d, :], ACT.Ln).then_inc(lf_ready, 1)
            for i in range(4):
                for b in range(NB):
                    n = f"in_g{i}"
                    wait_product(act, n, b)
                    nc.scalar.activation(gts[:, b, i * 512:(i + 1) * 512], bank((n, b)), ACT.Tanh, scale=0.5)\
                      .then_inc(emptied(n, b), 1)
            for b in range(NB):
                o = PLAN[("a_qT", b)] % 8
                move(a_qT[:, :, b * P:(b + 1) * P], "a_qT", b, src=ps[:, o, :].rearrange("p (c t) -> p c t", c=4))
            move(a_kT, "a_kT", n=S)
            act.wait_ge(mask_packed, 1)
            for b in range(NB):
                for n in range(4):
                    i, g = n // 2, n % 2
                    act.wait_ge(a_max, 4 * b + n + 1)
                    for j in range(2):
                        h = 4 * i + 2 * j + g
                        nc.scalar.activation(a_P[:, b, h, :], bank(("a_S", b, i, g), S, j * S), ACT.Exp,
                                             bias=mx1[:, 8 * b + h:8 * b + h + 1], scale=HD ** -0.5,
                                             accum_out=sum1[:, 8 * b + h:8 * b + h + 1]).then_inc(a_probs, 1)
            for b in range(NB):
                for q in range(2):
                    o = PLAN[("a_PT", b, 0, q)] % 8
                    move(a_PT[:, 0, 4 * q:4 * q + 4, :], "a_PT", b, 0, q,
                         src=ps[:, o, :].rearrange("p (c t) -> p c t", c=4))
                o = PLAN[("a_YT", b)] % 8
                move(yT[:, :, b * P:(b + 1) * P], "a_YT", b, src=ps[:, o, :].rearrange("p (c t) -> p c t", c=4))
            parts = 1
            for n in range(LEVELS):
                if n >= 1:
                    for i in range(parts, ADA_AT.get(n - 1, parts)):
                        ada_moves(i)
                    parts = ADA_AT.get(n - 1, parts)
                act.wait_ge(g_diff, n + 1)
                nc.scalar.activation(E[n % 2], E[n % 2], ACT.Exp).then_inc(g_exp, 1)
            for b in range(NB):
                rsqrt(G_STAT + b)
            ada_moves(EARLY - 1)
            for b in range(NB):
                o = PLAN[("g_OT", b)] % 8
                move(oT[:, :, b * P:(b + 1) * P], "g_OT", b, src=ps[:, o, :].rearrange("p (c t) -> p c t", c=4))
            move(modc[:, 4 * EARLY - 4:4 * EARLY], "ada_col", EARLY - 1, n=4)
            move_turned("mT")
            def query_turned(b):
                for h in range(2):
                    o = PLAN[("n2T", b, h)] % 8
                    move(h2T[b][:, 4 * h:4 * h + 4, :], "n2T", b, h, src=ps[:, o, :].rearrange("p (c t) -> p c t", c=4))

            def query_out(name, b):
                q = int(name[6])
                o = PLAN[(name, b)] % 8
                move(pqT[b][:, 4 * q:4 * q + 4, :], name, b, src=ps[:, o, :].rearrange("p (c t) -> p c t", c=4))

            def scores_out(b, q):
                o = PLAN[("keys", b, q)] % 8
                move(sc[b][:, 4 * q:4 * q + 4, :], "keys", b, q, src=ps[:, o, :].rearrange("p (c t) -> p c t", c=4))

            act.wait_ge(x_whole, 1)
            rms(1, 0)
            query_turned(0)
            act.wait_ge(x_whole, 2)
            rms(1, 1)
            query_out("peer_q0", 0)
            query_out("peer_q1", 0)
            scores_out(0, 0)
            query_out("peer_q2", 0)
            scores_out(0, 1)
            query_turned(1)
            query_out("peer_q3", 0)
            scores_out(0, 2)
            scores_out(0, 3)
            query_out("peer_q1", 1)
            query_out("peer_q2", 1)
            scores_out(1, 1)
            query_out("peer_q3", 1)
            scores_out(1, 2)
            query_out("peer_q0b", 1)
            scores_out(1, 3)
            scores_out(1, 0)

            def best(b):
                act.wait_ge(best_ready, b + 1)
                nc.scalar.activation(best_v, best_v, ACT.Exp).then_inc(best_exp, 1)

            for b in range(NB):
                for h in range(2):
                    move(pp[:, b, h * 512:(h + 1) * 512], "ple_proj", b, h)
            best(0)
            for i in range(EARLY, LATE):
                ada_moves(i)

            def spread(head):
                for half in range(2):
                    act.wait_ge(gelu_in, 2 * head + half + 1)
                    nc.scalar.activation(ge[1], ge[0], ACT.Tanh, scale=GELU_C).then_inc(gelu_exp, 1)
                    act.wait_ge(w_ready, 2 * head + half + 1)
                    for j in range(HALF):
                        act.wait_ge(v_free, head * TOPK + half * HALF + j + 1 + V_RING - DIAG_RING)
                        nc.scalar.activation(diag[:, j, :], ident, ACT.Copy,
                                             scale=w_now[:, half * HALF + j:half * HALF + j + 1])\
                          .then_inc(diag_built, 1)

            with act.Fori(0, SEARCH_END) as head:
                spread(head)
            best(1)
            for i in range(LATE, 12):
                ada_moves(i)
            with act.Fori(SEARCH_END, PH) as head:
                spread(head)

            def whole(b):
                for h in range(2):
                    move(x[:, b, h * 512:(h + 1) * 512], "experts", b, h)
                for h in range(2):
                    wait_moved(act, "experts", b, h)
                rms(2, b)

            def ple_tanh(b):
                for i in range(2):
                    wait_product(act, f"ple{i}", b)
                    if b:
                        act.wait_ge(ple_done, i + 1)
                    nc.scalar.activation(tmp2[:, i * 512:(i + 1) * 512], bank((f"ple{i}", b)), ACT.Tanh, scale=0.5)\
                      .then_inc(ple_exp, 1)

            whole(0)
            with act.Fori(PH, PLE_GATE) as head:
                spread(head)
            ple_tanh(0)
            with act.Fori(PLE_GATE, PLE_ADD) as head:
                spread(head)
            act.wait_ge(x_whole, 3)
            rms(3, 0)
            with act.Fori(PLE_ADD, 2 * PH) as head:
                spread(head)
            whole(1)
            ple_tanh(1)
            act.wait_ge(x_whole, 4)
            rms(3, 1)
            rsqrt(DA_STAT)
            rsqrt(DA_STAT + 1)
            for b in range(NB):
                move(va[:, b, :], "in2_v", b)
            for c in range(2):
                act.wait_ge(conv_done, c + 1)
                nc.scalar.activation(silu_e[:, 4 * c:4 * c + 4, :], qkm[:, 4 * c:4 * c + 4, :], ACT.Tanh, scale=0.5)\
                  .then_inc(conv_exp, 1)
            for name, dst in (("d_qT", d_qT), ("d_kT", d_kT)):
                for b in range(NB):
                    o = PLAN[(name, b)] % 8
                    move(dst[:, :, b * P:(b + 1) * P], name, b, src=ps[:, o, :].rearrange("p (c t) -> p c t", c=4))
            act.wait_ge(m_abs, 1)
            link(nc.scalar.activation(gl[0:GH, 2, :], gl[0:GH, 2, :], ACT.Exp))
            nc.scalar.activation(gl[0:GH, 2, :], gl[0:GH, 2, :], ACT.Ln, bias=1.0).then_inc(m_log, 1)
            for b in range(NB):
                move(vm[:, b, :], "in2_vm", b)
            for b in range(NB):
                P2 = (d_P0, d_P1)[b]
                act.wait_ge(d_max, b + 1)
                for h in range(AH):
                    nc.scalar.activation(P2[:, h, :], P2[:, h, :], ACT.Exp, bias=mx2[:, 8 * b + h:8 * b + h + 1],
                                         accum_out=sum2[:, 8 * b + h:8 * b + h + 1]).then_inc(d_probs, 1)
            for b in range(NB):
                wait_product(act, "in2_og", b)
                nc.scalar.activation(ogs[:, b, :], bank(("in2_og", b)), ACT.Tanh, scale=0.5)\
                  .then_inc(emptied("in2_og", b), 1)
            move(mcols, "m_cols", n=16)
            wait_moved(act, "m_cols")
            link(nc.scalar.activation(emt, mcols[:, 8:16], ACT.Exp, scale=-1.0))
            act.wait_ge(m_D, 2)
            for h in range(GH):
                nc.scalar.activation(DT0[:, h, :], DT0[:, h, :], ACT.Exp, bias=mcols[:, h:h + 1])
                nc.scalar.activation(DT1[:, h, :], DT1[:, h, :], ACT.Exp, bias=mcols[:, GH + h:GH + h + 1])\
                  .then_inc(m_Dexp, 1)
            for b in range(NB):
                for q in range(2):
                    o = PLAN[("d_PT", b, 0, q)] % 8
                    move(d_PT[:, 0, 4 * q:4 * q + 4, :], "d_PT", b, 0, q,
                         src=ps[:, o, :].rearrange("p (c t) -> p c t", c=4))
            rsqrt(M_STAT)
            rsqrt(M_STAT + 1)
            move_turned("catT")
            for b in range(NB):
                act.wait_ge(x_whole, 5 + b)
                rms(4, b)
            for i in range(6):
                for h in range(2 if i < 5 else 1):
                    n = 2 * i + h
                    wait_product(act, f"gate{i}", h)
                    if n >= 1:
                        act.wait_ge(ff_ready, n)
                    nc.scalar.activation(ff_e, bank((f"gate{i}", h)), ACT.Tanh, scale=0.5).then_inc(ff_exp, 1)

        @block.gpsimd
        def _(pool):
            steps = [0]

            def link(ins):
                steps[0] += 1
                ins.then_inc(pool_step, 1)
                pool.wait_ge(pool_step, steps[0])

            pool.wait_ge(mask_landed, 16)
            nc.gpsimd.tensor_copy(lmask[:, :], lmask_f).then_inc(mask_packed, 1)
            pool.wait_ge(g_scanned, 1)
            nc.gpsimd.tensor_tensor(ksum, kk[:, 0, :], kk[:, 1, :], ALU.add).then_inc(g_ks, 1)
            nc.gpsimd.memset(at(big, 14848, 2048), 0.0).then_inc(g_zeroed, 1)
            wait_product(pool, "a_YT", 1)
            for i in range(2):
                nc.gpsimd.memset(at(big, R + 2048 + 4096 * i, 4096), 0.0).then_inc(g_zeroed, 1)
            wait_moved(pool, "g_O", 0)
            pool.dma_start(gain, a["norm_ffn"].partition_broadcast(P)).then_inc(gain_landed, 16)
            wait_product(pool, "mT", 0, 0)
            pool.dma_start(pT, a["pT"].rearrange("(c p) t -> p c t", p=P)).then_inc(pT_landed, 16)
            pool.wait_ge(indexed, 1)
            wait_product(pool, "keys", 0, 3)

            def copy_idx(g):
                where = g[1] * HALF
                nc.gpsimd.tensor_copy(idx_now[:, g[1] % 4 * HALF:(g[1] % 4 + 1) * HALF],
                                      idx_t[:, bass.ds(g[0] * HALF + where, HALF)]).then_inc(idx_copied, 1)
                pool.wait_ge(idx_copied, g[0] + g[1] + 1)

            def gather(ring, table, j, g, free, landed):
                pool.wait_ge(free, (g[0] + g[1]) * HALF + j + 1)
                pool.sem_inc(slot_granted, 1)
                where = g[1] % 4 * HALF + j
                pool.indirect_dma_start(ring[:, j, :], None, table,
                                        bass.IndirectOffsetOnAxis(idx_now[:, where:where + 1], 0))\
                    .then_inc(landed[j], 16)

            def fetch(first, n, last=False):
                if not last:
                    copy_idx((first, n + 1))
                for j in range(HALF):
                    if not last:
                        gather(u_ring, a["peer_u"], j, (first, n + 1), u_free, u_landed)
                    gather(v_ring, a["peer_v"], j, (first, n), v_free, v_landed)

            copy_idx((0, 0))
            for j in range(HALF):
                gather(u_ring, a["peer_u"], j, (0, 0), u_free, u_landed)
            wait_product(pool, "keys", 1, 0)
            with pool.Fori(0, PH // 2 - 1) as pair:
                for n in range(4):
                    fetch(pair * 4, n)
            for i in range(8):
                wait_moved(pool, "ada_col", i)
            for i in range(8, 12):
                wait_moved(pool, f"ada{i}")
            link(nc.gpsimd.tensor_tensor(modc, modc, lane[:, L_ADA:L_ADA + 4 * KD], ALU.add))
            for j in range(2):
                scale = modc[:, (2 * j + 1) * KD:(2 * j + 2) * KD]
                link(nc.gpsimd.tensor_scalar(scale, scale, 1.0, None, ALU.add))
                link(nc.gpsimd.tensor_tensor(scale, scale, lane[:, L_GAIN2 + j * KD:L_GAIN2 + (j + 1) * KD], ALU.mult))
            pool.sem_inc(modc_ready, 1)
            pool.wait_ge(indexed, NB)
            with pool.Fori(PH // 2 - 1, PH - 1) as pair:
                for n in range(4):
                    fetch(pair * 4, n)
            for n in range(4):
                fetch(4 * (PH - 1), n, last=(n == 3))
            wait_product(pool, "experts", NB - 1, 1)
            for j in range(2):
                pool.dma_start(scratch_row, a["b_ada"][(3 * j + 2) * D:(3 * j + 3) * D].partition_broadcast(P))\
                    .then_inc(row_landed, 16)
                pool.wait_ge(row_landed, 16 * (j + 1))
                last = nc.gpsimd.tensor_tensor(mod[:, j, :], mod[:, j, :], scratch_row, ALU.add)
                if j == 0:
                    link(last)
            last.then_inc(mod_ready, 1)

        @block.vector
        def _(dve):
            steps = [0]

            def link(ins):
                steps[0] += 1
                ins.then_inc(dve_step, 1)
                dve.wait_ge(dve_step, steps[0])

            tt = nc.vector.tensor_tensor
            ts = nc.vector.tensor_scalar
            stt = nc.vector.scalar_tensor_tensor

            def mean(n, width):
                ts(stat(ms, n), stat(ms, n), 1.0 / width, EPS, ALU.mult, ALU.add).then_inc(ms_ready, 1)

            def group_squares(n, src, sq, groups, width):
                link(tt(sq, src, src, ALU.mult))
                link(nc.vector.tensor_reduce(stat(ms, n), sq.rearrange("p (g n) -> p g n", g=groups), AX, ALU.add))
                mean(n, width)

            def scale(k, b, gain_row=None):
                dve.wait_ge(rstd_ready, norm_stat(k, b) + 1)
                r = stat(rstd, norm_stat(k, b))
                if gain_row is None:
                    ts(h_t[:, b, :], x[:, b, :], r, None, ALU.mult).then_inc(h_ready, 1)
                else:
                    stt(h_t[:, b, :], x[:, b, :], r, gain_row, ALU.mult, ALU.mult).then_inc(h_ready, 1)

            def turned(name, b, to, gain_cols, shift_cols=None):
                for h in range(2):
                    wait_product(dve, name, b, h)
                    dst = to[:, 4 * h:4 * h + 4, b * P:(b + 1) * P]
                    last = tt(dst, heads(bank((name, b, h)), 4),
                              gain_cols[:, 4 * h:4 * h + 4].unsqueeze(2).to_broadcast([P, 4, P]), ALU.mult)
                    if shift_cols is not None:
                        link(last)
                        last = tt(dst, dst, shift_cols[:, 4 * h:4 * h + 4].unsqueeze(2).to_broadcast([P, 4, P]),
                                  ALU.add)
                    last.then_inc(emptied(name, b, h), 1)

            def heads(t, n):
                return t.rearrange("p (h n) -> p h n", h=n)

            def sigmoid(t):
                link(ts(t, t, 1.0, None, ALU.add))
                link(nc.vector.reciprocal(t, t))

            dve.wait_ge(lane_landed, 16)
            dve.wait_ge(c_exp, 1)
            link(ts(c_e, c_e, 0.5, 0.5, ALU.mult, ALU.add))
            link(tt(c_s, c_e, lane[:, L_C:L_C + KD], ALU.mult))
            nc.vector.tensor_copy(c_rep, c_s.unsqueeze(2).to_broadcast([P, KD, P])).then_inc(c_ready, 1)
            r0, r1 = lane[:, L_LB:L_LB + 8], lane[:, L_LB + 8:L_LB + 16]
            link(tt(lbs[:, 16:24], r0, r1, ALU.max))
            tt(lbs[:, 0:8], r0, lbs[:, 16:24], ALU.subtract)
            tt(lbs[:, 8:16], r1, lbs[:, 16:24], ALU.subtract).then_inc(lb_sub, 1)
            dve.wait_ge(lb_exp, 1)
            link(tt(one_lb, lbs[:, 0:8], lbs[:, 8:16], ALU.add))
            link(nc.vector.reciprocal(one_lb, one_lb))
            link(tt(lb, lbs[:, 0:8], one_lb, ALU.mult))
            link(ts(one_lb, lb, -1.0, 1.0, ALU.mult, ALU.add))

            for b in range(NB):
                scale(0, b)
            for b in range(NB):
                turned("n1T", b, hT, lane[:, L_MIX:L_MIX + KD])
            for b in range(NB):
                wait_product(dve, "in_q", b)
                nc.vector.tensor_copy(qkv[:, b, 0:512], bank(("in_q", b))).then_inc(emptied("in_q", b), 1)
            for b in range(NB):
                wait_product(dve, "in_kv", b)
                nc.vector.tensor_copy(qkv[:, b, 512:768], bank(("in_kv", b), 256)).then_inc(emptied("in_kv", b), 1)
            dve.wait_ge(rows_landed, 16 * 6)
            dve.wait_ge(const_landed, 16)
            for b in range(NB):
                wait_moved(dve, "in_q", b)
                wait_moved(dve, "in_kv", b)
                group_squares(A_STAT + b, qkv[:, b, 0:640], rot[:, b, :], 10, HD)
            for b in range(NB):
                dve.wait_ge(rstd_ready, A_STAT + b + 1)
                q = qkv[:, b, 0:640]
                link(tt(heads(q, 10), heads(q, 10), stat(rstd, A_STAT + b).unsqueeze(2).to_broadcast([P, 10, HD]),
                        ALU.mult))
                link(tt(q, q, gqk[:, :], ALU.mult))
                cs = const[:, C_ROPE + 64 * b:C_ROPE + 64 * (b + 1)].rearrange("p (f a n) -> p f a n", f=2, a=2)
                v5 = q.rearrange("p (h a s n) -> p h a s n", h=10, a=2, s=2)
                o5 = qn[:, b, :].rearrange("p (h a s n) -> p h a s n", h=10, a=2, s=2)
                r5 = rot[:, b, :].rearrange("p (h a s n) -> p h a s n", h=10, a=2, s=2)
                cos = cs[:, 0].unsqueeze(1).to_broadcast([P, 10, 2, 16])
                sin = cs[:, 1].unsqueeze(1).to_broadcast([P, 10, 2, 16])
                for s in range(2):
                    tt(o5[:, :, :, s, :], v5[:, :, :, s, :], cos, ALU.mult)
                    last = tt(r5[:, :, :, s, :], v5[:, :, :, 1 - s, :], sin, ALU.mult)
                link(last)
                tt(o5[:, :, :, 0, :], o5[:, :, :, 0, :], r5[:, :, :, 0, :], ALU.subtract)
                tt(o5[:, :, :, 1, :], o5[:, :, :, 1, :], r5[:, :, :, 1, :], ALU.add).then_inc(a_rot, 1)
            for h in range(2):
                dve.wait_ge(hq_exp, h + 1)
                t = hqs[:, h * 512:(h + 1) * 512]
                stt(t, t, 1.0, bank(("in_hq", h)), ALU.add, ALU.mult).then_inc(emptied("in_hq", h), 1)
            for d, n in enumerate(("in_hf", "in_hb")):
                for h in range(2):
                    wait_moved(dve, n, h)
                sigmoid(kk[:, d, :])
                for h in range(GH):
                    t = kk[:, d, h * S:(h + 1) * S]
                    c = d * GH + h
                    last = ts(t, t, one_lb[:, c:c + 1], lb[:, c:c + 1], ALU.mult, ALU.add)
                last.then_inc(hf_ready, 1)
            for d in range(2):
                dve.wait_ge(lf_ready, d + 1)
                ts(kk[:, d, :], kk[:, d, :], -1.0, 1.0, ALU.mult, ALU.add)
                for h in range(GH):
                    l, o = lf[:, d, h * S:(h + 1) * S], Pc[:, d, h * S:(h + 1) * S]
                    if d == 0:
                        last = nc.vector.tensor_tensor_scan(o, one.to_broadcast([P, S]), l, 0.0, ALU.mult, ALU.add)
                    else:
                        nc.vector.memset(o[:, 0:1], 0.0)
                        last = nc.vector.tensor_tensor_scan(o[:, 1:S], one.to_broadcast([P, S - 1]), l[:, 0:S - 1],
                                                            0.0, ALU.mult, ALU.add)
                if d == 1:
                    last.then_inc(g_scanned, 1)
            for b in range(NB):
                dve.wait_ge(hg_exp, b + 1)
                stt(hgs[:, b, :], hgs[:, b, :], 1.0, bank(("in_hg", b)), ALU.add, ALU.mult).then_inc(emptied("in_hg", b), 1)
            for b in range(NB):
                for n in range(4):
                    i, g = n // 2, n % 2
                    wait_product(dve, "a_S", b, i, g)
                    m = mx1[:, 8 * b + 4 * i + g:8 * b + 4 * i + g + 3:2]
                    link(nc.vector.tensor_reduce(m, heads(bank(("a_S", b, i, g)), 2), AX, ALU.max))
                    ts(m, m, -HD ** -0.5, None, ALU.mult).then_inc(a_max, 1)
            for b in range(NB):
                for n in range(4):
                    dve.wait_ge(a_probs, 8 * b + 2 * n + 2)
                    dve.sem_inc(emptied("a_S", b, n // 2, n % 2), 1)
            for b in range(NB):
                s8 = sum1[:, 8 * b:8 * b + 8]
                link(nc.vector.reciprocal(s8, s8))
                for q in range(2):
                    wait_product(dve, "a_PT", b, 1, q)
                    nc.vector.tensor_copy(a_PT[:, 1, 4 * q:4 * q + 4, :], heads(bank(("a_PT", b, 1, q)), 4))\
                      .then_inc(emptied("a_PT", b, 1, q), 1)
                wait_product(dve, "a_Y", b)
                tt(heads(a_y[:, b, :], AH), heads(bank(("a_Y", b)), AH), s8.unsqueeze(2).to_broadcast([P, AH, HD]),
                   ALU.mult).then_inc(a_out, 1)
                dve.wait_ge(a_out, b + 1)
                dve.sem_inc(emptied("a_Y", b), 1)
            dve.wait_ge(g_zeroed, 3)
            dve.wait_ge(mask_packed, 1)
            wait_product(dve, "a_YT", 1)

            def masked(mask, dst, *name):
                wait_product(dve, *name)
                nc.vector.copy_predicated(dst, mask.unsqueeze(1).to_broadcast([P, GH, P]), heads(bank(name), GH))\
                  .then_inc(emptied(*name), 1)

            def level_mask(lv, d):
                return lmask[:, (2 * lv + d) * P:(2 * lv + d + 1) * P]

            def differences(n):
                m = 1 << (LEVELS - 1 - n)
                p4 = Pc.rearrange("p d (g s m) -> p (d g) s m", s=2, m=m)
                e4 = E[n % 2].rearrange("p (g s m) -> p g s m", s=2, m=m)
                ref = p4[:, :, 0, m - 1:m].to_broadcast([P, 2 * GH * S // (2 * m), m])
                tt(e4[:, :, 0, :], ref, p4[:, :, 0, :], ALU.subtract)
                tt(e4[:, :, 1, :], p4[:, :, 1, :], ref, ALU.subtract).then_inc(g_diff, 1)

            def decayed(n):
                m = 1 << (LEVELS - 1 - n)
                dve.wait_ge(g_exp, n + 1)
                if n >= 2:
                    lv = LEVELS - 1 - (n - 2)
                    wait_product(dve, "g_A", lv, 0 if n == 2 else NB - 1, 1)
                view = "p (g s m) -> p g s m"
                for d in range(2):
                    e = E[n % 2][:, d * GH * S:(d + 1) * GH * S].rearrange(view, s=2, m=m)
                    q4, k4 = hqs.rearrange(view, s=2, m=m), kk[:, d, :].rearrange(view, s=2, m=m)
                    qo, ko = (t[n % 2][:, d, :].rearrange(view, s=2, m=m) for t in (qd, kd))
                    qs, ks = (1, 0) if d == 0 else (0, 1)
                    tt(qo[:, :, qs, :], q4[:, :, qs, :], e[:, :, qs, :], ALU.mult)
                    last = tt(ko[:, :, ks, :], k4[:, :, ks, :], e[:, :, ks, :], ALU.mult)
                last.then_inc(g_decayed, 1)

            def collect(n):
                lv = LEVELS - 1 - n
                if n == 0:
                    for d in range(2):
                        wait_product(dve, "g_A", lv, 0, d)
                        last = nc.vector.tensor_copy(AT[:, d, :, (1 - d) * P:(2 - d) * P],
                                                     heads(bank(("g_A", lv, 0, d)), GH))
                        last.then_inc(emptied("g_A", lv, 0, d), 1)
                    return
                for d in range(2):
                    for b in range(NB):
                        wait_moved(dve, *(("g_A", lv, b, 0) if d else ("g_A", lv + 1, b, 1) if n > 1 else
                                          ("g_diag", b)))
                        masked(level_mask(lv, d), AT[:, b, :, b * P:(b + 1) * P], "g_A", lv, b, d)

            for b in range(NB):
                masked(level_mask(LEVELS - 1, 0), AT[:, b, :, b * P:(b + 1) * P], "g_diag", b)
            differences(0)
            for n in range(LEVELS):
                if n + 1 < LEVELS:
                    if n >= 1:
                        dve.wait_ge(g_decayed, n)
                    differences(n + 1)
                decayed(n)
                if n >= 1:
                    collect(n - 1)
            collect(LEVELS - 1)
            wait_moved(dve, "g_A", 0, NB - 1, 1)
            dve.sem_inc(g_filled, 1)
            for b in range(NB):
                wait_product(dve, "g_O", b)
                ts(o_t[:, b, :], bank(("g_O", b)), 0.5, None, ALU.mult).then_inc(emptied("g_O", b), 1)
                wait_moved(dve, "g_O", b)
                group_squares(G_STAT + b, o_t[:, b, :], o_sq, GH, P)
            for b in range(NB):
                o = heads(o_t[:, b, :], GH)
                dve.wait_ge(rstd_ready, G_STAT + b + 1)
                link(tt(o, o, stat(rstd, G_STAT + b).unsqueeze(2).to_broadcast([P, GH, P]), ALU.mult))
                link(stt(o, o, 0.5, g_o[:, :].unsqueeze(1).to_broadcast([P, GH, P]), ALU.mult, ALU.mult))
                tt(o_t[:, b, :], o_t[:, b, :], hgs[:, b, :], ALU.mult).then_inc(g_out, 1)
            for i in range(4):
                for b in range(NB):
                    wait_moved(dve, f"in_g{i}", b)
            for b in range(NB):
                for h in range(2):
                    c = slice(h * 512, (h + 1) * 512)
                    wait_product(dve, "up_att", b, h)
                    stt(merged[:, b, c], gts[:, b, c], 1.0, bank(("up_att", b, h)), ALU.add, ALU.mult)\
                        .then_inc(emptied("up_att", b, h), 1)
                    wait_product(dve, "up_hg", b, h)
                    stt(tmp, gts[:, b, D + h * 512:D + (h + 1) * 512], 1.0, bank(("up_hg", b, h)), ALU.add, ALU.mult)\
                        .then_inc(emptied("up_hg", b, h), 1)
                    wait_moved(dve, "up_att", b, h)
                    wait_moved(dve, "up_hg", b, h)
                    tt(merged[:, b, c], merged[:, b, c], tmp, ALU.add).then_inc(merged_ready, 1)
                    dve.wait_ge(merged_ready, 2 * b + h + 1)
            for i in range(2):
                for b in range(NB):
                    c = slice(i * 512, (i + 1) * 512)
                    n = (f"out{i}", b)
                    wait_product(dve, *n)
                    stt(x[:, b, c], bank(n), 0.5, x[:, b, c], ALU.mult, ALU.add).then_inc(emptied(*n), 1)
                    if i == 1:
                        wait_moved(dve, "out0", b)
                        wait_moved(dve, "out1", b)
                        dve.sem_inc(x_whole, 1)
                        if b == 0:
                            dve.wait_ge(gain_landed, 16)
                            scale(1, 0, gain)
            scale(1, 1, gain)

            def top16(values, indices, src, spare):
                link(nc.vector.max(values[:, 0:8], src))
                link(nc.vector.match_replace(spare, values[:, 0:8], src, NEG))
                nc.vector.max_index(indices[:, 0:8], values[:, 0:8], src)
                link(nc.vector.max(values[:, 8:16], spare))
                return nc.vector.max_index(indices[:, 8:16], values[:, 8:16], spare)

            def candidates():
                nc.vector.tensor_copy(top_f.rearrange("p h s k -> p (h s k)"), top_i.rearrange("p n k -> p (n k)"))
                v4 = top_v.rearrange("p (h s) k -> p h s k", s=2)
                link(tt(cand, v4[:, :, 0, :].unsqueeze(3).to_broadcast([P, PH, TOPK, TOPK]),
                        v4[:, :, 1, :].unsqueeze(2).to_broadcast([P, PH, TOPK, TOPK]), ALU.add))

            def route(b):
                nc.vector.tensor_copy(g_max, best_v[:, :, 0])
                flat_i = best_i.rearrange("p h k -> p (h k)")
                ts(pos_u[:, 0, :], flat_i, 4, None, ALU.logical_shift_right)
                link(ts(pos_u[:, 1, :], flat_i, 15, None, ALU.bitwise_and))
                tt(best_v, best_v, g_max.unsqueeze(2).to_broadcast([P, PH, TOPK]), ALU.subtract)\
                    .then_inc(best_ready, 1)
                link(nc.vector.tensor_copy(pos_f.rearrange("p s n -> p (s n)"), pos_u.rearrange("p s n -> p (s n)")))
                for s in range(2):
                    h2 = hot.rearrange("p (n k) -> p n k", k=TOPK)
                    h4 = hot.rearrange("p (h n k) -> p h n k", h=PH, k=TOPK)
                    link(tt(h2, iota.unsqueeze(1).to_broadcast([P, SLOTS, TOPK]),
                            pos_f[:, s, :].unsqueeze(2).to_broadcast([P, SLOTS, TOPK]), ALU.is_equal))
                    link(tt(h4, h4, top_f[:, :, s, :].unsqueeze(2).to_broadcast([P, PH, TOPK, TOPK]), ALU.mult))
                    link(nc.vector.tensor_reduce(part[:, s, :], h2, AX, ALU.add))
                stt(idx_t[:, b * SLOTS:(b + 1) * SLOTS], part[:, 0, :], float(NKEYS), part[:, 1, :],
                    ALU.mult, ALU.add).then_inc(indexed, 1)
                if b == 0:
                    dve.sem_inc(u_free, U_RING)
                dve.wait_ge(best_exp, b + 1)
                link(nc.vector.tensor_reduce(g_sum, best_v, AX, ALU.add))
                link(nc.vector.reciprocal(g_sum, g_sum))
                gb = heads(gate_t[:, b * SLOTS:(b + 1) * SLOTS], PH)
                tt(gb, best_v, g_sum.unsqueeze(2).to_broadcast([P, PH, TOPK]), ALU.mult).then_inc(routed, 1)
                dve.wait_ge(routed, b + 1)

            for n in range(2 * PH):
                if n % 4 == 0:
                    wait_moved(dve, "keys", 0, n // 4)
                last = top16(top_v[:, n, :], top_i[:, n, :], sc[0][:, n, :], cut[:, 0:NKEYS])
            link(last)
            candidates()
            for h in range(PH):
                last = top16(best_v[:, h, :], best_i[:, h, :], cand[:, h].rearrange("p i j -> p (i j)"),
                             cut[:, 0:TOPK * TOPK])
            link(last)
            route(0)

            for q in range(4):
                wait_moved(dve, "keys", 1, q)

            def dots(b, head, half):
                for j in range(HALF):
                    dve.wait_ge(u_landed[j], 16 * (2 * head + half + 1))
                    nc.vector.tensor_tensor_reduce(u_ring[:, j, :], u_ring[:, j, :], h_t[:, b, :], 1.0, 0.0,
                                                   ALU.mult, ALU.add, a_dot[:, j:j + 1]).then_inc(u_free, 1)
                dve.wait_ge(u_free, head * TOPK + (half + 1) * HALF + U_RING)
                g = 2 * head + half

                def chain(ins, k):
                    ins.then_inc(gelu_step, 1)
                    dve.wait_ge(gelu_step, g * 4 + k)
                chain(tt(ge[2], a_dot, a_dot, ALU.mult), 1)
                chain(ts(ge[2], ge[2], 0.044715, 1.0, ALU.mult, ALU.add), 2)
                tt(ge[0], ge[2], a_dot, ALU.mult).then_inc(gelu_in, 1)
                chain(stt(ge[3], a_dot, 0.5, gate_t[:, bass.ds(head * TOPK + half * HALF, HALF)],
                          ALU.mult, ALU.mult), 3)
                dve.wait_ge(gelu_exp, g + 1)
                stt(w_now[:, half * HALF:(half + 1) * HALF], ge[1], 1.0, ge[3], ALU.add, ALU.mult)\
                    .then_inc(w_ready, 1)
                dve.wait_ge(w_ready, g + 1)
                dve.sem_inc(gelu_step, 1)

            def search(piece, src, at_, width, values, indices, to):
                def chain(ins, k):
                    ins.then_inc(search_step, 1)
                    dve.wait_ge(search_step, piece * 6 + k)
                    dve.sem_inc(search_go, 1)
                two = two_in[:, 0:2 * width].rearrange("p (n k) -> p n k", n=2)
                left = cut[:, 0:2 * width].rearrange("p (n k) -> p n k", n=2)
                chain(nc.vector.tensor_copy(two_in[:, 0:2 * width], src[:, bass.ds(at_, 2 * width)]), 1)
                for k, ops in enumerate((
                        lambda n: nc.vector.max(two_v[:, n, 0:8], two[:, n, :]),
                        lambda n: nc.vector.match_replace(left[:, n, :], two_v[:, n, 0:8], two[:, n, :], NEG),
                        lambda n: (nc.vector.max_index(two_i[:, n, 0:8], two_v[:, n, 0:8], two[:, n, :]),
                                   nc.vector.max(two_v[:, n, 8:16], left[:, n, :]))[1],
                        lambda n: nc.vector.max_index(two_i[:, n, 8:16], two_v[:, n, 8:16], left[:, n, :]))):
                    ops(0)
                    chain(ops(1), k + 2)
                nc.vector.tensor_copy(values[:, bass.ds(to, 2 * TOPK)], two_v.rearrange("p n k -> p (n k)"))
                chain(nc.vector.tensor_copy(indices[:, bass.ds(to, 2 * TOPK)], two_i.rearrange("p n k -> p (n k)")), 6)

            with dve.Fori(0, PH // 2) as head:
                for half in range(2):
                    dots(0, head, half)
                    n = 2 * head + half
                    search(n, sc[1].rearrange("p n k -> p (n k)"), n * 2 * NKEYS, NKEYS,
                           top_v.rearrange("p n k -> p (n k)"), top_i.rearrange("p n k -> p (n k)"), n * 2 * TOPK)
            candidates()
            with dve.Fori(PH // 2, SEARCH_END) as head:
                for half in range(2):
                    dots(0, head, half)
                    n = 2 * head + half
                    search(n, cand.rearrange("p h i j -> p (h i j)"), (n - PH) * 2 * TOPK * TOPK, TOPK * TOPK,
                           best_v.rearrange("p h k -> p (h k)"), best_i.rearrange("p h k -> p (h k)"),
                           (n - PH) * 2 * TOPK)
            route(1)
            with dve.Fori(SEARCH_END, PH) as head:
                for half in range(2):
                    dots(0, head, half)
            def ple_add(b):
                for i in range(2):
                    n = (f"ple{i}", b)
                    c = slice(i * 512, (i + 1) * 512)
                    t = tmp2[:, i * 512:(i + 1) * 512]
                    dve.wait_ge(ple_exp, 2 * b + i + 1)
                    dve.sem_inc(emptied(*n), 1)
                    link(stt(t, t, 1.0, pp[:, b, c], ALU.add, ALU.mult))
                    stt(x[:, b, c], t, 0.5, x[:, b, c], ALU.mult, ALU.add).then_inc(ple_done, 1)
                dve.wait_ge(ple_done, 2 * b + 2)
                dve.sem_inc(x_whole, 1)

            with dve.Fori(PH, PLE_SCALE) as head:
                for half in range(2):
                    dots(1, head, half)
            scale(2, 0)
            with dve.Fori(PLE_SCALE, PLE_TURN) as head:
                for half in range(2):
                    dots(1, head, half)
            turned("n3T", 0, h3T, lane[:, L_PLE:L_PLE + KD])
            with dve.Fori(PLE_TURN, PLE_ADD) as head:
                for half in range(2):
                    dots(1, head, half)
            ple_add(0)
            with dve.Fori(PLE_ADD, 2 * PH) as head:
                for half in range(2):
                    dots(1, head, half)
            scale(3, 0)
            dve.wait_ge(modc_ready, 1)
            turned("n4T", 0, hT, modc[:, KD:2 * KD], modc[:, 0:KD])
            def qk_out(n, b):
                i = ("in2_q", "in2_k").index(n)
                wait_product(dve, n, b)
                nc.vector.tensor_copy(qk2[:, b, i * 512:(i + 1) * 512], bank((n, b))).then_inc(emptied(n, b), 1)

            scale(2, 1)
            qk_out("in2_q", 0)
            turned("n3T", 1, h3T, lane[:, L_PLE:L_PLE + KD])
            ple_add(1)
            qk_out("in2_k", 0)
            scale(3, 1)
            turned("n4T", 1, hT, modc[:, KD:2 * KD], modc[:, 0:KD])
            for n in ("in2_q", "in2_k"):
                qk_out(n, 1)
            for b in range(NB):
                wait_moved(dve, "in2_q", b)
                wait_moved(dve, "in2_k", b)
                group_squares(DA_STAT + b, qk2[:, b, :], sq2[:, b, :], 16, HD)
            for b in range(NB):
                dve.wait_ge(rstd_ready, DA_STAT + b + 1)
                q = qk2[:, b, :]
                link(tt(heads(q, 16), heads(q, 16), stat(rstd, DA_STAT + b).unsqueeze(2).to_broadcast([P, 16, HD]),
                        ALU.mult))
                q4 = q.rearrange("p (s h n) -> p s h n", s=2, h=AH)
                tt(q4, q4, heads(gqk2[:, :], 2).unsqueeze(2).to_broadcast([P, 2, AH, HD]), ALU.mult)\
                    .then_inc(d_norm, 1)
            for i, n in enumerate(("in2_qm", "in2_km")):
                for h in range(2):
                    wait_product(dve, n, h)
                    for c2 in range(2):
                        ch = 4 * i + 2 * h + c2
                        z = bank((n, h), S, c2 * S)
                        y = qkm[:, ch, :]
                        w = [lane[:, L_CONV + 8 * k + ch:L_CONV + 8 * k + ch + 1] for k in range(4)]
                        link(ts(y, z, w[3], lane[:, L_CONVB + ch:L_CONVB + ch + 1], ALU.mult, ALU.add))
                        for k in range(3):
                            back = 3 - k
                            last = stt(y[:, back:S], z[:, 0:S - back], w[k], y[:, back:S], ALU.mult, ALU.add)
                            link(last)
                    dve.sem_inc(emptied(n, h), 1)
                dve.sem_inc(conv_done, 1)
            for c in range(2):
                dve.wait_ge(conv_exp, c + 1)
                last = stt(qkm[:, 4 * c:4 * c + 4, :], silu_e[:, 4 * c:4 * c + 4, :], 1.0,
                           qkm[:, 4 * c:4 * c + 4, :], ALU.add, ALU.mult)
            last.then_inc(qkm_ready, 1)
            wait_product(dve, "in2_if")
            row = [gl[0:GH, r, :] for r in range(10)]
            bi = bank(("in2_if",))
            ts(row[0], bi[0:GH, 0:S], lane[0:GH, L_IF:L_IF + 1], None, ALU.add)
            link(ts(row[1], bi[0:GH, S:2 * S], lane[0:GH, L_IF + 1:L_IF + 2], None, ALU.add))
            dve.sem_inc(emptied("in2_if"), 1)
            link(ts(row[3], row[1], 0.0, None, ALU.min))
            stt(row[2], row[3], 2.0, row[1], ALU.mult, ALU.subtract).then_inc(m_abs, 1)
            link(nc.vector.memset(row[9], 0.0))
            dve.wait_ge(m_log, 1)
            link(tt(row[3], row[3], row[2], ALU.subtract))
            link(nc.vector.tensor_tensor_scan(row[4], one[0:GH, :].to_broadcast([GH, S]), row[3], 0.0, ALU.mult, ALU.add))
            link(tt(row[5], row[0], row[4], ALU.subtract))
            link(nc.vector.tensor_tensor_scan(row[6], row[9], row[5], 0.0, ALU.add, ALU.max))
            tt(row[7], row[4], row[6], ALU.add).then_inc(m_rows, 1)
            for b in range(NB):
                w = (b + 1) * P
                P2 = (d_P0, d_P1)[b]
                for n in range(4):
                    i, g = n // 2, n % 2
                    wait_product(dve, "d_S", b, i, g)
                    lc = const[:, C_LOGC + b * S:C_LOGC + b * S + w].unsqueeze(1).to_broadcast([P, 2, w])
                    stt(P2[:, 4 * i + g:4 * i + g + 3:2, :], heads(bank(("d_S", b, i, g), 2 * w), 2), HD ** -0.5, lc,
                        ALU.mult, ALU.add).then_inc(emptied("d_S", b, i, g), 1)
                for n in range(4):
                    wait_moved(dve, "d_S", b, n // 2, n % 2)
                m = mx2[:, 8 * b:8 * b + 8]
                link(nc.vector.tensor_reduce(m, P2, AX, ALU.max))
                ts(m, m, -1.0, None, ALU.mult).then_inc(d_max, 1)
            for i in range(2):
                wait_product(dve, "m_M", i)
                mb = heads(bank(("m_M", i)), 2)
                tt(DT0[:, 2 * i:2 * i + 2, :], tri.unsqueeze(1).to_broadcast([P, 2, S]), mb, ALU.subtract)
                tt(DT1[:, 2 * i:2 * i + 2, :], tri[:, 0:P].unsqueeze(1).to_broadcast([P, 2, P]), mb[:, :, P:S],
                   ALU.subtract).then_inc(m_D, 1)
                dve.wait_ge(m_D, i + 1)
                dve.sem_inc(emptied("m_M", i), 1)
            for h in range(GH):
                dve.wait_ge(m_Dexp, h + 1)
                wait_product(dve, "m_S", h)
                s_ = bank(("m_S", h))
                stt(DT0[:, h, :], s_[:, 0:S], 0.25 * P ** -0.5, DT0[:, h, :], ALU.mult, ALU.mult)
                stt(DT1[:, h, :], s_[:, S:S + P], 0.25 * P ** -0.5, DT1[:, h, :], ALU.mult, ALU.mult).then_inc(m_A, 1)
                dve.wait_ge(m_A, h + 1)
                dve.sem_inc(emptied("m_S", h), 1)
            def attention_out(b):
                s8 = sum2[:, 8 * b:8 * b + 8]
                dve.wait_ge(d_probs, 8 * b + 8)
                link(nc.vector.reciprocal(s8, s8))
                wait_product(dve, "d_Y", b)
                tt(heads(cat[:, b, 0:512], AH), heads(bank(("d_Y", b)), AH), s8.unsqueeze(2).to_broadcast([P, AH, HD]),
                   ALU.mult).then_inc(cat_ready, 1)
                dve.wait_ge(cat_ready, 2 * b + 1)
                dve.sem_inc(emptied("d_Y", b), 1)

            def mlstm_divided(b):
                wait_product(dve, "m_den", b)
                wait_moved(dve, "m_cols")
                dn, em = den[:, 4 * b:4 * b + 4], emt[:, 4 * b:4 * b + 4]
                nq = bank(("m_den", b), GH)
                link(stt(dn, nq, -1.0, em, ALU.mult, ALU.max))
                link(tt(dn, nq, dn, ALU.max))
                dve.sem_inc(emptied("m_den", b), 1)
                link(nc.vector.reciprocal(dn, dn))
                hm = cat[:, b, 512:1024]
                tt(heads(hm, GH), heads(bank(("m_num", b)), GH), dn.unsqueeze(2).to_broadcast([P, GH, P]), ALU.mult)\
                    .then_inc(emptied("m_num", b), 1)
                wait_moved(dve, "m_num", b)
                group_squares(M_STAT + b, hm, hm_sq, GH, P)

            def mlstm_out(b):
                hm = cat[:, b, 512:1024]
                dve.wait_ge(rstd_ready, M_STAT + b + 1)
                link(tt(heads(hm, GH), heads(hm, GH), stat(rstd, M_STAT + b).unsqueeze(2).to_broadcast([P, GH, P]),
                        ALU.mult))
                link(stt(hm, hm, 0.5, g_m[:, :], ALU.mult, ALU.mult))
                wait_moved(dve, "in2_og", b)
                stt(hm, ogs[:, b, :], 1.0, hm, ALU.add, ALU.mult).then_inc(cat_ready, 1)

            attention_out(0)
            for q in range(2):
                wait_product(dve, "d_PT", 1, 1, q)
                nc.vector.tensor_copy(d_PT[:, 1, 4 * q:4 * q + 4, :], heads(bank(("d_PT", 1, 1, q)), 4))\
                  .then_inc(emptied("d_PT", 1, 1, q), 1)
            mlstm_divided(0)
            mlstm_divided(1)
            mlstm_out(0)
            attention_out(1)
            mlstm_out(1)

            def gated_add(src, gate_row, b, c, t, factor):
                link(stt(t, src, factor, gate_row[:, c], ALU.mult, ALU.mult))
                return tt(x[:, b, c], x[:, b, c], t, ALU.add)

            dve.wait_ge(mod_ready, 1)
            for i in range(2):
                for b in range(NB):
                    n = (f"out2_{i}", b)
                    wait_product(dve, *n)
                    if i == 1:
                        wait_moved(dve, "out2_0", b)
                    gated_add(bank(n), mod[:, 0, :], b, slice(i * 512, (i + 1) * 512),
                              tmp2[:, b * 512:(b + 1) * 512], 1.0)\
                        .then_inc(emptied(*n), 1)
                    if i == 1:
                        wait_moved(dve, "out2_1", b)
                        dve.sem_inc(x_whole, 1)
                        if b == 0:
                            scale(4, 0)
            turned("n5T", 0, hT, modc[:, 3 * KD:4 * KD], modc[:, 2 * KD:3 * KD])
            scale(4, 1)
            turned("n5T", 1, hT, modc[:, 3 * KD:4 * KD], modc[:, 2 * KD:3 * KD])
            for i in range(6):
                for h in range(2 if i < 5 else 1):
                    n = 2 * i + h
                    dve.wait_ge(ff_exp, n + 1)
                    link(stt(ff_e, ff_e, 1.0, bank((f"gate{i}", h)), ALU.add, ALU.mult))
                    dve.sem_inc(emptied(f"gate{i}", h), 1)
                    wait_product(dve, f"up{i}", h)
                    tt(gT[:, 2 * n:2 * n + 2, :].rearrange("p c t -> p (c t)"), ff_e, bank((f"up{i}", h)), ALU.mult)\
                        .then_inc(ff_ready, 1)
                    dve.wait_ge(ff_ready, n + 1)
                    dve.sem_inc(emptied(f"up{i}", h), 1)
            for b in range(NB):
                for h in range(2):
                    wait_product(dve, "down", b, h)
                    if b == 1 and h == 0:
                        dve.wait_ge(x_ready, 1)
                    last = gated_add(bank(("down", b, h)), mod[:, 1, :], b, slice(h * 512, (h + 1) * 512),
                                     tmp2[:, h * 512:(h + 1) * 512], 0.5)
                last.then_inc(x_ready, 1)


def kernel(**inputs):
    import concourse.bacc as bacc
    from concourse.bass_utils import run_bass_kernel_spmd

    i = {k: np.asarray(v) for k, v in inputs.items()}
    order = np.arange(AH * HD).reshape(AKV, AH // AKV, HD).transpose(1, 0, 2).reshape(-1)
    w_in = i["w_in"][0]
    arrays = {
        "x": i["x"][0], "w_in": np.concatenate([w_in[:, order], w_in[:, AH * HD:]], axis=1),
        "w_up_att": i["w_up_att"][0][order], "w_up_hg": i["w_up_hg"][0], "w_out": i["w_out"][0],
        "peer_wq": i["peer_wq"][0],
        "subkeys": i["peer_subkeys"][0].transpose(3, 0, 1, 2).reshape(P, -1),
        "peer_u": i["peer_u"][0], "peer_v": i["peer_v"][0],
        "w_ada": i["w_ada_2"][0], "b_ada": i["b_ada_2"][0], "ple_gate": i["ple_gate"][0],
        "ple_proj": i["ple_proj"][0], "pT": i["p"][0, 0].T, "w_in_2": i["w_in_2"][0], "w_out_2": i["w_out_2"][0],
        "w_gate": i["w_gate_2"][0], "w_up": i["w_up_2"][0], "w_down": i["w_down_2"][0],
        "norm_ffn": i["norm_ffn"][0],
        "q_norm": i["q_norm"][0], "k_norm": i["k_norm"][0], "hg_out_norm": i["hg_out_norm"][0],
        "q_norm_g_2": i["q_norm_g_2"][0], "k_norm_g_2": i["k_norm_g_2"][0], "mlstm_norm_g_2": i["mlstm_norm_g_2"][0],
    }
    pad = np.zeros((P, 2), np.float32)
    pad[:GH, 0], pad[:GH, 1] = i["b_igate_2"][0], i["b_fgate_2"][0]
    arrays["lane"] = np.concatenate([
        i["hg_lb_raw"].reshape(2, 2, GH, P).transpose(3, 0, 1, 2).reshape(P, 16),
        i["w_conv_2"][0].reshape(4, 8, P).transpose(2, 0, 1).reshape(P, 32),
        i["b_conv_2"][0].reshape(8, P).T, i["c_2"][0].reshape(KD, P).T, pad,
        i["norm_mix"][0].reshape(KD, P).T, i["norm_ple"][0].reshape(KD, P).T,
        i["b_ada_2"][0].reshape(6, KD, P)[[0, 1, 3, 4]].transpose(2, 0, 1).reshape(P, 4 * KD),
        i["g_mix_2"][0].reshape(KD, P).T, i["g_ffn_2"][0].reshape(KD, P).T,
        np.full((P, 1), EPS, np.float32)], axis=1)

    pos = np.arange(S)
    inv = 10000.0 ** (-np.arange(16, dtype=np.float32) / 16)
    ang = np.stack([(pos // 64)[:, None] * inv, (pos % 64)[:, None] * inv], axis=1).astype(np.float32)
    const = np.zeros((P, C_END), np.float32)
    rope = np.stack([np.cos(ang), np.sin(ang)], axis=1).reshape(NB, P, 64)
    const[:, C_ROPE:C_LOGC] = rope.transpose(1, 0, 2).reshape(P, -1)
    back = pos[:, None] - pos[None, :]
    count = sum(((back >= 0) & (back <= w) & (back % d == 0)).astype(int) for w, d in ((128, 1), (512, 4), (2048, 16)))
    logc = np.where(count > 0, np.log(np.maximum(count, 1)), -1e30).astype(np.float32)
    const[:, C_LOGC:C_TRI] = logc.reshape(NB, P, S).transpose(1, 0, 2).reshape(P, -1)
    const[:, C_TRI:C_IOTA] = np.where(pos[None, :] >= np.arange(P)[:, None], 0.0, -1e30)
    const[:, C_IOTA:C_IDENT] = np.arange(TOPK)
    const[:, C_IDENT:C_SEL] = np.eye(P)
    for h in range(GH):
        const[h, C_SEL + h * P:C_SEL + (h + 1) * P] = 1.0
    const[:, C_ONE] = 1.0
    arrays["const"] = const
    lmask = np.zeros((P, LEVELS, 2, P), np.float32)
    s_, t_ = np.arange(P)[:, None], np.arange(P)[None, :]
    for lv in range(LEVELS - 1):
        m = 1 << lv
        same = s_ // (2 * m) == t_ // (2 * m)
        lmask[:, lv, 0] = same & (s_ // m % 2 == 0) & (t_ // m % 2 == 1)
        lmask[:, lv, 1] = same & (s_ // m % 2 == 1) & (t_ // m % 2 == 0)
    lmask[:, LEVELS - 1, 0] = s_ == t_
    arrays["lmask"] = lmask.reshape(P, -1)

    nc = bacc.Bacc("TRN2", target_bir_lowering=False, num_devices=1)
    sent, a = {}, {}
    for name, v in arrays.items():
        v = np.ascontiguousarray(v)
        sent[f"in_{name}"] = v
        a[name] = nc.dram_tensor(f"in_{name}", v.shape, mybir.dt.from_np(v.dtype), kind="ExternalInput").ap()
    out = nc.dram_tensor("out", (S, D), F32, kind="ExternalOutput").ap()
    two_blocks(nc, a, out)
    r = run_bass_kernel_spmd(nc, [sent], core_ids=[0])
    return r.results[0]["out"].reshape(1, S, D)
```
